# Optimizing a Trainium2 kernel written in Bass

```python
import jax, jax.numpy as jnp
from jax import lax
import numpy as np

D_MODEL = 1024
BATCH = 1
SEQ = 512
DEPTH = 2
DEC_BATCH = 1
DEC_SEQ = 256
PAST_LEN = 128

GRID_W = 64
HEAD_DIM = 64
ROPE_THETA = 10000.0
NORM_EPS = 1e-6
Q_BLOCK = 128
A_Q_HEADS = 4
A_KV_HEADS = 2
CONV_CH = 256
CONV_WIDTH = 31
C_Q_HEADS = 4
C_KV_HEADS = 2
WINDOW = 128
GLA_HEADS = 4
GLA_DK = 64
GLA_DV = 64
GLA_RANK = 16
GLA_TAU = 16.0
GLA_CHUNK = 64
N_BRANCH = 4
BRANCH_W = 256
N_EXPERTS = 16
EXPERT_FF = 1024
EC_CAPACITY = 2
PLE_DIM = 256

A_COLS = (A_Q_HEADS + 2 * A_KV_HEADS) * HEAD_DIM
B_COLS = 2 * CONV_CH
C_COLS = (C_Q_HEADS + 2 * C_KV_HEADS) * HEAD_DIM
D_COLS = GLA_HEADS * (2 * GLA_DK + 2 * GLA_DV) + 2 * GLA_RANK
G_COLS = N_BRANCH * D_MODEL
IN_COLS = A_COLS + B_COLS + C_COLS + D_COLS + G_COLS

kernel_name = 'hybrid_parallel_encoder_ec_moe'

F32 = jnp.float32

def rmsnorm(x, g):
    xf = x.astype(F32)
    y = xf * lax.rsqrt(jnp.mean(xf * xf, axis=-1, keepdims=True) + NORM_EPS) * g.astype(F32)
    return y.astype(x.dtype)

def rope_cos_sin(pos, dim):
    inv = ROPE_THETA ** (-jnp.arange(0, dim, 2, dtype=F32) / dim)
    ang = pos.astype(F32)[:, None] * inv[None, :]
    return jnp.cos(ang), jnp.sin(ang)

def apply_rope(x, cos, sin):
    xf = x.astype(F32)
    half = xf.shape[-1] // 2
    x1, x2 = xf[..., :half], xf[..., half:]
    c = cos[None, :, None, :]
    s = sin[None, :, None, :]
    return jnp.concatenate([x1 * c - x2 * s, x1 * s + x2 * c], axis=-1).astype(x.dtype)

def axial_rope(x, row_cs, col_cs):
    h = HEAD_DIM // 2
    return jnp.concatenate([apply_rope(x[..., :h], *row_cs), apply_rope(x[..., h:], *col_cs)], axis=-1)

def position_tables(S):
    rows = S // GRID_W
    row = jnp.repeat(jnp.arange(rows), GRID_W)
    col = jnp.tile(jnp.arange(GRID_W), rows)
    t = jnp.arange(S)
    return (rope_cos_sin(row, HEAD_DIM // 2), rope_cos_sin(col, HEAD_DIM // 2),
            rope_cos_sin(t, HEAD_DIM))

def global_attention(q, k, v):
    B, S, Hq, d = q.shape
    Hkv = k.shape[2]
    G = Hq // Hkv
    nb = S // Q_BLOCK
    scale = d ** -0.5
    qb = jnp.moveaxis(q.reshape(B, nb, Q_BLOCK, Hkv, G, d), 1, 0)

    def block(qblk):
        s = jnp.einsum('bqkgd,bskd->bkgqs', qblk, k).astype(F32) * scale
        p = jax.nn.softmax(s, axis=-1).astype(v.dtype)
        return jnp.einsum('bkgqs,bskd->bqkgd', p, v)

    o = lax.map(block, qb)
    return jnp.moveaxis(o, 0, 1).reshape(B, S, Hq * d)

def window_attention(q, k, v, sink):
    B, S, Hq, d = q.shape
    Hkv = k.shape[2]
    G = Hq // Hkv
    nb = S // Q_BLOCK
    scale = d ** -0.5
    qb = q.reshape(B, nb, Q_BLOCK, Hkv, G, d)

    def band(t):
        tp = jnp.pad(t, ((0, 0), (Q_BLOCK, Q_BLOCK), (0, 0), (0, 0))).reshape(B, nb + 2, Q_BLOCK, Hkv, d)
        return jnp.concatenate([tp[:, :-2], tp[:, 1:-1], tp[:, 2:]], axis=2)

    kb, vb = band(k), band(v)
    s = jnp.einsum('bnqkgd,bnskd->bnkgqs', qb, kb).astype(F32) * scale
    blk = jnp.arange(nb)[:, None] * Q_BLOCK
    qpos = blk + jnp.arange(Q_BLOCK)[None, :]
    kpos = blk - Q_BLOCK + jnp.arange(3 * Q_BLOCK)[None, :]
    kp = kpos[:, None, :]
    valid = (jnp.abs(kp - qpos[:, :, None]) <= WINDOW) & (kp >= 0) & (kp < S)
    s = jnp.where(valid[None, :, None, None], s, -jnp.inf)
    sk = sink.astype(F32).reshape(Hkv, G)[None, None, :, :, None, None]
    m = jnp.maximum(jnp.max(s, axis=-1, keepdims=True), sk)
    e = jnp.exp(s - m)
    p = e / (jnp.sum(e, axis=-1, keepdims=True) + jnp.exp(sk - m))
    o = jnp.einsum('bnkgqs,bnskd->bnqkgd', p.astype(v.dtype), vb)
    return o.reshape(B, S, Hq * d)

def conv_module(u, w_dw, b_dw, ln_g, ln_b):
    a, g = jnp.split(u, 2, axis=-1)
    z = a * jax.nn.sigmoid(g)
    z = lax.conv_general_dilated(z, w_dw.astype(z.dtype)[:, None, :], window_strides=(1,),
                                 padding=[(CONV_WIDTH // 2, CONV_WIDTH // 2)],
                                 dimension_numbers=('NWC', 'WIO', 'NWC'),
                                 feature_group_count=CONV_CH)
    zf = z.astype(F32) + b_dw.astype(F32)
    mu = jnp.mean(zf, axis=-1, keepdims=True)
    var = jnp.mean(jnp.square(zf - mu), axis=-1, keepdims=True)
    zf = (zf - mu) * lax.rsqrt(var + NORM_EPS) * ln_g.astype(F32) + ln_b.astype(F32)
    return jax.nn.silu(zf).astype(u.dtype)

def gla_direction(q, k, v, log_a):
    B, S, H, dk = q.shape
    dv = v.shape[-1]
    L = GLA_CHUNK
    nc = S // L
    q, k, v, log_a = (t.reshape(B, nc, L, H, t.shape[-1]) for t in (q, k, v, log_a))
    b = jnp.cumsum(log_a, axis=2)
    b_mid = b[:, :, L // 2 - 1:L // 2]
    b_last = b[:, :, -1]
    att = jnp.einsum('bcihd,bcjhd->bchij', q * jnp.exp(b - b_mid), k * jnp.exp(b_mid - b))
    tri = jnp.tril(jnp.ones((L, L), dtype=bool))
    att = jnp.where(tri, att, 0.0)
    o_intra = jnp.einsum('bchij,bcjhe->bcihe', att, v)
    kv = jnp.einsum('bcjhd,bcjhe->bchde', k * jnp.exp(b_last[:, :, None] - b), v)

    def step(state, inp):
        dec, kv_c = inp
        return jnp.exp(dec)[..., None] * state + kv_c, state

    s0 = jnp.zeros((B, H, dk, dv), q.dtype)
    _, prev = lax.scan(step, s0, (jnp.moveaxis(b_last, 1, 0), jnp.moveaxis(kv, 1, 0)))
    prev = jnp.moveaxis(prev, 0, 1)
    o_inter = jnp.einsum('bcihd,bchde->bcihe', q * jnp.exp(b), prev)
    return (o_intra + o_inter).reshape(B, S, H, dv)

def gla_mixer(qd, kd, vd, rd, zlr, w2, b2, gn):
    B, S, _ = qd.shape
    q = qd.astype(F32).reshape(B, S, GLA_HEADS, GLA_DK) * (GLA_DK ** -0.5)
    k = kd.astype(F32).reshape(B, S, GLA_HEADS, GLA_DK)
    v = vd.astype(F32).reshape(B, S, GLA_HEADS, GLA_DV)
    z = zlr.astype(F32).reshape(B, S, 2, GLA_RANK)
    la = jax.nn.log_sigmoid(jnp.einsum('bsnr,nrc->bsnc', z, w2.astype(F32)) + b2.astype(F32)) / GLA_TAU
    la_f = la[:, :, 0].reshape(B, S, GLA_HEADS, GLA_DK)
    la_b = la[:, :, 1].reshape(B, S, GLA_HEADS, GLA_DK)
    flip = lambda t: jnp.flip(t, axis=1)
    o = gla_direction(q, k, v, la_f) + flip(gla_direction(flip(q), flip(k), flip(v), flip(la_b)))
    o = o * lax.rsqrt(jnp.mean(o * o, axis=-1, keepdims=True) + NORM_EPS) * gn.astype(F32)
    o = o.reshape(B, S, GLA_HEADS * GLA_DV) * jax.nn.silu(rd.astype(F32))
    return o.astype(qd.dtype)

def mixer_block(h, w_in, qk_g, sink, dw, dwb, lng, lnb, g2, gb2, gn, w_branch, w_out, tables):
    B, S, _ = h.shape
    row_cs, col_cs, t_cs = tables
    u = h @ w_in
    sizes = [A_Q_HEADS * HEAD_DIM, A_KV_HEADS * HEAD_DIM, A_KV_HEADS * HEAD_DIM,
             B_COLS,
             C_Q_HEADS * HEAD_DIM, C_KV_HEADS * HEAD_DIM, C_KV_HEADS * HEAD_DIM,
             GLA_HEADS * GLA_DK, GLA_HEADS * GLA_DK, GLA_HEADS * GLA_DV, GLA_HEADS * GLA_DV,
             2 * GLA_RANK, G_COLS]
    (qa, ka, va, ub, qc, kc, vc, qd, kd, vd, rd, zlr, gates) = jnp.split(u, np.cumsum(sizes)[:-1], axis=-1)
    qa = axial_rope(rmsnorm(qa.reshape(B, S, A_Q_HEADS, HEAD_DIM), qk_g[0]), row_cs, col_cs)
    ka = axial_rope(rmsnorm(ka.reshape(B, S, A_KV_HEADS, HEAD_DIM), qk_g[1]), row_cs, col_cs)
    oa = global_attention(qa, ka, va.reshape(B, S, A_KV_HEADS, HEAD_DIM))
    ob = conv_module(ub, dw, dwb, lng, lnb)
    qc = apply_rope(qc.reshape(B, S, C_Q_HEADS, HEAD_DIM), *t_cs)
    kc = apply_rope(kc.reshape(B, S, C_KV_HEADS, HEAD_DIM), *t_cs)
    oc = window_attention(qc, kc, vc.reshape(B, S, C_KV_HEADS, HEAD_DIM), sink)
    od = gla_mixer(qd, kd, vd, rd, zlr, g2, gb2, gn)
    gates = jax.nn.sigmoid(gates.reshape(B, S, N_BRANCH, D_MODEL))
    merged = 0.0
    for i, o in enumerate((oa, ob, oc, od)):
        merged = merged + gates[:, :, i] * (o @ w_branch[i])
    return merged @ w_out

def expert_choice_ffn(h, w_router, wg, wu, wd):
    B, S, D = h.shape
    N = B * S
    hf = h.reshape(N, D)
    aff = jax.nn.softmax((hf @ w_router).astype(F32), axis=-1)
    cap = max(1, EC_CAPACITY * N // N_EXPERTS)
    gate, idx = lax.top_k(aff.T, cap)
    xe = hf[idx]
    hid = jax.nn.silu(jnp.einsum('ecd,edf->ecf', xe, wg)) * jnp.einsum('ecd,edf->ecf', xe, wu)
    ye = jnp.einsum('ecf,efd->ecd', hid, wd) * gate[..., None].astype(h.dtype)
    out = jnp.zeros_like(hf).at[idx.reshape(-1)].add(ye.reshape(-1, D))
    return out.reshape(B, S, D)

def trunk(x, p, weights):
    (norm_mix, w_in, qk_norm, sink_logit, conv_dw, conv_dw_b, conv_ln_g, conv_ln_b,
     gla_w2, gla_b2, gla_norm, w_branch, w_out, norm_ffn, w_router, w_gate_e, w_up_e,
     w_down_e, norm_ple, w_ple_gate, w_ple_proj, norm_final) = weights
    tables = position_tables(x.shape[1])
    for i in range(DEPTH):
        h = rmsnorm(x, norm_mix[i])
        x = x + mixer_block(h, w_in[i], qk_norm[i], sink_logit[i], conv_dw[i], conv_dw_b[i],
                            conv_ln_g[i], conv_ln_b[i], gla_w2[i], gla_b2[i], gla_norm[i],
                            w_branch[i], w_out[i], tables)
        x = x + expert_choice_ffn(rmsnorm(x, norm_ffn[i]), w_router[i], w_gate_e[i], w_up_e[i], w_down_e[i])
        x = x + jax.nn.sigmoid(rmsnorm(x, norm_ple[i]) @ w_ple_gate[i]) * (p[i] @ w_ple_proj[i])
    return rmsnorm(x, norm_final)

def setup_inputs(seed: int = 0) -> dict:
    key = jax.random.key(seed)
    ks = jax.random.split(key, 32)
    nrm = lambda k, shape, scale: jax.random.normal(k, shape, F32) * scale
    return {
        'x_prompt': nrm(ks[0], (BATCH, SEQ, D_MODEL), 1.0),
        'x_sample': nrm(ks[1], (DEC_BATCH, DEC_SEQ, D_MODEL), 1.0),
        'p_prompt': nrm(ks[2], (DEPTH, BATCH, SEQ, PLE_DIM), 1.0),
        'p_sample': nrm(ks[3], (DEPTH, DEC_BATCH, DEC_SEQ, PLE_DIM), 1.0),
        'norm_mix': 1.0 + nrm(ks[4], (DEPTH, D_MODEL), 0.02),
        'w_in': nrm(ks[5], (DEPTH, D_MODEL, IN_COLS), D_MODEL ** -0.5),
        'qk_norm': 1.0 + nrm(ks[6], (DEPTH, 2, HEAD_DIM), 0.02),
        'sink_logit': nrm(ks[7], (DEPTH, C_Q_HEADS), 0.5),
        'conv_dw': nrm(ks[8], (DEPTH, CONV_WIDTH, CONV_CH), CONV_WIDTH ** -0.5),
        'conv_dw_b': nrm(ks[9], (DEPTH, CONV_CH), 0.02),
        'conv_ln_g': 1.0 + nrm(ks[10], (DEPTH, CONV_CH), 0.02),
        'conv_ln_b': nrm(ks[11], (DEPTH, CONV_CH), 0.02),
        'gla_w2': nrm(ks[12], (DEPTH, 2, GLA_RANK, GLA_HEADS * GLA_DK), GLA_RANK ** -0.5),
        'gla_b2': nrm(ks[13], (DEPTH, 2, GLA_HEADS * GLA_DK), 0.02),
        'gla_norm': 1.0 + nrm(ks[14], (DEPTH, GLA_DV), 0.02),
        'w_branch': nrm(ks[15], (DEPTH, N_BRANCH, BRANCH_W, D_MODEL), BRANCH_W ** -0.5),
        'w_out': nrm(ks[16], (DEPTH, D_MODEL, D_MODEL), D_MODEL ** -0.5),
        'norm_ffn': 1.0 + nrm(ks[17], (DEPTH, D_MODEL), 0.02),
        'w_router': nrm(ks[18], (DEPTH, D_MODEL, N_EXPERTS), D_MODEL ** -0.5),
        'w_gate_e': nrm(ks[19], (DEPTH, N_EXPERTS, D_MODEL, EXPERT_FF), D_MODEL ** -0.5),
        'w_up_e': nrm(ks[20], (DEPTH, N_EXPERTS, D_MODEL, EXPERT_FF), D_MODEL ** -0.5),
        'w_down_e': nrm(ks[21], (DEPTH, N_EXPERTS, EXPERT_FF, D_MODEL), EXPERT_FF ** -0.5),
        'norm_ple': 1.0 + nrm(ks[22], (DEPTH, D_MODEL), 0.02),
        'w_ple_gate': nrm(ks[23], (DEPTH, D_MODEL, D_MODEL), D_MODEL ** -0.5),
        'w_ple_proj': nrm(ks[24], (DEPTH, PLE_DIM, D_MODEL), PLE_DIM ** -0.5),
        'norm_final': 1.0 + nrm(ks[25], (D_MODEL,), 0.02),
    }

def reference(x_prompt, x_sample, p_prompt, p_sample, norm_mix, w_in, qk_norm, sink_logit,
              conv_dw, conv_dw_b, conv_ln_g, conv_ln_b, gla_w2, gla_b2, gla_norm, w_branch,
              w_out, norm_ffn, w_router, w_gate_e, w_up_e, w_down_e, norm_ple, w_ple_gate,
              w_ple_proj, norm_final):
    weights = (norm_mix, w_in, qk_norm, sink_logit, conv_dw, conv_dw_b, conv_ln_g, conv_ln_b,
               gla_w2, gla_b2, gla_norm, w_branch, w_out, norm_ffn, w_router, w_gate_e, w_up_e,
               w_down_e, norm_ple, w_ple_gate, w_ple_proj, norm_final)
    y_prompt = trunk(x_prompt, p_prompt, weights)
    y_sample = trunk(x_sample, p_sample, weights)
    return (y_prompt, y_sample)


_drawn_inputs = setup_inputs


def setup_inputs(seed=0):
    import zlib

    import numpy as np

    out = dict(_drawn_inputs(seed))
    spreads = {}
    factors = {'qk_norm': 7.251,
     'sink_logit': 8.0,
     'conv_dw_b': 2.722,
     'conv_ln_g': 3.321,
     'conv_ln_b': 3.696,
     'gla_b2': 6.555,
     'gla_norm': 3.955,
     'norm_ffn': 3.21,
     'norm_ple': 8.0,
     'norm_final': 2.803}
    for name, (base, spread) in spreads.items():
        noise = np.random.default_rng([zlib.crc32(name.encode()), seed]).standard_normal(out[name].shape)
        drawn = base * np.exp(spread * noise) if base else spread * noise
        out[name] = __import__('jax').numpy.asarray(drawn.astype(out[name].dtype))
    for name, factor in factors.items():
        out[name] = (out[name] * factor).astype(out[name].dtype)
    return out
```

```python
from contextlib import ExitStack

import concourse.bass as bass
from concourse import mybir
import numpy as np

F32 = mybir.dt.float32
F32R = mybir.dt.float32r
I32 = mybir.dt.int32
U32 = mybir.dt.uint32
ALU = mybir.AluOpType
ACT = mybir.ActivationFunctionType
AX = mybir.AxisListType

DEPTH, D, SEQ, DEC = 2, 1024, 512, 256
TOK = SEQ + DEC
NT = TOK // 128
GROUPS = [(0, SEQ // 128), (SEQ // 128, NT)]
TILE_GROUP = [GROUPS[0]] * (SEQ // 128) + [GROUPS[1]] * (DEC // 128)
KT = D // 128
HD = 64
EPS = 1e-6
UC = 2592
IN_COLS = UC + 4 * D
NCH = 6
CW = UC // NCH
NB = 4
NE, CAPP, CAPS = 16, 2 * SEQ // 16, 2 * DEC // 16
CAP = CAPP + CAPS
FF = 1024
PLE = 256
CONVW = 31
PAD = CONVW // 2
ZW = PAD + SEQ + PAD + DEC + PAD
AW = ZW - 2 * PAD

QA, KA, VA, UB, UG, QC, KC, VC, QD, KD, VD, RD, ZL = (
    0, 256, 384, 512, 768, 1024, 1280, 1408, 1536, 1792, 2048, 2304, 2560)

ES = 24
S_W, S_G, S_O, S_E = 0, 4 * NCH, 4 * NCH + 16 * NB, 4 * NCH + 16 * NB + 8
S_P = S_E + ES * NE
SPL = S_P + 16
RAW, SPLIT = 8, 4

T_N0, T_G, T_M, T_N1 = 0, 12, 12 + 6 * NB, 24 + 6 * NB
T_E = T_N1 + 12
T_N2 = T_E + 4 * NE + 2
T_P = T_N2 + 12
TPL = T_P + 6
C_G, C_O, C_P, CPL = 6, 22, 24, 28
AA_G, AA_O, AA_P, AAPL = 36, 84, 96, 108
AD_P, ADPL = 48, 60

K_ID = 0
K_WM = 128
K_CUM = K_WM + 384
K_IND = K_CUM + 6 * 128
K_GM = K_IND + 2
K_RA = K_GM + 512
K_RC = K_RA + 2 * 4 * HD
K_N = K_RC + 2 * 4 * HD


def shape_constants():
    c = np.zeros((128, K_N), np.float32)
    i = np.arange(128)
    c[:, K_ID:K_ID + 128] = np.eye(128)
    c[:, K_WM:K_WM + 128] = np.where(i[None, :] >= i[:, None], 0, -1e30)
    c[:, K_WM + 256:K_WM + 384] = np.where(i[None, :] <= i[:, None], 0, -1e30)
    same = (i[:, None] // 64) == (i[None, :] // 64)
    j, q = i[:, None], i[None, :]
    jl = j % 64
    mats = [
        same & (j <= q), (same & (j <= q)) * 1 - (same & (jl <= 31)) * 1, same & (j > q),
        same & (j >= q), (same & (j >= q)) * 1 - (same & (jl >= 32)) * 1, same & (j < q),
    ]
    for n, m in enumerate(mats):
        c[:, K_CUM + n * 128:K_CUM + (n + 1) * 128] = np.asarray(m, np.float32) / 16
    c[:, K_IND] = (i < 64) / 16
    c[:, K_IND + 1] = (i >= 64) / 16
    for d in range(2):
        m = same & ((j <= q) if d == 0 else (j >= q))
        for p in range(2):
            c[:, K_GM + (2 * d + p) * 128:K_GM + (2 * d + p + 1) * 128] = m

    def tables(pos, dim):
        inv = np.float32(10000.0) ** (-np.arange(0, dim, 2, dtype=np.float32) / np.float32(dim))
        a = pos.astype(np.float32)[:, None] * inv[None, :]
        return np.cos(a), np.sin(a)

    s = np.arange(SEQ)
    rc, rs = tables(s // 64, 32)
    cc, cs = tables(s % 64, 32)
    tc, ts = tables(s, 64)
    ca = np.concatenate([rc, rc, cc, cc], 1)
    sa = np.concatenate([-rs, rs, -cs, cs], 1)
    cp = np.concatenate([tc, tc], 1)
    sp = np.concatenate([-ts, ts], 1)
    for n, m in enumerate([ca, sa, cp, sp]):
        c[:, K_RA + n * 256:K_RA + (n + 1) * 256] = m.reshape(4, 128, HD).transpose(1, 0, 2).reshape(128, 256)
    return c


def build(nc, x_p, x_s, p_p, p_s, norm_mix, w_in, qk_norm, sink, conv_w, conv_b, ln_g, ln_b, gla_w2, gla_b2,
          gla_norm, w_branch, w_out, norm_ffn, w_router, w_gate, w_up, w_down, norm_ple, w_pg, w_pp,
          norm_final, consts, y_p, y_s):
    ctx = ExitStack()
    with ctx:
        def sb(name, shape, dt=F32):
            return ctx.enter_context(nc.sbuf_tensor(name, shape, dt))

        def sem(name):
            return ctx.enter_context(nc.semaphore(name))

        x_d = nc.dram_tensor("x_res", [TOK, D], F32).ap()
        h2_d = nc.dram_tensor("h2_rows", [TOK, D], F32).ap()

        cst = sb("cst", [128, K_N])
        ident = cst[:, K_ID:K_ID + 128]
        raw = [sb(f"raw{i}", [128, 1024]) for i in range(RAW)]
        gqk = sb("gqk", [128, 6, HD])
        sink_b = sb("sink_b", [128, 4])
        cw = sb("cw", [128, 2, CONVW])
        cb = sb("cb", [128, 2])
        lng = sb("lng", [128, 256])
        lnb = sb("lnb", [128, 256])
        gng = sb("gng", [128, HD])
        w2b = sb("w2b", [33, 512])
        wr = sb("wr", [128, KT, NE])
        stage = sb("stage", [128, 2, 256])
        ms = sb("ms", [128, NT])
        rs = sb("rs", [128, NT])
        small = sb("small", [128, 64])
        nm = sb("nm", [128, 48])
        sm = sb("sm", [128, 48])
        sk = sb("sk", [128, 24])
        es = sb("es", [128, 24])
        rcp = sb("rcp", [128, 48])
        rqk = sb("rqk", [128, NT, 6])
        bns = sb("bns", [128, NT, 6])
        bnv = sb("bnv", [128, NT, 2])
        oss = sb("oss", [128, NT, 4])
        eps1, eps64 = sb("eps1", [128, 1]), sb("eps64", [128, 1])
        base = (nc.sbuf_base + 31) // 32 * 32
        H0 = base
        U0 = H0 + 2 * KT * TOK * 4
        M0 = U0 + (NT * UC * 4 + 31) // 32 * 32
        END = M0 + 4 * 8192 + 4 * TOK * 4
        fence = sb("fence", [128, (END - base) // 4])
        assert nc.sbuf_base <= nc.sbuf_usable_end

        def at(name, shape, off, dt=F32):
            return nc.alloc_sbuf_tensor_at(name, shape, dt, offset=off)

        hT = [at(f"hT{n}", [128, KT, TOK], H0 + n * KT * TOK * 4, F32R) for n in range(2)]
        hTf = at("hTf", [128, KT, TOK], H0)
        u = at("u", [128, NT, UC], U0)
        rows = at("rows", [128, NT, D], U0)
        gain = at("gain", [128, D], U0 + NT * D * 4)
        gsig = at("gsig", [128, NT, 512], U0 + (NT * D + D) * 4)
        prow = at("prow", [128, NT, PLE], U0 + (NT * D + D + NT * 512) * 4)
        whi = [at(f"whi{n}", [128, 1024], M0 + n * 4096, F32R) for n in range(SPLIT)]
        wlo = [at(f"wlo{n}", [128, 1024], M0 + (SPLIT + n) * 4096, F32R) for n in range(SPLIT)]
        oT = [at(f"oT{n}", [128, 2, TOK], M0 + 4 * 8192 + n * 2 * TOK * 4, F32R) for n in range(2)]
        ublk = u[:, :, 0:2048].rearrange("p t (b h n) -> p t b h n", h=2, n=256)
        e_at = [U0 + (NT * D + D) * 4]

        def moe(name, shape, dt=F32):
            n = 4
            for v in shape[1:]:
                n *= v
            off = e_at[0]
            e_at[0] = (off + n + 31) // 32 * 32
            assert e_at[0] <= M0
            return at(name, shape, off, dt)

        xe = moe("xe", [CAP, D])
        xeT = [moe(f"xeT{n}", [128, KT, CAP], F32R) for n in range(2)]
        sil = moe("sil", [CAP, FF])
        hidT = [moe(f"hidT{n}", [128, KT, CAP], F32R) for n in range(2)]
        ye = moe("ye", [CAP, D])
        lg = moe("lg", [128, NT, NE])
        lmx = moe("lmx", [128, NT])
        lsm = moe("lsm", [128, NT])
        scores = moe("scores", [48, SEQ])
        top = moe("top", [48, CAPP])
        topi = moe("topi", [48, CAPP], U32)
        pick = moe("pick", [NE, 2, CAP])
        idxT = moe("idxT", [CAP, NE + 1], U32)
        gateT = moe("gateT", [CAP, NE])
        idx_g = moe("idx_g", [CAP, 1], U32)
        idx_s = moe("idx_s", [CAP, 1], U32)
        m_at = [M0]

        def mix(name, shape):
            n = 4
            for v in shape[1:]:
                n *= v
            off = m_at[0]
            m_at[0] = (off + n + 31) // 32 * 32
            assert m_at[0] <= END, (name, m_at[0] - END)
            return at(name, shape, off)

        qkA = mix("qkA", [128, 3, TOK])
        qkC = mix("qkC", [128, 3, TOK])
        rA = mix("rA", [128, 2, 384])
        rC = mix("rC", [128, 2, 384])
        s1 = mix("s1", [128, 384])
        s2 = mix("s2", [128, 384])
        s3 = mix("s3", [128, 384])
        c1 = mix("c1", [128, 384])
        c2 = mix("c2", [128, 384])
        P = mix("P", [128, 2, 512])
        PT = mix("PT", [128, 2, 512])
        sC = s1, s2
        m_at[0] = M0
        zsg = mix("zsg", [128, 2, 256])
        zr = mix("zr", [128, 2, 256])
        zT = mix("zT", [128, 2, ZW])
        zacc = mix("zacc", [128, 2, AW])
        zn = mix("zn", [128, 2, 256])
        m_at[0] = M0
        la = mix("la", [128, NT, 512])
        kvs = mix("kvs", [128, 2 * NT, 4, HD])
        E3 = mix("E3", [128, 3, 512])
        TT = mix("TT", [128, 3, 512])
        att = mix("att", [128, 2, 512])
        dec = mix("dec", [128, NT, 8])
        zlT = mix("zlT", [33, 128])
        osq = mix("osq", [128, 256])

        PS = ctx.enter_context(nc.psum_tensor("PS", [128, 8, 512], F32))

        s_cst = sem("s_cst")
        s_init = sem("s_init")
        s_raw = [sem(f"s_raw{i}") for i in range(RAW)]
        s_hi = sem("s_hi")
        s_lo = sem("s_lo")
        s_used = sem("s_used")
        s_xin = [sem(f"s_xin{i}") for i in range(NT)]
        s_gain = sem("s_gain")
        s_small = sem("s_small")
        s_smallx = sem("s_smallx")
        s_sq = sem("s_sq")
        s_eps = sem("s_eps")
        s_ssq, s_rqk = sem("s_ssq"), sem("s_rqk")
        s_bn, s_bnr = sem("s_bn"), sem("s_bnr")
        s_oss, s_or = sem("s_oss"), sem("s_or")
        s_xn = sem("s_xn")
        s_tp = sem("s_tp")
        s_thi = sem("s_thi")
        s_tlo = sem("s_tlo")
        s_acc = sem("s_acc")
        s_ea = sem("s_ea")
        s_ed = sem("s_ed")
        s_xadd = sem("s_xadd")
        s_rA, s_rC = sem("s_rA"), sem("s_rC")
        s_tA, s_tC = sem("s_tA"), sem("s_tC")
        s_qA, s_qC = sem("s_qA"), sem("s_qC")
        s_sc = sem("s_sc")
        s_nm = sem("s_nm")
        s_p = sem("s_p")
        s_pt = sem("s_pt")
        s_ptA, s_ptC = sem("s_ptA"), sem("s_ptC")
        s_pv = sem("s_pv")
        s_sk = sem("s_sk")
        s_es = sem("s_es")
        s_o = sem("s_o")
        s_zpad = sem("s_zpad")
        s_zs = sem("s_zs")
        s_zr = sem("s_zr")
        s_zt = sem("s_zt")
        s_zT = sem("s_zT")
        s_conv = sem("s_conv")
        s_zb = sem("s_zb")
        s_zn = sem("s_zn")
        s_ob = sem("s_ob")
        s_az = sem("s_az")
        s_g = [sem(f"s_g{i}") for i in range(11)]
        s_scan = sem("s_scan")
        s_h = [sem(f"s_h{i}") for i in range(11)]
        s_od = sem("s_od")
        s_mz = sem("s_mz")
        s_st = sem("s_st")
        s_h2 = [sem(f"s_h2{i}") for i in range(2)]
        s_rt = sem("s_rt")
        s_lm = sem("s_lm")
        s_le = sem("s_le")
        s_af = sem("s_af")
        s_aft = sem("s_aft")
        s_scz = sem("s_scz")
        s_pick = sem("s_pick")
        s_pickt = sem("s_pickt")
        s_idx = sem("s_idx")
        s_ga = sem("s_ga")
        s_sil = sem("s_sil")
        s_hid = sem("s_hid")
        s_y = sem("s_y")
        s_sca = sem("s_sca")
        s_pin = sem("s_pin")
        s_yo = sem("s_yo")

        w_in_f = w_in.rearrange("l k n -> (l k) n")
        w_br_f = w_branch.rearrange("l b k n -> (l b k) n")
        w_out_f = w_out.rearrange("l k n -> (l k) n")
        wg_f = w_gate.rearrange("l e k n -> (l e k) n")
        wu_f = w_up.rearrange("l e k n -> (l e k) n")
        wd_f = w_down.rearrange("l e k n -> (l e k) n")
        wpg_f = w_pg.rearrange("l k n -> (l k) n")
        wpp_f = w_pp.rearrange("l k n -> (l k) n")
        block = ctx.enter_context(nc.Block())

        def cols(tile, nk, n):
            return tile[:, 0:nk * n].rearrange("p (k n) -> p k n", n=n)

        def lo_count(j):
            return j + 1 if j < T_N1 else j + 1 - 12
        TLL = TPL - 12

        def pt_done(l, m):
            return (s_ptA, l * 24 + m + 1) if m < 24 else (s_ptC, l * 24 + m - 24 + 1)

        def wait_alone(eng, sem_, value):
            value = eng.to_reg(value)
            eng.wait_ge(s_cst, 16)
            eng.wait_ge(sem_, value)

        def accumulated(eng, chunks, step_, t):
            if t < NT - 1:
                eng.wait_ge(s_acc, chunks * (NT - 1) + (t + 1))
            else:
                eng.wait_ge(s_used, step_ + (1 + SPLIT))

        @block.sync
        def _(sp):
            sp.dma_start(cst[:], consts).then_inc(s_cst, 16)
            sp.dma_start(x_d[0:SEQ, :], x_p.rearrange("a s d -> (a s) d")).then_inc(s_init, 16)
            sp.dma_start(x_d[SEQ:TOK, :], x_s.rearrange("a s d -> (a s) d")).then_inc(s_init, 16)

            def load(step, j, src, r0, nk, c0, n):
                sp.wait_ge(s_lo, step + 1)
                sp.dma_start(cols(raw[j % RAW], nk, n),
                             src[bass.ds(r0, nk * 128), :][:, bass.ds(c0, n)].rearrange("(k p) n -> p k n", p=128)
                             ).then_inc(s_raw[j % RAW], 16)

            with sp.Fori(0, DEPTH) as l:
                with sp.Fori(0, NCH // 2) as i:
                    for j in range(8):
                        load(l * SPL + i * 8 + j, j, w_in_f, l * D + (j % 4) * 256, 2,
                             i * (2 * CW) + (j // 4) * CW, CW)
                with sp.Fori(0, NB) as i:
                    for c in range(2):
                        for j in range(4):
                            load(l * SPL + i * 16 + (S_G + 8 * c + j), j, w_in_f, l * D + j * 256, 2,
                                 i * D + (UC + c * 512), 512)
                        for j in range(4):
                            load(l * SPL + i * 16 + (S_G + 8 * c + 4 + j), 4 + j, w_br_f,
                                 l * (NB * 256) + i * 256 + (j % 2) * 128, 1, c * 512 + (j // 2) * 256, 256)
                for j in range(8):
                    load(l * SPL + (S_O + j), j, w_out_f, l * D + (j % 4) * 256, 2, (j // 4) * 512, 512)
                with sp.Fori(0, NE) as e:
                    for c in range(2):
                        for n, src in enumerate((wg_f, wu_f)):
                            for j in range(4):
                                s = 8 * c + 4 * n + j
                                load(l * SPL + e * ES + (S_E + s), s, src, l * (NE * D) + e * D + j * 256, 2,
                                     c * 512, 512)
                    for j in range(8):
                        load(l * SPL + e * ES + (S_E + 16 + j), j, wd_f,
                             l * (NE * FF) + e * FF + (j // 4) * 512 + (j % 2) * 256, 2, (j // 2 % 2) * 512, 512)
                for c in range(2):
                    for j in range(4):
                        load(l * SPL + (S_P + 8 * c + j), j, wpg_f, l * D + j * 256, 2, c * 512, 512)
                    for j in range(4):
                        load(l * SPL + (S_P + 8 * c + 4 + j), 4 + j, wpp_f, l * PLE + (j % 2) * 128, 1,
                             c * 512 + (j // 2) * 256, 256)
            for t in range(NT):
                sp.wait_ge(s_xn, DEPTH * 18 + t + 1)
                dst = y_p[0, t * 128:(t + 1) * 128, :] if t < 4 else y_s[0, (t - 4) * 128:(t - 3) * 128, :]
                sp.dma_start(dst, rows[:, t, :]).then_inc(s_yo, 16)
            sp.wait_ge(s_yo, 16 * NT)

        @block.gpsimd
        def _(pool):
            def wait(s, value):
                if isinstance(value, int):
                    pool.wait_ge(s, value)
                else:
                    wait_alone(pool, s, value)

            wait(s_init, 32)
            wait(s_cst, 16)

            def load_x(row):
                for t in range(NT):
                    pool.dma_start(rows[:, t, :], x_d[t * 128:(t + 1) * 128, :]).then_inc(s_xin[t], 16)
                pool.dma_start(gain[:], row.broadcast_to([128, D])).then_inc(s_gain, 16)

            nc.gpsimd.memset(w2b[:], 0.0)
            nc.gpsimd.memset(eps1[:], EPS)
            nc.gpsimd.memset(eps64[:], HD * EPS)
            pool.drain().then_inc(s_eps, 1)
            wait(s_cst, 16)
            with pool.Fori(0, DEPTH) as l:
                load_x(norm_mix[bass.ds(l, 1), :])
                for k in range(2):
                    src = qk_norm.rearrange("l k d -> l (k d)")[bass.ds(l, 1), k * HD:(k + 1) * HD]
                    for h in ((0, 1, 2, 3) if k == 0 else (4, 5)):
                        pool.dma_start(gqk[:, h, :], src.broadcast_to([128, HD])).then_inc(s_small, 16)
                pool.dma_start(sink_b[:], sink[bass.ds(l, 1), :].broadcast_to([128, 4])).then_inc(s_small, 16)
                pool.dma_start(cw[:], conv_w.rearrange("l c w -> (l c) w")[bass.ds(l * 256, 256), :]
                               .rearrange("(h p) w -> p h w", p=128)).then_inc(s_small, 16)
                pool.dma_start(cb[:], conv_b.rearrange("l (c o) -> (l c) o", o=1)[bass.ds(l * 256, 256), :]
                               .rearrange("(h p) o -> p (h o)", p=128), allow_slow_non_contiguous=True).then_inc(s_small, 16)
                pool.dma_start(lng[:], ln_g[bass.ds(l, 1), :].broadcast_to([128, 256])).then_inc(s_small, 16)
                pool.dma_start(lnb[:], ln_b[bass.ds(l, 1), :].broadcast_to([128, 256])).then_inc(s_small, 16)
                pool.dma_start(gng[:], gla_norm[bass.ds(l, 1), :].broadcast_to([128, HD])).then_inc(s_small, 16)
                for n in range(2):
                    pool.dma_start(w2b[16 * n:16 * n + 16, 256 * n:256 * n + 256],
                                   gla_w2.rearrange("l n r c -> (l n r) c")[bass.ds(l * 32 + n * 16, 16), :]
                                   ).then_inc(s_small, 16)
                pool.dma_start(w2b[32:33, :], gla_b2.rearrange("l n c -> l (n c)")[bass.ds(l, 1), :]).then_inc(s_small, 16)
                pool.dma_start(wr[:], w_router.rearrange("l k n -> (l k) n")[bass.ds(l * D, D), :]
                               .rearrange("(k p) n -> p k n", p=128)).then_inc(s_small, 16)
                NSM = 16 * 16
                wait(s_small, l * NSM + NSM)
                nc.gpsimd.tensor_scalar(gqk[:, 4:6, :], gqk[:, 4:6, :], 8.0, None, ALU.mult)
                nc.gpsimd.tensor_scalar(gng[:], gng[:], 8.0, None, ALU.mult).then_inc(s_smallx, 1)

                wait(s_ea, l * AAPL + 36 + 6)
                for t in range(NT):
                    pt = t - TILE_GROUP[t][0]
                    cs_ = cst[:, K_RC + pt * HD:K_RC + (pt + 1) * HD]
                    sn_ = cst[:, K_RC + 256 + pt * HD:K_RC + 256 + (pt + 1) * HD]
                    x = u[:, t, QC:QC + 384].rearrange("p (h d) -> p h d", d=HD)
                    a = c1[:].rearrange("p (h d) -> p h d", d=HD)
                    b = c2[:].rearrange("p (h d) -> p h d", d=HD)
                    nc.gpsimd.tensor_tensor(a, x, cs_.unsqueeze(1).broadcast_to([128, 6, HD]), ALU.mult)
                    for hf in range(2):
                        o, i_ = 32 * hf, 32 * (1 - hf)
                        nc.gpsimd.tensor_tensor(b[:, :, o:o + 32], x[:, :, i_:i_ + 32],
                                                sn_[:, o:o + 32].unsqueeze(1).broadcast_to([128, 6, 32]), ALU.mult)
                    pool.drain()
                    if t >= 2:
                        wait(s_tC, l * NT + t - 1)
                    r = rC[:, t % 2, :]
                    nc.gpsimd.tensor_tensor(r[:, 0:256].rearrange("p (a g d) -> p g a d", g=2, d=HD),
                                            c1[:, 0:256].rearrange("p (g a d) -> p g a d", g=2, d=HD),
                                            c2[:, 0:256].rearrange("p (g a d) -> p g a d", g=2, d=HD), ALU.add)
                    nc.gpsimd.tensor_tensor(r[:, 256:384], c1[:, 256:384], c2[:, 256:384], ALU.add)
                    pool.drain().then_inc(s_rC, 1)

                wait(s_o, l * 12 + 12)
                nc.gpsimd.memset(zT[:], 0.0).then_inc(s_zpad, 1)
                wait(s_ob, l * NT + NT)
                nc.gpsimd.memset(att[:], 0.0)
                pool.drain()
                nc.gpsimd.memset(zlT[32:33, :], 1.0)
                pool.drain().then_inc(s_az, 1)
                wait(s_od, l + 1)
                for t in range(NT):
                    nc.gpsimd.memset(ublk[:, t, :, 1, :], 0.0)
                pool.drain().then_inc(s_mz, 1)

                for t in range(NT):
                    wait(s_ea, l * AAPL + (AA_O + 6 + t + 1) + 6)
                    pool.dma_start(x_d[t * 128:(t + 1) * 128, :], rows[:, t, :], accum_op=ALU.add).then_inc(s_xadd, 16)
                wait(s_xadd, l * 192 + 96)
                load_x(norm_ffn[bass.ds(l, 1), :])

                wait(s_xn, l * 18 + 12)
                nc.gpsimd.memset(scores[:], -1.0).then_inc(s_scz, 1)
                for n in range(2):
                    wait(s_h2[n], l * 48 + 48)
                wait(s_idx, l + 1)
                nc.gpsimd.tensor_copy(idx_g[:], idxT[:, 0:1])
                pool.drain()
                pool.indirect_dma_start(out=xe[:], out_offset=None, in_=h2_d,
                                        in_offset=bass.IndirectOffsetOnAxis(ap=idx_g[:, 0:1], axis=0)).then_inc(s_ga, 16)
                with pool.Fori(0, NE) as e:
                    nc.gpsimd.tensor_copy(idx_s[:], idxT[:, bass.ds(e, 1)])
                    wait(s_tp, l * TPL + e * 4 + (T_E + 2))
                    wait(s_ga, l * (17 * 16) + e * 16 + 16)
                    nc.gpsimd.tensor_copy(idx_g[:], idxT[:, bass.ds(e + 1, 1)])
                    pool.drain()
                    pool.indirect_dma_start(out=xe[:], out_offset=None, in_=h2_d,
                                            in_offset=bass.IndirectOffsetOnAxis(ap=idx_g[:, 0:1], axis=0)
                                            ).then_inc(s_ga, 16)
                    wait(s_y, l * 32 + e * 2 + 2)
                    pool.indirect_dma_start(out=x_d, out_offset=bass.IndirectOffsetOnAxis(ap=idx_s[:, 0:1], axis=0),
                                            in_=ye[:], in_offset=None, compute_op=ALU.add).then_inc(s_sca, 16)
                    wait(s_sca, l * 256 + e * 16 + 16)

                load_x(norm_ple[bass.ds(l, 1), :])
                wait(s_used, l * SPL + S_P + 2)
                for n, (src, t0, nt) in enumerate(((p_p, 0, 4), (p_s, 4, 2))):
                    pool.dma_start(prow[:, t0:t0 + nt, :],
                                   src.rearrange("l a s d -> (l a s) d")[bass.ds(l * (nt * 128), nt * 128), :]
                                   .rearrange("(t p) d -> p t d", p=128)).then_inc(s_pin, 16)
                for t in range(NT):
                    wait(s_ed, l * ADPL + (AD_P + 6 + t + 1) + 6)
                    pool.dma_start(x_d[t * 128:(t + 1) * 128, :], rows[:, t, :], accum_op=ALU.add).then_inc(s_xadd, 16)
                wait(s_xadd, l * 192 + 192)
            load_x(norm_final.rearrange("(a d) -> a d", a=1))

        @block.scalar
        def _(act):
            A = nc.scalar.activation
            act.drain().then_inc(s_thi, 2)
            act.drain().then_inc(s_ea, 6)
            act.wait_ge(s_eps, 1)

            def hi(step, j, w):
                act.wait_ge(s_raw[j % RAW], (step - j) * 2 + (j // RAW * 16 + 16))
                act.wait_ge(s_used, step + 1)
                A(whi[j % SPLIT][:, 0:w], raw[j % RAW][:, 0:w], ACT.Copy).then_inc(s_hi, 1)

            def mean_square(l3, t):
                act.wait_ge(s_xin[t], l3 * 16 + 16)
                A(PS[:, 0:2, :], rows[:, t, :].rearrange("p (a n) -> p a n", a=2), ACT.Square, scale=1.0 / 32,
                  accum_out=ms[:, t:t + 1])
                act.drain()
                A(ms[:, t:t + 1], ms[:, t:t + 1], ACT.Sqrt, bias=eps1[:]).then_inc(s_sq, 1)

            def t_hi(j, dst, src):
                act.wait_ge(s_tp, j + 1)
                A(dst, src, ACT.Copy).then_inc(s_thi, 1)

            def tbank(j, n=4, w=128):
                return PS[:, 6 + j % 2, 0:n * w].rearrange("p (k n) -> p k n", n=w)

            def norm(l, n, j0, dst):
                mean_square(l * 3 + n, 0)
                mean_square(l * 3 + n, 1)
                for t in range(NT):
                    if t + 2 < NT:
                        mean_square(l * 3 + n, t + 2)
                    for c in range(2):
                        t_hi(l * TPL + (j0 + 2 * t + c), dst[:, 4 * c:4 * c + 4, t * 128:(t + 1) * 128], tbank(c))

            with act.Fori(0, DEPTH) as l:
                norm(l, 0, T_N0, hT[0])

                def u_out(ck, t):
                    accumulated(act, l * CPL + ck, l * SPL + ck * 4 + 3, t)
                    A(u[:, t, bass.ds(ck * CW, CW)], PS[:, t, 0:CW], ACT.Copy).then_inc(s_ea, 1)

                def w_chunk(ck, j, ahead):
                    for n in range(3 if ahead else 0):
                        hi(l * SPL + ck * 4 + (4 + n), j + 4 + n, 2 * CW)
                    for t in range(NT):
                        u_out(ck, t)
                    if ahead:
                        hi(l * SPL + ck * 4 + 7, j + 7, 2 * CW)

                for n in range(4):
                    hi(l * SPL + n, n, 2 * CW)
                with act.Fori(0, 2) as i:
                    for j in range(2):
                        w_chunk(i * 2 + j, 4 * j, True)
                w_chunk(4, 0, True)
                w_chunk(5, 4, False)

                act.wait_ge(s_ssq, l + 1)
                A(rqk[:], rqk[:], ACT.Sqrt, bias=eps64[:]).then_inc(s_rqk, 1)
                for t in range(NT):
                    act.wait_ge(s_tA, l * NT + t + 1)
                    A(qkA[:, :, t * 128:(t + 1) * 128], PS[:, 6, 0:384].rearrange("p (k n) -> p k n", n=128),
                      ACT.Copy).then_inc(s_qA, 1)
                    act.wait_ge(s_tC, l * NT + t + 1)
                    A(qkC[:, :, t * 128:(t + 1) * 128], PS[:, 7, 0:384].rearrange("p (k n) -> p k n", n=128),
                      ACT.Copy).then_inc(s_qC, 1)
                for n in range(49):
                    if n < 48:
                        kind, t, h, k0, nk = unit(n)
                        act.wait_ge(s_nm, l * 48 + n + 1)
                        if n >= 2:
                            act.wait_ge(s_pt, l * 48 + n - 1)
                        src = PS[:, n % 2, 0:nk * 128] if kind == "A" else sC[n % 2][:, 0:nk * 128]
                        A(P[:, n % 2, 0:nk * 128], src, ACT.Exp, bias=nm[:, n:n + 1],
                          accum_out=sm[:, n:n + 1]).then_inc(s_p, 1)
                    if n >= 1 and unit(n - 1)[0] == "C":
                        m = n - 1
                        kind, t, h, k0, nk = unit(m)
                        act.wait_ge(s_pt, l * 48 + m + 1)
                        act.wait_ge(s_pv, l * 48 + m - 1)
                        A(PT[:, m % 2, 0:nk * 128], PS[:, 2 + m % 2, 0:nk * 128], ACT.Copy).then_inc(s_ptC, 1)
                        if h == 3:
                            act.wait_ge(s_sk, l * NT + t + 1)
                            A(es[:, 4 * t:4 * t + 4], sk[:, 4 * t:4 * t + 4], ACT.Exp).then_inc(s_es, 1)

                act.wait_ge(s_o, l * 12 + 12)
                act.wait_ge(s_zpad, l + 1)
                for t in range(NT + 1):
                    if t < NT:
                        if t >= 2:
                            act.wait_ge(s_zr, l * NT + t - 1)
                        A(zsg[:, t % 2, :], u[:, t, UG:UG + 256], ACT.Sigmoid).then_inc(s_zs, 1)
                    if t >= 1:
                        m = t - 1
                        act.wait_ge(s_zt, l * NT + m + 1)
                        z0 = PAD + m * 128 + (PAD if m >= 4 else 0)
                        A(zT[:, :, z0:z0 + 128], PS[:, m % 2, 0:256].rearrange("p (c n) -> p c n", c=2),
                          ACT.Copy).then_inc(s_zT, 1)
                act.wait_ge(s_bn, l + 1)
                A(bnv[:, :, 1], bnv[:, :, 1], ACT.Sqrt, bias=eps1[:]).then_inc(s_bnr, 1)
                for t in range(NT):
                    act.wait_ge(s_zn, l * NT + t + 1)
                    A(u[:, t, UB:UB + 256], zn[:, t % 2, :], ACT.Silu).then_inc(s_ob, 1)
                A(u[:, :, RD:RD + 256], u[:, :, RD:RD + 256], ACT.Silu)
                act.drain().then_inc(s_g[10], 1)

                act.wait_ge(s_az, l + 1)
                for n in range(NT + 1):
                    buf = (E3 if n % 2 == 0 else TT)
                    old = (TT if n % 2 == 0 else E3)
                    if n < NT:
                        act.wait_ge(s_g[0], l * NT + n + 1)
                        A(zlT[0:32, :], PS[0:32, 0, 0:128], ACT.Copy).then_inc(s_g[1], 1)
                    if n >= 1:
                        act.wait_ge(s_g[5], l * NT + n)
                        A(old[:, 1, :], PS[:, 2, :], ACT.Exp)
                        A(dec[:, n - 1, :], PS[:, 3, 0:8], ACT.Exp)
                        act.drain().then_inc(s_g[6], 1)
                    if n < NT:
                        act.wait_ge(s_g[2], l * NT + n + 1)
                        A(buf[:, 0, :], PS[:, 1, :], ACT.Abs)
                        act.drain()
                        A(buf[:, 0, :], buf[:, 0, :], ACT.Exp, scale=-1.0)
                        act.drain()
                        A(buf[:, 0, :], buf[:, 0, :], ACT.Ln, bias=1.0).then_inc(s_g[3], 1)
                act.wait_ge(s_scan, l + 1)
                for t in range(NT):
                    act.wait_ge(s_h[0], l * NT + t + 1)
                    A(E3[:, 0, :], PS[:, 0, :], ACT.Exp)
                    A(E3[:, 1, :], PS[:, 0, :], ACT.Exp, scale=-1.0)
                    A(E3[:, 2, :], PS[:, 1, :], ACT.Exp)
                    act.drain().then_inc(s_h[1], 1)
                    act.wait_ge(s_h[3], l * NT + t + 1)
                    A(TT[:, 0, :], PS[:, 2, :], ACT.Copy)
                    A(TT[:, 1, :], PS[:, 3, :], ACT.Copy)
                    act.drain().then_inc(s_h[4], 1)

                act.wait_ge(s_oss, l + 1)
                A(oss[:], oss[:], ACT.Sqrt, bias=eps64[:]).then_inc(s_or, 1)
                act.wait_ge(s_od, l + 1)
                act.wait_ge(s_mz, l + 1)
                for n in range(4):
                    hi(l * SPL + (S_G + n), n, 1024)
                with act.Fori(0, NB) as i:
                    for t in range(NT):
                        t_hi(l * TPL + i * 6 + (T_G + t), oT[0][:, :, t * 128:(t + 1) * 128], tbank(t, 2))
                    for c in range(2):
                        s = l * SPL + i * 16 + (S_G + 8 * c)
                        for n in range(4, 7):
                            hi(s + n, n, 256)
                        for t in range(NT):
                            accumulated(act, l * CPL + i * 4 + (C_G + 2 * c), s + 3, t)
                            A(u[:, t, 2048:2560], PS[:, t, :], ACT.Sigmoid).then_inc(s_ea, 1)
                        hi(s + 7, 7, 256)
                        for n in range(8, 12):
                            hi(s + n, n, 1024)
                for t in range(NT):
                    for c in range(2):
                        t_hi(l * TPL + (T_M + 2 * t + c), hT[0][:, 4 * c:4 * c + 4, t * 128:(t + 1) * 128], tbank(c))
                for c in range(2):
                    for n in range(4, 7):
                        hi(l * SPL + (S_O + 4 * c + n), 4 * c + n, 1024)
                    for t in range(NT):
                        accumulated(act, l * CPL + (C_O + c), l * SPL + (S_O + 4 * c + 3), t)
                        A(rows[:, t, c * 512:(c + 1) * 512], PS[:, t, :], ACT.Copy).then_inc(s_ea, 1)
                    hi(l * SPL + (S_O + 4 * c + 7), 4 * c + 7, 1024)

                mean_square(l * 3 + 1, 0)
                mean_square(l * 3 + 1, 1)
                for t in range(NT):
                    if t + 2 < NT:
                        mean_square(l * 3 + 1, t + 2)
                    for c in range(2):
                        t_hi(l * TPL + (T_N1 + 2 * t + c), hTf[:, 4 * c:4 * c + 4, t * 128:(t + 1) * 128], tbank(c))
                    act.dma_start(h2_d[t * 128:(t + 1) * 128, :], rows[:, t, :]).then_inc(s_h2[t % 2], 16)
                act.wait_ge(s_lm, l + 1)
                A(lg[:], lg[:], ACT.Exp).then_inc(s_le, 1)
                for c in range(2):
                    t_hi(l * TPL + (T_E + c), xeT[0][:, 4 * c:4 * c + 4, :], tbank(c, 4, CAP))
                with act.Fori(0, NE) as e:
                    for s in range(ES):
                        done = l * SPL + e * ES + (S_E + s + 1 + SPLIT)
                        j = l * TPL + e * 4 + (T_E + 2)
                        if s in (3, 11):
                            c = s // 8
                            act.wait_ge(s_used, done)
                            A(sil[:, c * 512:(c + 1) * 512], PS[0:CAP, c, :], ACT.Silu).then_inc(s_sil, 1)
                        if s == 11:
                            t_hi(j, hidT[0][:, 0:4, :], tbank(0, 4, CAP))
                        if s == 17:
                            t_hi(j + 1, hidT[0][:, 4:8, :], tbank(1, 4, CAP))
                        if s == 19:
                            t_hi(j + 2, xeT[0][:, 0:4, :], tbank(0, 4, CAP))
                        if s == 21:
                            t_hi(j + 3, xeT[0][:, 4:8, :], tbank(1, 4, CAP))
                        if s in (21, 23):
                            c = (s - 21) // 2
                            wait_alone(act, s_used, done)
                            A(ye[:, c * 512:(c + 1) * 512], PS[0:CAP, 4 + c, :], ACT.Copy,
                              scale=gateT[:, bass.ds(e, 1)]).then_inc(s_y, 1)
                        hi(l * SPL + e * ES + (S_E + s + 4), s + 4, 1024)

                norm(l, 2, T_N2, hT[0])
                for t in range(NT):
                    t_hi(l * TPL + (T_P + t), oT[0][:, :, t * 128:(t + 1) * 128], tbank(t, 2))
                for c in range(2):
                    s = l * SPL + (S_P + 8 * c)
                    for n in range(4, 7):
                        hi(s + n, n, 256)
                    for t in range(NT):
                        accumulated(act, l * CPL + (C_P + 2 * c), s + 3, t)
                        if c == 1:
                            act.wait_ge(s_ed, l * ADPL + (AD_P + t + 1) + 6)
                        A(gsig[:, t, :], PS[:, t, :], ACT.Sigmoid).then_inc(s_ea, 1)
                    hi(s + 7, 7, 256)
                    if c == 0:
                        for n in range(8, 12):
                            hi(s + n, n, 1024)
            for t in range(NT):
                mean_square(DEPTH * 3, t)

        @block.vector
        def _(dve):
            V = nc.vector
            dve.drain().then_inc(s_lo, RAW)
            dve.drain().then_inc(s_tlo, 2)
            dve.drain().then_inc(s_ed, 6)

            def lo(step, j, w):
                dve.wait_ge(s_hi, step + 1)
                V.tensor_tensor(wlo[j % SPLIT][:, 0:w], raw[j % RAW][:, 0:w], whi[j % SPLIT][:, 0:w].bitcast(F32),
                                ALU.subtract).then_inc(s_lo, 1)

            def t_lo(j, dst, src, hi_part):
                dve.wait_ge(s_thi, j + 1 + 2)
                V.tensor_tensor(dst, src, hi_part.bitcast(F32), ALU.subtract).then_inc(s_tlo, 1)

            def tbank(j, n=4, w=128):
                return PS[:, 6 + j % 2, 0:n * w].rearrange("p (k n) -> p k n", n=w)

            def normalise(l3, sq, t):
                if t == 0:
                    dve.wait_ge(s_gain, l3 * 16 + 16)
                dve.wait_ge(s_sq, sq + t + 1)
                V.reciprocal(rs[:, t:t + 1], ms[:, t:t + 1])
                dve.drain()
                V.scalar_tensor_tensor(rows[:, t, :], rows[:, t, :], rs[:, t:t + 1], gain[:], ALU.mult,
                                       ALU.mult).then_inc(s_xn, 1)

            def norm(l, n, j0):
                normalise(l * 3 + n, l * 18 + n * 6, 0)
                normalise(l * 3 + n, l * 18 + n * 6, 1)
                for t in range(NT):
                    for c in range(2):
                        k, s = slice(4 * c, 4 * c + 4), slice(t * 128, (t + 1) * 128)
                        t_lo(l * TPL + (j0 + 2 * t + c), hT[1][:, k, s], tbank(c), hT[0][:, k, s])
                    if t + 2 < NT:
                        normalise(l * 3 + n, l * 18 + n * 6, t + 2)

            def bc(ap, n):
                return ap.unsqueeze(2).broadcast_to([128, ap.shape[1], n])

            def heads(ap):
                return ap.rearrange("p (h d) -> p h d", d=HD)

            dve.wait_ge(s_cst, 16)
            with dve.Fori(0, DEPTH) as l:
                norm(l, 0, T_N0)
                with dve.Fori(0, NCH // 2) as i:
                    for j in range(8):
                        lo(l * SPL + i * 8 + j, j, 2 * CW)

                dve.wait_ge(s_smallx, l + 1)
                dve.wait_ge(s_ea, l * AAPL + 36 + 6)
                dve.wait_ge(s_used, l * SPL + (S_G + SPLIT))
                for t in range(NT):
                    x = u[:, t, QA:QA + 384]
                    V.tensor_tensor(s3[:] if t % 2 else s1[:], x, x, ALU.mult)
                    dve.drain()
                    V.tensor_reduce(rqk[:, t, :], heads(s3[:] if t % 2 else s1[:]), AX.X, ALU.add)
                dve.drain().then_inc(s_ssq, 1)
                dve.wait_ge(s_rqk, l + 1)
                V.reciprocal(rqk[:], rqk[:])
                dve.drain()
                for t in range(NT):
                    pt = t - TILE_GROUP[t][0]
                    cs_ = cst[:, K_RA + pt * HD:K_RA + (pt + 1) * HD]
                    sn_ = cst[:, K_RA + 256 + pt * HD:K_RA + 256 + (pt + 1) * HD]
                    x = u[:, t, QA:QA + 384]
                    V.tensor_tensor(heads(s2[:]), heads(x), bc(rqk[:, t, :], HD), ALU.mult)
                    dve.drain()
                    V.tensor_tensor(s2[:], s2[:], gqk[:].rearrange("p h d -> p (h d)"), ALU.mult)
                    dve.drain()
                    V.tensor_tensor(heads(s1[:]), heads(s2[:]), cs_.unsqueeze(1).broadcast_to([128, 6, HD]), ALU.mult)
                    for hf in range(2):
                        o, i_ = 16 * hf, 16 * (1 - hf)
                        V.tensor_tensor(s3[:].rearrange("p (h a d) -> p h a d", a=2, d=32)[:, :, :, o:o + 16],
                                        s2[:].rearrange("p (h a d) -> p h a d", a=2, d=32)[:, :, :, i_:i_ + 16],
                                        sn_.rearrange("p (a d) -> p a d", d=32)[:, :, o:o + 16].unsqueeze(1)
                                        .broadcast_to([128, 6, 2, 16]), ALU.mult)
                    dve.drain()
                    if t >= 2:
                        dve.wait_ge(s_tA, l * NT + t - 1)
                    r = rA[:, t % 2, :]
                    V.tensor_tensor(r[:, 0:256].rearrange("p (a g d) -> p g a d", g=2, d=HD),
                                    s1[:, 0:256].rearrange("p (g a d) -> p g a d", g=2, d=HD),
                                    s3[:, 0:256].rearrange("p (g a d) -> p g a d", g=2, d=HD), ALU.add)
                    V.tensor_tensor(r[:, 256:384], s1[:, 256:384], s3[:, 256:384], ALU.add)
                    dve.drain().then_inc(s_rA, 1)

                for n in range(51):
                    if n < 48:
                        kind, t, h, k0, nk = unit(n)
                        dve.wait_ge(s_sc, l * 48 + n + 1)
                        s = PS[:, n % 2, 0:nk * 128]
                        if kind == "A":
                            V.tensor_reduce(nm[:, n:n + 1], s, AX.X, ALU.max, negate=True).then_inc(s_nm, 1)
                        else:
                            m0 = K_WM + (k0 - (t - 1)) * 128
                            if n >= 26:
                                dve.wait_ge(s_p, l * 48 + n - 1)
                            V.scalar_tensor_tensor(sC[n % 2][:, 0:nk * 128], s, 0.125, cst[:, m0:m0 + nk * 128],
                                                   ALU.mult, ALU.add)
                            dve.drain()
                            V.tensor_reduce(small[:, 16:17], sC[n % 2][:, 0:nk * 128], AX.X, ALU.max)
                            dve.drain()
                            V.tensor_scalar(nm[:, n:n + 1], small[:, 16:17], sink_b[:, h:h + 1], -1.0, ALU.max,
                                            ALU.mult).then_inc(s_nm, 1)
                            if h == 3:
                                dve.drain()
                                V.tensor_tensor(sk[:, 4 * t:4 * t + 4], nm[:, n - 3:n + 1], sink_b[:],
                                                ALU.add).then_inc(s_sk, 1)
                    if 1 <= n <= 48 and unit(n - 1)[0] == "A":
                        m = n - 1
                        nk = unit(m)[4]
                        dve.wait_ge(s_pt, l * 48 + m + 1)
                        if m >= 2:
                            dve.wait_ge(s_pv, l * 48 + m - 1)
                        V.tensor_copy(PT[:, m % 2, 0:nk * 128], PS[:, 2 + m % 2, 0:nk * 128]).then_inc(s_ptA, 1)
                    if n >= 3 and unit(n - 3)[2] == 3:
                        m = n - 3
                        kind, t, h, k0, nk = unit(m)
                        dve.wait_ge(s_pv, l * 48 + m + 1)
                        tot = sm[:, m - 3:m + 1]
                        if kind == "C":
                            dve.wait_ge(s_es, l * NT + t + 1)
                            V.tensor_tensor(rcp[:, m - 3:m + 1], tot, es[:, 4 * t:4 * t + 4], ALU.add)
                            dve.drain()
                            tot = rcp[:, m - 3:m + 1]
                        V.reciprocal(rcp[:, m - 3:m + 1], tot)
                        dve.drain()
                        q0 = QA if kind == "A" else QC
                        V.tensor_tensor(heads(u[:, t, q0:q0 + 256]), heads(PS[:, 4 + (m // 4) % 2, 0:256]),
                                        bc(rcp[:, m - 3:m + 1], HD), ALU.mult).then_inc(s_o, 1)

                for t in range(NT):
                    dve.wait_ge(s_zs, l * NT + t + 1)
                    if t >= 2:
                        dve.wait_ge(s_zt, l * NT + t - 1)
                    V.tensor_tensor(zr[:, t % 2, :], u[:, t, UB:UB + 256], zsg[:, t % 2, :],
                                    ALU.mult).then_inc(s_zr, 1)
                dve.wait_ge(s_zT, l * NT + NT)
                for k in range(CONVW):
                    for c in range(2):
                        z = zT[:, c, k:k + AW]
                        if k == 0:
                            V.tensor_scalar(zacc[:, c, :], z, cw[:, c, 0:1], cb[:, c:c + 1], ALU.mult,
                                            ALU.add).then_inc(s_conv, 1)
                        else:
                            dve.wait_ge(s_conv, l * (2 * CONVW) + 2 * k + c - 1)
                            V.scalar_tensor_tensor(zacc[:, c, :], z, cw[:, c, k:k + 1], zacc[:, c, :], ALU.mult,
                                                   ALU.add).then_inc(s_conv, 1)
                for t in range(NT):
                    dve.wait_ge(s_zb, l * NT + t + 1)
                    V.bn_stats(bns[:, t, :], PS[:, 2 + t, 0:256])
                    dve.drain()
                    V.bn_aggr(bnv[:, t, :], bns[:, t, :])
                dve.drain().then_inc(s_bn, 1)
                dve.wait_ge(s_bnr, l + 1)
                V.reciprocal(bnv[:, :, 1], bnv[:, :, 1])
                dve.drain()
                for t in range(NT):
                    if t >= 2:
                        dve.wait_ge(s_ob, l * NT + t - 1)
                    V.tensor_scalar(zn[:, t % 2, :], PS[:, 2 + t, 0:256], bnv[:, t, 0:1], bnv[:, t, 1:2],
                                    ALU.subtract, ALU.mult)
                    dve.drain()
                    V.tensor_tensor(zn[:, t % 2, :], zn[:, t % 2, :], lng[:], ALU.mult)
                    dve.drain()
                    V.tensor_tensor(zn[:, t % 2, :], zn[:, t % 2, :], lnb[:], ALU.add).then_inc(s_zn, 1)

                dve.wait_ge(s_g[10], l + 1)
                dve.wait_ge(s_az, l + 1)
                for n in range(NT + 1):
                    buf = (E3 if n % 2 == 0 else TT)
                    old = (TT if n % 2 == 0 else E3)
                    if n >= 1:
                        m = n - 1
                        dve.wait_ge(s_g[6], l * NT + m + 1)
                        V.tensor_tensor(old[:, 1, :].rearrange("p (a n) -> p a n", a=2),
                                        u[:, m, KD:KD + 256].unsqueeze(1).broadcast_to([128, 2, 256]),
                                        old[:, 1, :].rearrange("p (a n) -> p a n", a=2), ALU.mult).then_inc(s_g[7], 1)
                        dve.wait_ge(s_g[8], l * NT + m + 1)
                        for c in range(2):
                            V.tensor_copy(kvs[:, 2 * m + c, :, :],
                                          PS[:, 4 + c, 0:256].rearrange("p (a n) -> p a n", n=HD))
                        dve.drain().then_inc(s_g[9], 1)
                    if n < NT:
                        dve.wait_ge(s_g[3], l * NT + n + 1)
                        V.scalar_tensor_tensor(la[:, n, :], PS[:, 1, :], 0.0, buf[:, 0, :], ALU.min,
                                               ALU.subtract).then_inc(s_g[4], 1)
                for r in range(1, 8):
                    for (a, b) in GROUPS:
                        c0, c1_ = 2 * a, 2 * b
                        if r >= c1_ - c0:
                            continue
                        for d in range(2):
                            c = c0 + r if d == 0 else c1_ - 1 - r
                            prev = c - 1 if d == 0 else c + 1
                            for p in range(2):
                                k = 2 * d + p
                                V.scalar_tensor_tensor(kvs[:, c, k, :], kvs[:, prev, k, :],
                                                       dec[:, c // 2, 2 * k + c % 2:2 * k + c % 2 + 1],
                                                       kvs[:, c, k, :], ALU.mult, ALU.add)
                    dve.drain()
                dve.drain().then_inc(s_scan, 1)
                for n in range(NT + 1):
                    m = n - 1
                    if n >= 1:
                        wait_alone(dve, s_h[6], l * NT + m + 1)
                        for par in range(2):
                            V.copy_predicated(att[:, par, :], cst[:, K_GM:K_GM + 512].bitcast(I32), PS[:, 5 + par, :])
                        dve.drain().then_inc(s_h[7], 1)
                    if n < NT:
                        dve.wait_ge(s_h[1], l * NT + n + 1)
                        for k, (src, f) in enumerate(((QD, 0.125), (KD, 1.0), (QD, 0.125))):
                            e = E3[:, k, :].rearrange("p (a n) -> p a n", a=2)
                            V.scalar_tensor_tensor(e, u[:, n, src:src + 256].unsqueeze(1).broadcast_to([128, 2, 256]),
                                                   f, e, ALU.mult, ALU.mult)
                        dve.drain().then_inc(s_h[2], 1)
                    if n >= 1:
                        dve.wait_ge(s_h[8], l * NT + m + 1)
                        ob = u[:, m, QD:QD + 256].rearrange("p (a h d) -> p a h d", h=2, d=HD)
                        for par in range(2):
                            V.tensor_copy(ob[:, :, par, :], PS[:, (7, 2)[par], 0:128].rearrange("p (a d) -> p a d", d=HD))
                        dve.drain().then_inc(s_h[9], 1)
                    if n < NT:
                        dve.wait_ge(s_h[3], l * NT + n + 1)
                        V.tensor_copy(TT[:, 2, :], PS[:, 4, :]).then_inc(s_h[5], 1)
                    if n >= 1:
                        V.tensor_tensor(osq[:], u[:, m, QD:QD + 256], u[:, m, QD:QD + 256], ALU.mult)
                        dve.drain()
                        V.tensor_reduce(oss[:, m, :], heads(osq[:]), AX.X, ALU.add)
                dve.drain().then_inc(s_oss, 1)
                od = u[:, :, QD:QD + 256]
                od4 = od.rearrange("p t (h d) -> p t h d", d=HD)
                dve.wait_ge(s_or, l + 1)
                V.reciprocal(oss[:], oss[:])
                dve.drain()
                V.tensor_tensor(od4, od4, oss[:].unsqueeze(3).broadcast_to([128, NT, 4, HD]), ALU.mult)
                dve.drain()
                V.tensor_tensor(od4, od4, gng[:].unsqueeze(1).unsqueeze(1).broadcast_to([128, NT, 4, HD]), ALU.mult)
                dve.drain()
                V.tensor_tensor(od, od, u[:, :, RD:RD + 256], ALU.mult).then_inc(s_od, 1)

                dve.wait_ge(s_mz, l + 1)
                for n in range(4):
                    lo(l * SPL + (S_G + n), n, 1024)
                with dve.Fori(0, NB) as i:
                    for t in range(NT + 1):
                        if t < NT:
                            dve.wait_ge(s_tlo, l * TLL + i * 6 + (T_G + t + 1))
                            V.tensor_copy(stage[:, t % 2, :], u[:, t, bass.ds(i * 512, 256)]).then_inc(s_st, 1)
                        if t >= 1:
                            m = t - 1
                            s = slice(m * 128, (m + 1) * 128)
                            t_lo(l * TPL + i * 6 + (T_G + m), oT[1][:, :, s], tbank(m, 2), oT[0][:, :, s])
                    for c in range(2):
                        s = l * SPL + i * 16 + (S_G + 8 * c)
                        for n in range(4, 8):
                            lo(s + n, n, 256)
                        for n in range(8, 11):
                            lo(s + n, n, 1024)
                        for t in range(NT):
                            accumulated(dve, l * CPL + i * 4 + (C_G + 2 * c + 1), s + 7, t)
                            g = u[:, t, 2048:2560]
                            V.tensor_tensor(g, g, PS[:, t, :], ALU.mult)
                            dve.drain()
                            mg = ublk[:, t, 2 * c:2 * c + 2, 1, :]
                            V.tensor_tensor(mg, mg, g.rearrange("p (a n) -> p a n", a=2), ALU.add).then_inc(s_ed, 1)
                        lo(s + 11, 11, 1024)
                for t in range(NT):
                    for c in range(2):
                        k, s = slice(4 * c, 4 * c + 4), slice(t * 128, (t + 1) * 128)
                        t_lo(l * TPL + (T_M + 2 * t + c), hT[1][:, k, s], tbank(c), hT[0][:, k, s])
                for j in range(4, 12):
                    lo(l * SPL + (S_O + j), j, 1024)

                for t in range(NT):
                    normalise(l * 3 + 1, l * 18 + 6, t)
                dve.wait_ge(s_rt, l + 1)
                pr = PS[:, 2, 0:NT * NE].rearrange("p (t e) -> p t e", e=NE)
                V.tensor_reduce(lmx[:], pr, AX.X, ALU.max)
                dve.drain()
                V.tensor_tensor(lg[:], pr, bc(lmx[:], NE), ALU.subtract).then_inc(s_lm, 1)
                dve.wait_ge(s_le, l + 1)
                V.tensor_reduce(lsm[:], lg[:], AX.X, ALU.add)
                dve.drain()
                V.reciprocal(lmx[:], lsm[:])
                dve.drain()
                V.tensor_tensor(lg[:], lg[:], bc(lmx[:], NE), ALU.mult).then_inc(s_af, 1)
                dve.wait_ge(s_aft, l + 1)
                dve.wait_ge(s_scz, l + 1)
                V.tensor_copy(scores[0:NE, :], PS[0:NE, 3, :])
                V.tensor_copy(scores[32:32 + NE, 0:DEC], PS[0:NE, 4, 0:DEC])
                dve.drain()
                for r in range(CAPP // 8):
                    v, ix = top[:, 8 * r:8 * r + 8], topi[:, 8 * r:8 * r + 8]
                    V.max(v, scores[:])
                    dve.drain()
                    V.max_index(ix, v, scores[:])
                    dve.drain()
                    V.match_replace(scores[:], v, scores[:], -1.0)
                    dve.drain()
                V.tensor_copy(pick[:, 0, 0:CAPP], topi[0:NE, :])
                V.tensor_copy(pick[:, 1, 0:CAPP], top[0:NE, :])
                V.tensor_scalar(pick[:, 0, CAPP:CAP], topi[32:32 + NE, 0:CAPS], float(SEQ), None, ALU.add)
                V.tensor_copy(pick[:, 1, CAPP:CAP], top[32:32 + NE, 0:CAPS])
                dve.drain().then_inc(s_pick, 1)
                dve.wait_ge(s_pickt, l + 1)
                V.tensor_copy(idxT[:, 0:NE], PS[0:CAP, 5, 0:NE])
                V.tensor_copy(idxT[:, NE:NE + 1], PS[0:CAP, 5, 0:1])
                V.tensor_copy(gateT[:], PS[0:CAP, 5, NE:2 * NE])
                dve.drain().then_inc(s_idx, 1)
                for c in range(2):
                    k = slice(4 * c, 4 * c + 4)
                    t_lo(l * TPL + (T_E + c), xeT[1][:, k, :], tbank(c, 4, CAP), xeT[0][:, k, :])
                with dve.Fori(0, NE) as e:
                    for s in range(ES):
                        j = l * TPL + e * 4 + (T_E + 2)
                        if s in (7, 15):
                            c = s // 8
                            dve.wait_ge(s_used, l * SPL + e * ES + (S_E + s + 1 + SPLIT))
                            dve.wait_ge(s_sil, l * 32 + e * 2 + (c + 1))
                            h = sil[:, c * 512:(c + 1) * 512]
                            V.tensor_tensor(h, h, PS[0:CAP, 2 + c, :], ALU.mult).then_inc(s_hid, 1)
                        if s == 11:
                            t_lo(j, hidT[1][:, 0:4, :], tbank(0, 4, CAP), hidT[0][:, 0:4, :])
                        if s == 17:
                            t_lo(j + 1, hidT[1][:, 4:8, :], tbank(1, 4, CAP), hidT[0][:, 4:8, :])
                        if s == 19:
                            t_lo(j + 2, xeT[1][:, 0:4, :], tbank(0, 4, CAP), xeT[0][:, 0:4, :])
                        if s == 21:
                            t_lo(j + 3, xeT[1][:, 4:8, :], tbank(1, 4, CAP), xeT[0][:, 4:8, :])
                        lo(l * SPL + e * ES + (S_E + s + 4), s + 4, 1024)

                norm(l, 2, T_N2)
                for t in range(NT):
                    s = slice(t * 128, (t + 1) * 128)
                    t_lo(l * TPL + (T_P + t), oT[1][:, :, s], tbank(t, 2), oT[0][:, :, s])
                for c in range(2):
                    s = l * SPL + (S_P + 8 * c)
                    for n in range(4, 8):
                        lo(s + n, n, 256)
                    if c == 0:
                        for n in range(8, 12):
                            lo(s + n, n, 1024)
                    for t in range(NT):
                        accumulated(dve, l * CPL + (C_P + 2 * c + 1), s + 7, t)
                        V.tensor_tensor(rows[:, t, c * 512:(c + 1) * 512], gsig[:, t, :], PS[:, t, :],
                                        ALU.mult).then_inc(s_ed, 1)
            for t in range(NT):
                normalise(DEPTH * 3, DEPTH * 18, t)

        @block.tensor
        def _(pe):
            pe.drain().then_inc(s_used, SPLIT)
            pe.wait_ge(s_cst, 16)

            def transposes(j, b, blocks, free, np_=128, w=128):
                sm_, v = free
                pe.wait_ge(sm_, v)
                for n, x in enumerate(blocks):
                    m = nc.tensor.transpose(PS[:, 6 + b, n * np_:(n + 1) * np_], x, ident[0:np_, 0:np_])
                m.then_inc(s_tp, 1)

            def norm(l, n, j0, plain=False):
                for t in range(NT):
                    pe.wait_ge(s_xn, l * 18 + (n * 6 + t + 1))
                    for c in range(2):
                        j = j0 + 2 * t + c
                        if plain and j - 2 >= j0:
                            free = (s_thi, l * TPL + (j - 1) + 2)
                        else:
                            free = (s_tlo, l * TLL + lo_count(j - 2) + 2)
                        transposes(j, c, [rows[:, t, k * 128:(k + 1) * 128] for k in range(4 * c, 4 * c + 4)], free)

            def product(out, x, w, first, last):
                nc.tensor.matmul(out, x[0], w[0], start=first, stop=False)
                nc.tensor.matmul(out, x[0], w[1], start=False, stop=False)
                return nc.tensor.matmul(out, x[1], w[0], start=False, stop=last)

            def step(val, j, nk, n, x, k0, first, last, free=None, c0=0, final=True):
                pe.wait_ge(s_lo, val + 1 + RAW)
                for k in range(nk):
                    for t in range(NT):
                        if free is not None and k == 0:
                            pe.wait_ge(*free(t))
                        s = slice(t * 128, (t + 1) * 128)
                        m = product(PS[:, t, c0:c0 + n], (x[0][:, k0 + k, s], x[1][:, k0 + k, s]),
                                    (cols(whi[j % SPLIT], nk, n)[:, k, :], cols(wlo[j % SPLIT], nk, n)[:, k, :]),
                                    first and k == 0, last and k == nk - 1)
                        if last and final and k == nk - 1 and t < NT - 1:
                            m.then_inc(s_acc, 1)
                m.then_inc(s_used, 1)

            def chunk(val, n, free):
                for j in range(4):
                    step(val + j, j, 2, n, hT, 2 * j, j == 0, j == 3, free if j == 0 else None)

            def branch_chunk(val, free):
                for j in range(4):
                    step(val + j, j, 1, 256, oT, j % 2, j % 2 == 0, j % 2 == 1, free if j == 0 else None,
                         (j // 2) * 256, j == 3)

            with pe.Fori(0, DEPTH) as l:
                norm(l, 0, T_N0)
                wait_alone(pe, s_tlo, l * TLL + lo_count(T_N0 + 11) + 2)
                with pe.Fori(0, NCH // 2) as i:
                    for j in range(2):
                        chunk(l * SPL + i * 8 + 4 * j, CW, lambda t: (s_ea, l * AAPL + i * 12 + (j * 6 + t + 1)))

                for t in range(NT):
                    pe.wait_ge(s_rA, l * NT + t + 1)
                    if t >= 1:
                        pe.wait_ge(s_qA, l * NT + t)
                    for k in range(3):
                        m = nc.tensor.transpose(PS[:, 6, k * 128:(k + 1) * 128], rA[:, t % 2, k * 128:(k + 1) * 128], ident)
                    m.then_inc(s_tA, 1)
                    pe.wait_ge(s_rC, l * NT + t + 1)
                    if t >= 1:
                        pe.wait_ge(s_qC, l * NT + t)
                    for k in range(3):
                        m = nc.tensor.transpose(PS[:, 7, k * 128:(k + 1) * 128], rC[:, t % 2, k * 128:(k + 1) * 128], ident)
                    m.then_inc(s_tC, 1)
                pe.wait_ge(s_qA, l * NT + NT)
                pe.wait_ge(s_qC, l * NT + NT)
                for n in range(50):
                    if n < 48:
                        kind, t, h, k0, nk = unit(n)
                        if n >= 2:
                            pe.wait_ge(s_p, l * 48 + n - 1)
                        qk = qkA if kind == "A" else qkC
                        g = slice(64 * (h // 2), 64 * (h // 2) + 64)
                        nc.tensor.matmul(PS[:, n % 2, 0:nk * 128], qk[g, h % 2, t * 128:(t + 1) * 128],
                                         qk[g, 2, k0 * 128:(k0 + nk) * 128], start=True, stop=True).then_inc(s_sc, 1)
                    if 1 <= n <= 48:
                        m = n - 1
                        kind, t, h, k0, nk = unit(m)
                        pe.wait_ge(s_p, l * 48 + m + 1)
                        if m >= 2:
                            pe.wait_ge(*pt_done(l, m - 2))
                        for k in range(nk):
                            mm = nc.tensor.transpose(PS[:, 2 + m % 2, k * 128:(k + 1) * 128],
                                                     P[:, m % 2, k * 128:(k + 1) * 128], ident)
                        mm.then_inc(s_pt, 1)
                    if n >= 2:
                        m = n - 2
                        kind, t, h, k0, nk = unit(m)
                        pe.wait_ge(*pt_done(l, m))
                        if h == 0 and m >= 8:
                            pe.wait_ge(s_o, l * 12 + m // 4 - 1)
                        v0 = (VA if kind == "A" else VC) + 64 * (h // 2)
                        for k in range(nk):
                            mm = nc.tensor.matmul(PS[:, 4 + (m // 4) % 2, h * HD:(h + 1) * HD],
                                                  PT[:, m % 2, k * 128:(k + 1) * 128], u[:, k0 + k, v0:v0 + HD],
                                                  start=k == 0, stop=k == nk - 1)
                        mm.then_inc(s_pv, 1)

                for t in range(NT):
                    pe.wait_ge(s_zr, l * NT + t + 1)
                    if t >= 2:
                        pe.wait_ge(s_zT, l * NT + t - 1)
                    for c in range(2):
                        m = nc.tensor.transpose(PS[:, t % 2, c * 128:(c + 1) * 128], zr[:, t % 2, c * 128:(c + 1) * 128], ident)
                    m.then_inc(s_zt, 1)
                pe.wait_ge(s_conv, l * (2 * CONVW) + 2 * CONVW)
                for t in range(NT):
                    a0 = t * 128 + (PAD if t >= 4 else 0)
                    for c in range(2):
                        m = nc.tensor.transpose(PS[:, 2 + t, c * 128:(c + 1) * 128], zacc[:, c, a0:a0 + 128], ident)
                    m.then_inc(s_zb, 1)

                pe.wait_ge(s_az, l + 1)
                cum = [cst[:, K_CUM + n * 128:K_CUM + (n + 1) * 128] for n in range(6)]
                for n in range(NT + 1):
                    m = n - 1
                    if n < NT:
                        pe.wait_ge(s_ob, l * NT + NT)
                        if n >= 1:
                            pe.wait_ge(s_g[1], l * NT + n)
                        nc.tensor.transpose(PS[0:32, 0, 0:128], u[:, n, ZL:ZL + 32], ident).then_inc(s_g[0], 1)
                    if n >= 1:
                        pe.wait_ge(s_g[4], l * NT + n)
                        for d in range(2):
                            nc.tensor.matmul(PS[:, 2, d * 256:(d + 1) * 256], cum[3 * d + 2],
                                             la[:, m, d * 256:(d + 1) * 256], start=True, stop=True)
                        for k in range(4):
                            mm = nc.tensor.matmul(PS[:, 3, 2 * k:2 * k + 2], la[:, m, k * 128:(k + 1) * 128],
                                                  cst[:, K_IND:K_IND + 2], start=True, stop=True)
                        mm.then_inc(s_g[5], 1)
                    if n < NT:
                        pe.wait_ge(s_g[1], l * NT + n + 1)
                        nc.tensor.matmul(PS[:, 1, :], zlT[0:33, :], w2b[0:33, :], start=True, stop=True).then_inc(s_g[2], 1)
                    if n >= 1:
                        wait_alone(pe, s_g[7], l * NT + n)
                        if n >= 2:
                            pe.wait_ge(s_g[9], l * NT + n - 1)
                        old = (TT if n % 2 == 0 else E3)
                        for c in range(2):
                            cr = slice(64 * c, 64 * c + 64)
                            for d in range(2):
                                for h in range(4):
                                    mm = nc.tensor.matmul(
                                        PS[64 * (h % 2):64 * (h % 2) + 64, 4 + c, (2 * d + h // 2) * HD:(2 * d + h // 2 + 1) * HD],
                                        old[cr, 1, d * 256 + h * HD:d * 256 + (h + 1) * HD],
                                        u[cr, m, VD + h * HD:VD + (h + 1) * HD], start=True, stop=True)
                        mm.then_inc(s_g[8], 1)
                pe.wait_ge(s_scan, l + 1)
                for n in range(NT + 1):
                    m = n - 1
                    if n < NT:
                        if n >= 1:
                            pe.wait_ge(s_h[1], l * NT + n)
                        for b, k in ((0, 1), (1, 0)):
                            for d in range(2):
                                mm = nc.tensor.matmul(PS[:, b, d * 256:(d + 1) * 256], cum[3 * d + k],
                                                      la[:, n, d * 256:(d + 1) * 256], start=True, stop=True)
                        mm.then_inc(s_h[0], 1)
                    if n >= 1:
                        pe.wait_ge(s_h[4], l * NT + n)
                        pe.wait_ge(s_h[5], l * NT + n)
                        if n >= 2:
                            pe.wait_ge(s_h[7], l * NT + n - 1)
                        for par in range(2):
                            g = slice(64 * par, 64 * par + 64)
                            for k in range(4):
                                mm = nc.tensor.matmul(PS[:, 5 + par, k * 128:(k + 1) * 128],
                                                      TT[g, 1, k * 128:(k + 1) * 128], TT[g, 0, k * 128:(k + 1) * 128],
                                                      start=True, stop=True)
                        mm.then_inc(s_h[6], 1)
                        pe.wait_ge(s_h[7], l * NT + n)
                        if n >= 2:
                            pe.wait_ge(s_h[9], l * NT + n - 1)
                        ga, gb = TILE_GROUP[m]
                        for par in range(2):
                            g = slice(64 * par, 64 * par + 64)
                            for p in range(2):
                                h = 2 * p + par
                                ob = PS[:, (7, 2)[par], p * HD:(p + 1) * HD]
                                for d in range(2):
                                    k = 2 * d + p
                                    mm = nc.tensor.matmul(ob, att[:, par, k * 128:(k + 1) * 128],
                                                          u[:, m, VD + h * HD:VD + (h + 1) * HD],
                                                          start=d == 0, stop=False, skip_group_check=True)
                                for d in range(2):
                                    k = 2 * d + p
                                    for c in range(2):
                                        ch = 2 * m + c
                                        if ch == (2 * ga if d == 0 else 2 * gb - 1):
                                            continue
                                        mm = nc.tensor.matmul(
                                            PS[64 * c:64 * c + 64, (7, 2)[par], p * HD:(p + 1) * HD],
                                            TT[g, 2, k * 128 + 64 * c:k * 128 + 64 * c + 64],
                                            kvs[g, ch - 1 if d == 0 else ch + 1, k, :],
                                            start=False, stop=True, skip_group_check=True)
                        mm.then_inc(s_h[8], 1)
                    if n < NT:
                        pe.wait_ge(s_h[2], l * NT + n + 1)
                        if n >= 1:
                            pe.wait_ge(s_h[9], l * NT + n)
                        for b in range(3):
                            for k in range(4):
                                mm = nc.tensor.transpose(PS[:, 2 + b, k * 128:(k + 1) * 128],
                                                         E3[:, b, k * 128:(k + 1) * 128], ident)
                        mm.then_inc(s_h[3], 1)

                wait_alone(pe, s_mz, l + 1)
                with pe.Fori(0, NB) as i:
                    for c in range(2):
                        s = l * SPL + i * 16 + (S_G + 8 * c)
                        if c == 0:
                            for t in range(NT):
                                pe.wait_ge(s_st, l * 24 + i * 6 + t + 1)
                                transposes(None, t % 2, [stage[:, t % 2, k * 128:(k + 1) * 128] for k in range(2)],
                                           (s_tlo, l * TLL + i * 6 + (T_G + t + 1)))
                        chunk(s, 512, lambda t: (s_ed, l * ADPL + i * 12 + (c * 6 + t + 1)))
                        if c == 0:
                            pe.wait_ge(s_tlo, l * TLL + i * 6 + (T_G + 6 + 2))
                        branch_chunk(s + 4, lambda t: (s_ea, l * AAPL + i * 12 + (AA_G + c * 6 + t + 1 + 6)))
                pe.wait_ge(s_ed, l * ADPL + AD_P + 6)
                for t in range(NT):
                    for c in range(2):
                        transposes(None, c, [ublk[:, t, k // 2, 1, (k % 2) * 128:(k % 2) * 128 + 128]
                                             for k in range(4 * c, 4 * c + 4)],
                                   (s_tlo, l * TLL + (T_M + 2 * t + c + 1)))
                pe.wait_ge(s_tlo, l * TLL + (T_M + 12 + 2))
                for c in range(2):
                    of = (lambda t: (s_ed, l * ADPL + (AD_P - 6 + t + 1 + 6))) if c == 0 else \
                        (lambda t: (s_ea, l * AAPL + (AA_O + t + 1 + 6)))
                    chunk(l * SPL + (S_O + 4 * c), 512, of)

                norm(l, 1, T_N1, plain=True)
                pe.wait_ge(s_thi, l * TPL + (T_N1 + 12 + 2))
                for t in range(NT):
                    for k in range(KT):
                        mm = nc.tensor.matmul(PS[:, 2, t * NE:(t + 1) * NE], hTf[:, k, t * 128:(t + 1) * 128],
                                              wr[:, k, :], start=k == 0, stop=k == KT - 1)
                mm.then_inc(s_rt, 1)
                pe.wait_ge(s_af, l + 1)
                for t in range(NT):
                    b, o = (3, t) if t < 4 else (4, t - 4)
                    mm = nc.tensor.transpose(PS[0:NE, b, o * 128:(o + 1) * 128], lg[:, t, :], ident)
                mm.then_inc(s_aft, 1)
                wait_alone(pe, s_pick, l + 1)
                for n in range(2):
                    mm = nc.tensor.transpose(PS[0:CAP, 5, n * NE:(n + 1) * NE], pick[:, n, :], ident[0:NE, 0:NE])
                mm.then_inc(s_pickt, 1)
                pe.wait_ge(s_ga, l * (17 * 16) + 16)
                pe.wait_ge(s_idx, l + 1)
                for c in range(2):
                    transposes(None, c, [xe[:, k * 128:(k + 1) * 128] for k in range(4 * c, 4 * c + 4)],
                               (s_thi, l * TPL + (T_E + c - 1 + 2)), CAP)

                def expert_steps(e, s0, n, bank, x, k0, first, last):
                    for j in range(n):
                        pe.wait_ge(s_lo, l * SPL + e * ES + (S_E + s0 + j + 1 + RAW))
                        w = [cols(x_[(s0 + j) % SPLIT], 2, 512) for x_ in (whi, wlo)]
                        for k in range(2):
                            kk = k0 + 2 * j + k
                            m = product(PS[0:CAP, bank, :], (x[0][:, kk, :], x[1][:, kk, :]), (w[0][:, k, :], w[1][:, k, :]),
                                        first and j == 0 and k == 0, last and j == n - 1 and k == 1)
                        m.then_inc(s_used, 1)

                with pe.Fori(0, NE) as e:
                    tl = l * TLL + e * 4 + (T_E - 12 + 2 + 2)
                    pe.wait_ge(s_tlo, tl)
                    for c in range(2):
                        expert_steps(e, 8 * c, 4, c, xeT, 0, True, True)
                        if c == 1:
                            pe.wait_ge(s_hid, l * 32 + e * 2 + 1)
                            transposes(None, 0, [sil[:, k * 128:(k + 1) * 128] for k in range(4)], (s_tlo, tl), CAP)
                        expert_steps(e, 8 * c + 4, 4, 2 + c, xeT, 0, True, True)
                    pe.wait_ge(s_tlo, tl + 1)
                    expert_steps(e, 16, 2, 4, hidT, 0, True, False)
                    pe.wait_ge(s_hid, l * 32 + e * 2 + 2)
                    transposes(None, 1, [sil[:, k * 128:(k + 1) * 128] for k in range(4, 8)], (s_tlo, tl), CAP)
                    expert_steps(e, 18, 2, 5, hidT, 0, True, False)
                    pe.wait_ge(s_ga, l * (17 * 16) + e * 16 + 32)
                    transposes(None, 0, [xe[:, k * 128:(k + 1) * 128] for k in range(4)], (s_tlo, tl + 1), CAP)
                    pe.wait_ge(s_tlo, tl + 2)
                    expert_steps(e, 20, 2, 4, hidT, 4, False, True)
                    transposes(None, 1, [xe[:, k * 128:(k + 1) * 128] for k in range(4, 8)], (s_tlo, tl + 2), CAP)
                    expert_steps(e, 22, 2, 5, hidT, 4, False, True)

                norm(l, 2, T_N2)
                pe.wait_ge(s_pin, l * 32 + 32)
                for t in range(NT):
                    transposes(None, t % 2, [prow[:, t, k * 128:(k + 1) * 128] for k in range(2)],
                               (s_tlo, l * TLL + lo_count(T_P + t - 2) + 2))
                pe.wait_ge(s_tlo, l * TLL + lo_count(T_P + 5) + 2)
                for c in range(2):
                    s = l * SPL + (S_P + 8 * c)
                    chunk(s, 512, lambda t: (s_ed, l * ADPL + (AD_P + 6 * (c - 1) + t + 1 + 6)))
                    branch_chunk(s + 4, lambda t: (s_ea, l * AAPL + (AA_P + c * 6 + t + 1 + 6)))


def unit(n):
    kind, t, h = ("A", "C")[n // 24], n % 24 // 4, n % 4
    a, b = TILE_GROUP[t]
    if kind == "C":
        a, b = max(a, t - 1), min(b, t + 2)
    return kind, t, h, a, b - a


_NAMES = ["x_prompt", "x_sample", "p_prompt", "p_sample", "norm_mix", "w_in", "qk_norm", "sink_logit", "conv_dw",
          "conv_dw_b", "conv_ln_g", "conv_ln_b", "gla_w2", "gla_b2", "gla_norm", "w_branch", "w_out", "norm_ffn",
          "w_router", "w_gate_e", "w_up_e", "w_down_e", "norm_ple", "w_ple_gate", "w_ple_proj", "norm_final"]


def kernel(**inputs):
    import concourse.bacc as bacc
    from concourse.bass_utils import run_bass_kernel_spmd

    nc = bacc.Bacc("TRN2", target_bir_lowering=False, num_devices=1)
    arrays, args = {}, []
    for name in _NAMES:
        a = np.asarray(inputs[name])
        if name == "conv_dw":
            a = a.transpose(0, 2, 1)
        arrays[f"in_{name}"] = np.ascontiguousarray(a)
    arrays["in_consts"] = shape_constants()
    for name, a in arrays.items():
        args.append(nc.dram_tensor(name, a.shape, mybir.dt.from_np(a.dtype), kind="ExternalInput").ap())
    for n, s in (("out_prompt", SEQ), ("out_sample", DEC)):
        args.append(nc.dram_tensor(n, [1, s, D], F32, kind="ExternalOutput").ap())
    build(nc, *args)
    r = run_bass_kernel_spmd(nc, [arrays], core_ids=[0])
    return r.results[0]["out_prompt"], r.results[0]["out_sample"]
```

```python
from contextlib import ExitStack

import concourse.bass as bass
from concourse import mybir
import numpy as np

F32 = mybir.dt.float32
F32R = mybir.dt.float32r
I32 = mybir.dt.int32
U32 = mybir.dt.uint32
ALU = mybir.AluOpType
ACT = mybir.ActivationFunctionType
AX = mybir.AxisListType

DEPTH, D, SEQ, DEC = 2, 1024, 512, 256
TOK = SEQ + DEC
NT = TOK // 128
GROUPS = [(0, SEQ // 128), (SEQ // 128, NT)]
TILE_GROUP = [GROUPS[0]] * (SEQ // 128) + [GROUPS[1]] * (DEC // 128)
KT = D // 128
HD = 64
EPS = 1e-6
UC = 2592
IN_COLS = UC + 4 * D
NCH = 6
CW = UC // NCH
NB = 4
NE, CAPP, CAPS = 16, 2 * SEQ // 16, 2 * DEC // 16
CAP = CAPP + CAPS
FF = 1024
PLE = 256
CONVW = 31
PAD = CONVW // 2
ZW = PAD + SEQ + PAD + DEC + PAD
AW = ZW - 2 * PAD

QA, KA, VA, UB, UG, QC, KC, VC, QD, KD, VD, RD, ZL = (
    0, 256, 384, 512, 768, 1024, 1280, 1408, 1536, 1792, 2048, 2304, 2560)

ES = 24
S_W, S_G, S_O, S_E = 0, 4 * NCH, 4 * NCH + 8, 4 * NCH + 16
S_P = S_E + ES * NE
SPL = S_P + 16
RAW, SPLIT = 8, 4
NF, FRAW, FSPLIT = NB * D // 128, 3, 2
F_ROPE, F_Z, F_ATT, F_CONV, F_GLA = 0, 6, 8, 24, 26

T_N0, T_G, T_N1 = 0, 12, 24
T_E = T_N1 + 12
T_N2 = T_E + 4 * NE + 2
T_P = T_N2 + 12
TPL = T_P + 6
C_O, C_P, CPL = 6, 8, 12
AA_O, AA_P, AAPL = 36, 48, 60
ADPL = 12

K_ID = 0
K_WM = 128
K_CUM = K_WM + 384
K_IND = K_CUM + 6 * 128
K_GM = K_IND + 2
K_RA = K_GM + 512
K_RC = K_RA + 2 * 4 * HD
K_N = K_RC + 2 * 4 * HD


def shape_constants():
    c = np.zeros((128, K_N), np.float32)
    i = np.arange(128)
    c[:, K_ID:K_ID + 128] = np.eye(128)
    c[:, K_WM:K_WM + 128] = np.where(i[None, :] >= i[:, None], 0, -1e30)
    c[:, K_WM + 256:K_WM + 384] = np.where(i[None, :] <= i[:, None], 0, -1e30)
    same = (i[:, None] // 64) == (i[None, :] // 64)
    j, q = i[:, None], i[None, :]
    jl = j % 64
    mats = [
        same & (j <= q), (same & (j <= q)) * 1 - (same & (jl <= 31)) * 1, same & (j > q),
        same & (j >= q), (same & (j >= q)) * 1 - (same & (jl >= 32)) * 1, same & (j < q),
    ]
    for n, m in enumerate(mats):
        c[:, K_CUM + n * 128:K_CUM + (n + 1) * 128] = np.asarray(m, np.float32) / 16
    c[:, K_IND] = (i < 64) / 16
    c[:, K_IND + 1] = (i >= 64) / 16
    for d in range(2):
        m = same & ((j <= q) if d == 0 else (j >= q))
        for p in range(2):
            c[:, K_GM + (2 * d + p) * 128:K_GM + (2 * d + p + 1) * 128] = m

    def tables(pos, dim):
        inv = np.float32(10000.0) ** (-np.arange(0, dim, 2, dtype=np.float32) / np.float32(dim))
        a = pos.astype(np.float32)[:, None] * inv[None, :]
        return np.cos(a), np.sin(a)

    s = np.arange(SEQ)
    rc, rs = tables(s // 64, 32)
    cc, cs = tables(s % 64, 32)
    tc, ts = tables(s, 64)
    ca = np.concatenate([rc, rc, cc, cc], 1)
    sa = np.concatenate([-rs, rs, -cs, cs], 1)
    cp = np.concatenate([tc, tc], 1)
    sp = np.concatenate([-ts, ts], 1)
    for n, m in enumerate([ca, sa, cp, sp]):
        c[:, K_RA + n * 256:K_RA + (n + 1) * 256] = m.reshape(4, 128, HD).transpose(1, 0, 2).reshape(128, 256)
    return c


def build(nc, x_p, x_s, p_p, p_s, norm_mix, w_in, qk_norm, sink, conv_w, conv_b, ln_g, ln_b, gla_w2, gla_b2,
          gla_norm, w_branch, w_out, norm_ffn, w_router, w_gate, w_up, w_down, norm_ple, w_pg, w_pp,
          norm_final, consts, y_p, y_s):
    ctx = ExitStack()
    with ctx:
        def sb(name, shape, dt=F32):
            return ctx.enter_context(nc.sbuf_tensor(name, shape, dt))

        def sem(name):
            return ctx.enter_context(nc.semaphore(name))

        x_d = nc.dram_tensor("x_res", [TOK, D], F32).ap()
        g_d = nc.dram_tensor("gate_logits", [NF, 128, TOK], F32).ap()
        h2_d = nc.dram_tensor("h2_rows", [TOK, D], F32).ap()

        cst = sb("cst", [128, K_N])
        ident = cst[:, K_ID:K_ID + 128]
        gqk = sb("gqk", [128, 6, HD])
        sink_b = sb("sink_b", [128, 4])
        cw = sb("cw", [128, 2, CONVW])
        cb = sb("cb", [128, 2])
        lng = sb("lng", [128, 256])
        lnb = sb("lnb", [128, 256])
        gng = sb("gng", [128, HD])
        w2b = sb("w2b", [33, 512])
        wr = sb("wr", [128, KT, NE])
        ms = sb("ms", [128, NT])
        rs = sb("rs", [128, NT])
        small = sb("small", [128, 64])
        nm = sb("nm", [128, 48])
        sm = sb("sm", [128, 48])
        sk = sb("sk", [128, 24])
        es = sb("es", [128, 24])
        rcp = sb("rcp", [128, 48])
        rqk = sb("rqk", [128, NT, 6])
        bns = sb("bns", [128, NT, 6])
        bnv = sb("bnv", [128, NT, 2])
        oss = sb("oss", [128, NT, 4])
        eps1, eps64 = sb("eps1", [128, 1]), sb("eps64", [128, 1])
        base = (nc.sbuf_base + 31) // 32 * 32
        R0 = base
        H0 = R0 + RAW * 4096
        U0 = H0 + 2 * KT * TOK * 4
        M0 = U0 + (NT * UC * 4 + 31) // 32 * 32
        MIX = 42752
        END = M0 + MIX + TOK * 4
        fence = sb("fence", [128, (END - base) // 4])
        assert nc.sbuf_base <= nc.sbuf_usable_end

        def at(name, shape, off, dt=F32):
            return nc.alloc_sbuf_tensor_at(name, shape, dt, offset=off)

        raw = [at(f"raw{i}", [128, 1024], R0 + i * 4096) for i in range(RAW)]
        hT = [at(f"hT{n}", [128, KT, TOK], H0 + n * KT * TOK * 4, F32R) for n in range(2)]
        hTf = at("hTf", [128, KT, TOK], H0)
        merged = at("merged", [128, KT, TOK], H0 + KT * TOK * 4)
        u = at("u", [128, NT, UC], U0)
        rows = at("rows", [128, NT, D], U0)
        gain = at("gain", [128, D], U0 + NT * D * 4)
        gsig = at("gsig", [128, NT, 512], U0 + (NT * D + D) * 4)
        prow = at("prow", [128, NT, PLE], U0 + (NT * D + D + NT * 512) * 4)
        whi = [at(f"whi{n}", [128, 1024], M0 + n * 4096, F32R) for n in range(SPLIT)]
        wlo = [at(f"wlo{n}", [128, 1024], M0 + (SPLIT + n) * 4096, F32R) for n in range(SPLIT)]
        oT = [at(f"oT{n}", [128, 2, TOK], M0 + 4 * 8192 + n * 2 * TOK * 4, F32R) for n in range(2)]
        ur = at("ur", [128, NT, UC], U0, F32R)
        ublk = u[:, :, 0:2048].rearrange("p t (b h n) -> p t b h n", h=2, n=256)
        urblk = ur[:, :, 0:2048].rearrange("p t (b h n) -> p t b h n", h=2, n=256)
        gates0 = at("gates0", [128, NB, NT, 128], M0 + 4 * 8192)
        gates = (gates0, u[:, :, 2048:2560].rearrange("p t (i n) -> p i t n", n=128))
        gates_all = (gates0[:].rearrange("p i t n -> p (i t n)"), u[:, :, 2048:2560])
        fhi = [at(f"fhi{n}", [128, KT, 128], R0 + (4 + 2 * n) * 4096, F32R) for n in range(FSPLIT)]
        flo = [at(f"flo{n}", [128, KT, 128], R0 + (5 + 2 * n) * 4096, F32R) for n in range(FSPLIT)]
        fout = [raw[3][:, 0:TOK], at("fout1", [128, TOK], M0 + MIX)[:]]
        e_at = [U0 + (NT * D + D) * 4]

        def moe(name, shape, dt=F32):
            n = 4
            for v in shape[1:]:
                n *= v
            off = e_at[0]
            e_at[0] = (off + n + 31) // 32 * 32
            assert e_at[0] <= M0
            return at(name, shape, off, dt)

        xe = moe("xe", [CAP, D])
        xeT = [moe(f"xeT{n}", [128, KT, CAP], F32R) for n in range(2)]
        sil = moe("sil", [CAP, FF])
        hidT = [moe(f"hidT{n}", [128, KT, CAP], F32R) for n in range(2)]
        ye = moe("ye", [CAP, D])
        lg = moe("lg", [128, NT, NE])
        lmx = moe("lmx", [128, NT])
        lsm = moe("lsm", [128, NT])
        scores = moe("scores", [48, SEQ])
        top = moe("top", [48, CAPP])
        topi = moe("topi", [48, CAPP], U32)
        pick = moe("pick", [NE, 2, CAP])
        idxT = moe("idxT", [CAP, NE + 1], U32)
        gateT = moe("gateT", [CAP, NE])
        idx_g = moe("idx_g", [CAP, 1], U32)
        idx_s = moe("idx_s", [CAP, 1], U32)
        m_at = [M0]

        def mix(name, shape):
            n = 4
            for v in shape[1:]:
                n *= v
            off = m_at[0]
            m_at[0] = (off + n + 31) // 32 * 32
            assert m_at[0] <= M0 + MIX, name
            return at(name, shape, off)

        qkA = mix("qkA", [128, 3, TOK])
        qkC = mix("qkC", [128, 3, TOK])
        s1 = mix("s1", [128, 384])
        s2 = mix("s2", [128, 384])
        at_z = m_at[0]
        zsg = mix("zsg", [128, 2, 256])
        zn = mix("zn", [128, 2, 256])
        zr = mix("zr", [128, 2, 256])
        m_at[0] = at_z
        P = mix("P", [128, 2, 512])
        PT = mix("PT", [128, 2, 512])
        at_r = m_at[0]
        zT = mix("zT", [128, 2, ZW])
        zacc = mix("zacc", [128, 2, AW])
        m_at[0] = at_r
        rA = mix("rA", [128, 2, 384])
        rC = mix("rC", [128, 2, 384])
        s3 = mix("s3", [128, 384])
        c1 = mix("c1", [128, 384])
        c2 = mix("c2", [128, 384])
        sC = s1, s2
        m_at[0] = M0
        la = mix("la", [128, NT, 512])
        kvs = mix("kvs", [128, 2 * NT, 4, HD])
        E3 = mix("E3", [128, 3, 512])
        TT = mix("TT", [128, 3, 512])
        att = mix("att", [128, 2, 512])
        dec = mix("dec", [128, NT, 8])
        zlT = mix("zlT", [33, 128])
        osq = mix("osq", [128, 256])

        PS = ctx.enter_context(nc.psum_tensor("PS", [128, 8, 512], F32))

        s_cst = sem("s_cst")
        s_init = sem("s_init")
        s_raw = [sem(f"s_raw{i}") for i in range(RAW)]
        s_hi = sem("s_hi")
        s_lo = sem("s_lo")
        s_used = sem("s_used")
        s_xin = [sem(f"s_xin{i}") for i in range(NT)]
        s_gain = sem("s_gain")
        s_small = sem("s_small")
        s_smallx = sem("s_smallx")
        s_sq = sem("s_sq")
        s_eps = sem("s_eps")
        s_ssq, s_rqk = sem("s_ssq"), sem("s_rqk")
        s_bn, s_bnr = sem("s_bn"), sem("s_bnr")
        s_oss, s_or = sem("s_oss"), sem("s_or")
        s_xn = sem("s_xn")
        s_tp = sem("s_tp")
        s_thi = sem("s_thi")
        s_tlo = sem("s_tlo")
        s_acc = sem("s_acc")
        s_ea = sem("s_ea")
        s_ed = sem("s_ed")
        s_xadd = sem("s_xadd")
        s_rA, s_rC = sem("s_rA"), sem("s_rC")
        s_tA, s_tC = sem("s_tA"), sem("s_tC")
        s_qA, s_qC = sem("s_qA"), sem("s_qC")
        s_sc = sem("s_sc")
        s_nm = sem("s_nm")
        s_p = sem("s_p")
        s_pt = sem("s_pt")
        s_ptA, s_ptC = sem("s_ptA"), sem("s_ptC")
        s_pv = sem("s_pv")
        s_sk = sem("s_sk")
        s_es = sem("s_es")
        s_o = sem("s_o")
        s_zpad = sem("s_zpad")
        s_zs = sem("s_zs")
        s_zr = sem("s_zr")
        s_zt = sem("s_zt")
        s_zT = sem("s_zT")
        s_conv = sem("s_conv")
        s_zb = sem("s_zb")
        s_zn = sem("s_zn")
        s_ob = sem("s_ob")
        s_az = sem("s_az")
        s_g = [sem(f"s_g{i}") for i in range(11)]
        s_scan = sem("s_scan")
        s_h = [sem(f"s_h{i}") for i in range(11)]
        s_od = sem("s_od")
        s_fraw = [sem(f"s_fraw{i}") for i in range(FRAW)]
        s_fhi = sem("s_fhi")
        s_flo = sem("s_flo")
        s_fused = sem("s_fused")
        s_fev = sem("s_fev")
        s_fout = [sem(f"s_fout{i}") for i in range(2)]
        s_gl = [sem(f"s_gl{i}") for i in range(2)]
        s_sg = sem("s_sg")
        s_br = [sem(f"s_br{i}") for i in range(NB - 1)]
        s_gm = [sem(f"s_gm{i}") for i in range(NB)]
        s_mg = sem("s_mg")
        s_mh, s_ml = sem("s_mh"), sem("s_ml")
        s_h2 = [sem(f"s_h2{i}") for i in range(2)]
        s_rt = sem("s_rt")
        s_lm = sem("s_lm")
        s_le = sem("s_le")
        s_af = sem("s_af")
        s_aft = sem("s_aft")
        s_scz = sem("s_scz")
        s_pick = sem("s_pick")
        s_pickt = sem("s_pickt")
        s_idx = sem("s_idx")
        s_ga = sem("s_ga")
        s_sil = sem("s_sil")
        s_hid = sem("s_hid")
        s_y = sem("s_y")
        s_sca = sem("s_sca")
        s_pin = sem("s_pin")
        s_yo = sem("s_yo")

        w_in_f = w_in.rearrange("l k n -> (l k) n")
        w_br_f = w_branch.rearrange("l b k n -> (l b k) n")
        w_out_f = w_out.rearrange("l k n -> (l k) n")
        wg_f = w_gate.rearrange("l e k n -> (l e k) n")
        wu_f = w_up.rearrange("l e k n -> (l e k) n")
        wd_f = w_down.rearrange("l e k n -> (l e k) n")
        wpg_f = w_pg.rearrange("l k n -> (l k) n")
        wpp_f = w_pp.rearrange("l k n -> (l k) n")
        block = ctx.enter_context(nc.Block())

        def cols(tile, nk, n):
            return tile[:, 0:nk * n].rearrange("p (k n) -> p k n", n=n)

        def lo_count(j):
            return j + 1 if j < T_N1 else j + 1 - 12
        TLL = TPL - 12

        def gate_bank(f):
            return 4 if f < F_Z else 6

        def pt_done(l, m):
            return (s_ptA, l * 24 + m + 1) if m < 24 else (s_ptC, l * 24 + m - 24 + 1)

        def wait_alone(eng, sem_, value):
            value = eng.to_reg(value)
            eng.wait_ge(s_cst, 16)
            eng.wait_ge(sem_, value)

        def accumulated(eng, chunks, step_, t):
            if t < NT - 1:
                eng.wait_ge(s_acc, chunks * (NT - 1) + (t + 1))
            else:
                eng.wait_ge(s_used, step_ + (1 + SPLIT))

        @block.sync
        def _(sp):
            sp.dma_start(cst[:], consts).then_inc(s_cst, 16)
            sp.dma_start(x_d[0:SEQ, :], x_p.rearrange("a s d -> (a s) d")).then_inc(s_init, 16)
            sp.dma_start(x_d[SEQ:TOK, :], x_s.rearrange("a s d -> (a s) d")).then_inc(s_init, 16)

            def load(step, j, src, r0, nk, c0, n):
                sp.wait_ge(s_lo, step + 1)
                sp.dma_start(cols(raw[j % RAW], nk, n),
                             src[bass.ds(r0, nk * 128), :][:, bass.ds(c0, n)].rearrange("(k p) n -> p k n", p=128)
                             ).then_inc(s_raw[j % RAW], 16)

            with sp.Fori(0, DEPTH) as l:
                with sp.Fori(0, NCH // 2) as i:
                    for j in range(8):
                        load(l * SPL + i * 8 + j, j, w_in_f, l * D + (j % 4) * 256, 2,
                             i * (2 * CW) + (j // 4) * CW, CW)
                def load_gate(f):
                    if f < FRAW:
                        sp.wait_ge(s_lo, l * SPL + (S_G + RAW))
                    else:
                        sp.wait_ge(s_flo, l * NF + (f - FRAW + 1))
                    sp.dma_start(raw[f % FRAW][:].rearrange("p (k n) -> p k n", n=128),
                                 w_in_f[bass.ds(l * D, D), UC + f % NB * D + f // NB * 128:UC + f % NB * D + f // NB * 128 + 128]
                                 .rearrange("(k p) n -> p k n", p=128)).then_inc(s_fraw[f % FRAW], 16)

                for f in range(FRAW):
                    load_gate(f)
                for f in range(NF):
                    if f + FRAW < NF:
                        load_gate(f + FRAW)
                    sp.wait_ge(s_fev, l * NF + f + 2)
                    sp.dma_start(g_d[f], fout[f % 2]).then_inc(s_fout[f % 2], 16)
                wait_alone(sp, s_flo, l * NF + NF)
                wait_alone(sp, s_fused, l * NF + NF + FSPLIT)
                for n in range(2):
                    wait_alone(sp, s_fout[n], l * (8 * NF) + 8 * NF)
                for g in range(8):
                    sp.wait_ge(s_lo, l * SPL + (S_G + g + 1))
                    sp.dma_start(raw[g][:].rearrange("p (k n) -> p k n", n=128),
                                 w_br_f[bass.ds(l * (NB * 256), NB * 256), g * 128:(g + 1) * 128]
                                 .rearrange("(k p) n -> p k n", p=128)).then_inc(s_raw[g], 16)
                for g in range(10):
                    if g < 8:
                        if g < 2:
                            sp.wait_ge(s_od, l + 1)
                        else:
                            sp.wait_ge(s_mg, l * 8 + (g - 1))
                        for i in range(NB):
                            sp.dma_start(gates[g % 2][:, i], g_d[g * NB + i].rearrange("p (t n) -> p t n", n=128)
                                         ).then_inc(s_gl[g % 2], 16)
                    if g >= 2:
                        j = g - 2
                        load(l * SPL + (S_O + j), j, w_out_f, l * D + (j % 4) * 256, 2, (j // 4) * 512, 512)
                with sp.Fori(0, NE) as e:
                    for c in range(2):
                        for n, src in enumerate((wg_f, wu_f)):
                            for j in range(4):
                                s = 8 * c + 4 * n + j
                                load(l * SPL + e * ES + (S_E + s), s, src, l * (NE * D) + e * D + j * 256, 2,
                                     c * 512, 512)
                    for j in range(8):
                        load(l * SPL + e * ES + (S_E + 16 + j), j, wd_f,
                             l * (NE * FF) + e * FF + (j // 4) * 512 + (j % 2) * 256, 2, (j // 2 % 2) * 512, 512)
                for c in range(2):
                    for j in range(4):
                        load(l * SPL + (S_P + 8 * c + j), j, wpg_f, l * D + j * 256, 2, c * 512, 512)
                    for j in range(4):
                        load(l * SPL + (S_P + 8 * c + 4 + j), 4 + j, wpp_f, l * PLE + (j % 2) * 128, 1,
                             c * 512 + (j // 2) * 256, 256)
            for t in range(NT):
                sp.wait_ge(s_xn, DEPTH * 18 + t + 1)
                dst = y_p[0, t * 128:(t + 1) * 128, :] if t < 4 else y_s[0, (t - 4) * 128:(t - 3) * 128, :]
                sp.dma_start(dst, rows[:, t, :]).then_inc(s_yo, 16)
            sp.wait_ge(s_yo, 16 * NT)

        @block.gpsimd
        def _(pool):
            def wait(s, value):
                if isinstance(value, int):
                    pool.wait_ge(s, value)
                else:
                    wait_alone(pool, s, value)

            wait(s_init, 32)
            wait(s_cst, 16)

            def load_x(row):
                for t in range(NT):
                    pool.dma_start(rows[:, t, :], x_d[t * 128:(t + 1) * 128, :]).then_inc(s_xin[t], 16)
                pool.dma_start(gain[:], row.broadcast_to([128, D])).then_inc(s_gain, 16)

            nc.gpsimd.memset(w2b[:], 0.0)
            nc.gpsimd.memset(eps1[:], EPS)
            nc.gpsimd.memset(eps64[:], HD * EPS)
            pool.drain().then_inc(s_eps, 1)
            wait(s_cst, 16)
            with pool.Fori(0, DEPTH) as l:
                load_x(norm_mix[bass.ds(l, 1), :])
                for k in range(2):
                    src = qk_norm.rearrange("l k d -> l (k d)")[bass.ds(l, 1), k * HD:(k + 1) * HD]
                    for h in ((0, 1, 2, 3) if k == 0 else (4, 5)):
                        pool.dma_start(gqk[:, h, :], src.broadcast_to([128, HD])).then_inc(s_small, 16)
                pool.dma_start(sink_b[:], sink[bass.ds(l, 1), :].broadcast_to([128, 4])).then_inc(s_small, 16)
                pool.dma_start(cw[:], conv_w.rearrange("l c w -> (l c) w")[bass.ds(l * 256, 256), :]
                               .rearrange("(h p) w -> p h w", p=128)).then_inc(s_small, 16)
                pool.dma_start(cb[:], conv_b.rearrange("l (c o) -> (l c) o", o=1)[bass.ds(l * 256, 256), :]
                               .rearrange("(h p) o -> p (h o)", p=128), allow_slow_non_contiguous=True).then_inc(s_small, 16)
                pool.dma_start(lng[:], ln_g[bass.ds(l, 1), :].broadcast_to([128, 256])).then_inc(s_small, 16)
                pool.dma_start(lnb[:], ln_b[bass.ds(l, 1), :].broadcast_to([128, 256])).then_inc(s_small, 16)
                pool.dma_start(gng[:], gla_norm[bass.ds(l, 1), :].broadcast_to([128, HD])).then_inc(s_small, 16)
                for n in range(2):
                    pool.dma_start(w2b[16 * n:16 * n + 16, 256 * n:256 * n + 256],
                                   gla_w2.rearrange("l n r c -> (l n r) c")[bass.ds(l * 32 + n * 16, 16), :]
                                   ).then_inc(s_small, 16)
                pool.dma_start(w2b[32:33, :], gla_b2.rearrange("l n c -> l (n c)")[bass.ds(l, 1), :]).then_inc(s_small, 16)
                pool.dma_start(wr[:], w_router.rearrange("l k n -> (l k) n")[bass.ds(l * D, D), :]
                               .rearrange("(k p) n -> p k n", p=128)).then_inc(s_small, 16)
                NSM = 16 * 16
                wait(s_small, l * NSM + NSM)
                nc.gpsimd.tensor_scalar(gqk[:, 4:6, :], gqk[:, 4:6, :], 8.0, None, ALU.mult)
                nc.gpsimd.tensor_scalar(gng[:], gng[:], 8.0, None, ALU.mult).then_inc(s_smallx, 1)

                wait(s_ea, l * AAPL + 36 + 6)
                for t in range(NT):
                    pt = t - TILE_GROUP[t][0]
                    cs_ = cst[:, K_RC + pt * HD:K_RC + (pt + 1) * HD]
                    sn_ = cst[:, K_RC + 256 + pt * HD:K_RC + 256 + (pt + 1) * HD]
                    x = u[:, t, QC:QC + 384].rearrange("p (h d) -> p h d", d=HD)
                    a = c1[:].rearrange("p (h d) -> p h d", d=HD)
                    b = c2[:].rearrange("p (h d) -> p h d", d=HD)
                    nc.gpsimd.tensor_tensor(a, x, cs_.unsqueeze(1).broadcast_to([128, 6, HD]), ALU.mult)
                    for hf in range(2):
                        o, i_ = 32 * hf, 32 * (1 - hf)
                        nc.gpsimd.tensor_tensor(b[:, :, o:o + 32], x[:, :, i_:i_ + 32],
                                                sn_[:, o:o + 32].unsqueeze(1).broadcast_to([128, 6, 32]), ALU.mult)
                    pool.drain()
                    if t >= 2:
                        wait(s_tC, l * NT + t - 1)
                    r = rC[:, t % 2, :]
                    nc.gpsimd.tensor_tensor(r[:, 0:256].rearrange("p (a g d) -> p g a d", g=2, d=HD),
                                            c1[:, 0:256].rearrange("p (g a d) -> p g a d", g=2, d=HD),
                                            c2[:, 0:256].rearrange("p (g a d) -> p g a d", g=2, d=HD), ALU.add)
                    nc.gpsimd.tensor_tensor(r[:, 256:384], c1[:, 256:384], c2[:, 256:384], ALU.add)
                    pool.drain().then_inc(s_rC, 1)

                wait(s_tA, l * NT + NT)
                wait(s_tC, l * NT + NT)
                nc.gpsimd.memset(zT[:], 0.0).then_inc(s_zpad, 1)
                wait(s_ob, l * NT + NT)
                nc.gpsimd.memset(att[:], 0.0)
                pool.drain()
                nc.gpsimd.memset(zlT[32:33, :], 1.0)
                pool.drain().then_inc(s_az, 1)
                for g in range(8):
                    for i in range(NB):
                        wait(s_gm[i], l * 8 + g + 1)
                    G = gates[g % 2]
                    for i in range(2):
                        nc.gpsimd.tensor_tensor(G[:, 2 * i], G[:, 2 * i], G[:, 2 * i + 1], ALU.add)
                    pool.drain()
                    nc.gpsimd.tensor_tensor(merged[:, g, :].rearrange("p (t n) -> p t n", n=128), G[:, 0], G[:, 2],
                                            ALU.add).then_inc(s_mg, 1)

                for t in range(NT):
                    wait(s_ea, l * AAPL + (AA_O + 6 + t + 1) + 6)
                    pool.dma_start(x_d[t * 128:(t + 1) * 128, :], rows[:, t, :], accum_op=ALU.add).then_inc(s_xadd, 16)
                wait(s_xadd, l * 192 + 96)
                load_x(norm_ffn[bass.ds(l, 1), :])

                wait(s_xn, l * 18 + 12)
                nc.gpsimd.memset(scores[:], -1.0).then_inc(s_scz, 1)
                for n in range(2):
                    wait(s_h2[n], l * 48 + 48)
                wait(s_idx, l + 1)
                nc.gpsimd.tensor_copy(idx_g[:], idxT[:, 0:1])
                pool.drain()
                pool.indirect_dma_start(out=xe[:], out_offset=None, in_=h2_d,
                                        in_offset=bass.IndirectOffsetOnAxis(ap=idx_g[:, 0:1], axis=0)).then_inc(s_ga, 16)
                with pool.Fori(0, NE) as e:
                    nc.gpsimd.tensor_copy(idx_s[:], idxT[:, bass.ds(e, 1)])
                    wait(s_tp, l * TPL + e * 4 + (T_E + 2))
                    wait(s_ga, l * (17 * 16) + e * 16 + 16)
                    nc.gpsimd.tensor_copy(idx_g[:], idxT[:, bass.ds(e + 1, 1)])
                    pool.drain()
                    pool.indirect_dma_start(out=xe[:], out_offset=None, in_=h2_d,
                                            in_offset=bass.IndirectOffsetOnAxis(ap=idx_g[:, 0:1], axis=0)
                                            ).then_inc(s_ga, 16)
                    wait(s_y, l * 32 + e * 2 + 2)
                    pool.indirect_dma_start(out=x_d, out_offset=bass.IndirectOffsetOnAxis(ap=idx_s[:, 0:1], axis=0),
                                            in_=ye[:], in_offset=None, compute_op=ALU.add).then_inc(s_sca, 16)
                    wait(s_sca, l * 256 + e * 16 + 16)

                load_x(norm_ple[bass.ds(l, 1), :])
                wait(s_used, l * SPL + S_P + 2)
                for n, (src, t0, nt) in enumerate(((p_p, 0, 4), (p_s, 4, 2))):
                    pool.dma_start(prow[:, t0:t0 + nt, :],
                                   src.rearrange("l a s d -> (l a s) d")[bass.ds(l * (nt * 128), nt * 128), :]
                                   .rearrange("(t p) d -> p t d", p=128)).then_inc(s_pin, 16)
                for t in range(NT):
                    wait(s_ed, l * ADPL + (6 + t + 1) + 6)
                    pool.dma_start(x_d[t * 128:(t + 1) * 128, :], rows[:, t, :], accum_op=ALU.add).then_inc(s_xadd, 16)
                wait(s_xadd, l * 192 + 192)
            load_x(norm_final.rearrange("(a d) -> a d", a=1))

        @block.scalar
        def _(act):
            A = nc.scalar.activation
            act.drain().then_inc(s_thi, 2)
            act.drain().then_inc(s_ea, 6)
            act.drain().then_inc(s_fev, 1)
            act.wait_ge(s_eps, 1)

            def hi(step, j, w):
                act.wait_ge(s_raw[j % RAW], (step - j) * 2 + (j // RAW * 16 + 16))
                act.wait_ge(s_used, step + 1)
                A(whi[j % SPLIT][:, 0:w], raw[j % RAW][:, 0:w], ACT.Copy).then_inc(s_hi, 1)

            def gate_hi(l, f):
                act.wait_ge(s_fraw[f % FRAW], l * (16 * len(range(f % FRAW, NF, FRAW))) + (f // FRAW * 16 + 16))
                act.wait_ge(s_fused, l * NF + f + 1)
                A(fhi[f % FSPLIT][:], raw[f % FRAW][:].rearrange("p (k n) -> p k n", n=128), ACT.Copy).then_inc(s_fhi, 1)

            def gate_out(l, f):
                act.wait_ge(s_fused, l * NF + (f + 1 + FSPLIT))
                if f >= 2:
                    act.wait_ge(s_fout[f % 2], l * (8 * NF) + f // 2 * 16)
                b = gate_bank(f)
                A(fout[f % 2], PS[:, b:b + 2, :].rearrange("p a n -> p (a n)")[:, 0:TOK], ACT.Copy).then_inc(s_fev, 1)

            def mean_square(l3, t):
                act.wait_ge(s_xin[t], l3 * 16 + 16)
                A(PS[:, 0:2, :], rows[:, t, :].rearrange("p (a n) -> p a n", a=2), ACT.Square, scale=1.0 / 32,
                  accum_out=ms[:, t:t + 1])
                act.drain()
                A(ms[:, t:t + 1], ms[:, t:t + 1], ACT.Sqrt, bias=eps1[:]).then_inc(s_sq, 1)

            def t_hi(j, dst, src):
                act.wait_ge(s_tp, j + 1)
                A(dst, src, ACT.Copy).then_inc(s_thi, 1)

            def tbank(j, n=4, w=128):
                return PS[:, 6 + j % 2, 0:n * w].rearrange("p (k n) -> p k n", n=w)

            def norm(l, n, j0, dst):
                mean_square(l * 3 + n, 0)
                mean_square(l * 3 + n, 1)
                for t in range(NT):
                    if t + 2 < NT:
                        mean_square(l * 3 + n, t + 2)
                    for c in range(2):
                        t_hi(l * TPL + (j0 + 2 * t + c), dst[:, 4 * c:4 * c + 4, t * 128:(t + 1) * 128], tbank(c))

            with act.Fori(0, DEPTH) as l:
                norm(l, 0, T_N0, hT[0])

                def u_out(ck, t):
                    accumulated(act, l * CPL + ck, l * SPL + ck * 4 + 3, t)
                    A(u[:, t, bass.ds(ck * CW, CW)], PS[:, t, 0:CW], ACT.Copy).then_inc(s_ea, 1)

                def w_chunk(ck, j, ahead):
                    for n in range(3 if ahead else 0):
                        hi(l * SPL + ck * 4 + (4 + n), j + 4 + n, 2 * CW)
                    for t in range(NT):
                        u_out(ck, t)
                    if ahead:
                        hi(l * SPL + ck * 4 + 7, j + 7, 2 * CW)

                for n in range(4):
                    hi(l * SPL + n, n, 2 * CW)
                with act.Fori(0, 2) as i:
                    for j in range(2):
                        w_chunk(i * 2 + j, 4 * j, True)
                w_chunk(4, 0, True)
                w_chunk(5, 4, False)

                act.wait_ge(s_lo, l * SPL + (S_G + RAW))
                gate_hi(l, 0)
                act.wait_ge(s_ssq, l + 1)
                A(rqk[:], rqk[:], ACT.Sqrt, bias=eps64[:]).then_inc(s_rqk, 1)
                for t in range(NT):
                    gate_hi(l, t + 1)
                    act.wait_ge(s_tA, l * NT + t + 1)
                    A(qkA[:, :, t * 128:(t + 1) * 128], PS[:, 6, 0:384].rearrange("p (k n) -> p k n", n=128),
                      ACT.Copy).then_inc(s_qA, 1)
                    act.wait_ge(s_tC, l * NT + t + 1)
                    A(qkC[:, :, t * 128:(t + 1) * 128], PS[:, 7, 0:384].rearrange("p (k n) -> p k n", n=128),
                      ACT.Copy).then_inc(s_qC, 1)
                    gate_out(l, t)
                act.wait_ge(s_zpad, l + 1)
                for t in range(NT + 1):
                    if t < NT:
                        if t >= 2:
                            act.wait_ge(s_zr, l * NT + t - 1)
                        A(zsg[:, t % 2, :], u[:, t, UG:UG + 256], ACT.Sigmoid).then_inc(s_zs, 1)
                    if t >= 1:
                        m = t - 1
                        act.wait_ge(s_zt, l * NT + m + 1)
                        z0 = PAD + m * 128 + (PAD if m >= 4 else 0)
                        A(zT[:, :, z0:z0 + 128], PS[:, m % 2, 0:256].rearrange("p (c n) -> p c n", c=2),
                          ACT.Copy).then_inc(s_zT, 1)
                    if t in (2, 4):
                        gate_hi(l, F_Z + t // 2)
                    if t in (3, 5):
                        gate_out(l, F_Z + t // 2 - 1)
                for n in range(49):
                    if n < 48:
                        kind, t, h, k0, nk = unit(n)
                        act.wait_ge(s_nm, l * 48 + n + 1)
                        if n >= 2:
                            act.wait_ge(s_pt, l * 48 + n - 1)
                        src = PS[:, n % 2, 0:nk * 128] if kind == "A" else sC[n % 2][:, 0:nk * 128]
                        A(P[:, n % 2, 0:nk * 128], src, ACT.Exp, bias=nm[:, n:n + 1],
                          accum_out=sm[:, n:n + 1]).then_inc(s_p, 1)
                        if n % 3 == 0:
                            gate_hi(l, F_ATT + n // 3 + 1)
                        if n % 3 == 1:
                            gate_out(l, F_ATT + n // 3)
                    if n >= 1 and unit(n - 1)[0] == "C":
                        m = n - 1
                        kind, t, h, k0, nk = unit(m)
                        act.wait_ge(s_pt, l * 48 + m + 1)
                        act.wait_ge(s_pv, l * 48 + m - 1)
                        A(PT[:, m % 2, 0:nk * 128], PS[:, 2 + m % 2, 0:nk * 128], ACT.Copy).then_inc(s_ptC, 1)
                        if h == 3:
                            act.wait_ge(s_sk, l * NT + t + 1)
                            A(es[:, 4 * t:4 * t + 4], sk[:, 4 * t:4 * t + 4], ACT.Exp).then_inc(s_es, 1)

                gate_hi(l, F_CONV + 1)
                act.wait_ge(s_bn, l + 1)
                A(bnv[:, :, 1], bnv[:, :, 1], ACT.Sqrt, bias=eps1[:]).then_inc(s_bnr, 1)
                for t in range(NT):
                    act.wait_ge(s_zn, l * NT + t + 1)
                    A(u[:, t, UB:UB + 256], zn[:, t % 2, :], ACT.Silu).then_inc(s_ob, 1)
                    if t == 1:
                        gate_out(l, F_CONV)
                        gate_hi(l, F_GLA)
                gate_out(l, F_CONV + 1)
                A(u[:, :, RD:RD + 256], u[:, :, RD:RD + 256], ACT.Silu)
                act.drain().then_inc(s_g[10], 1)

                act.wait_ge(s_az, l + 1)
                for n in range(NT + 1):
                    buf = (E3 if n % 2 == 0 else TT)
                    old = (TT if n % 2 == 0 else E3)
                    if n < NT:
                        act.wait_ge(s_g[0], l * NT + n + 1)
                        A(zlT[0:32, :], PS[0:32, 0, 0:128], ACT.Copy).then_inc(s_g[1], 1)
                    if n >= 1:
                        act.wait_ge(s_g[5], l * NT + n)
                        A(old[:, 1, :], PS[:, 2, :], ACT.Exp)
                        A(dec[:, n - 1, :], PS[:, 3, 0:8], ACT.Exp)
                        act.drain().then_inc(s_g[6], 1)
                    if n < NT:
                        act.wait_ge(s_g[2], l * NT + n + 1)
                        A(buf[:, 0, :], PS[:, 1, :], ACT.Abs)
                        act.drain()
                        A(buf[:, 0, :], buf[:, 0, :], ACT.Exp, scale=-1.0)
                        act.drain()
                        A(buf[:, 0, :], buf[:, 0, :], ACT.Ln, bias=1.0).then_inc(s_g[3], 1)
                        if F_GLA + n + 1 < NF:
                            gate_hi(l, F_GLA + n + 1)
                        gate_out(l, F_GLA + n)
                act.wait_ge(s_scan, l + 1)
                for t in range(NT):
                    act.wait_ge(s_h[0], l * NT + t + 1)
                    A(E3[:, 0, :], PS[:, 0, :], ACT.Exp)
                    A(E3[:, 1, :], PS[:, 0, :], ACT.Exp, scale=-1.0)
                    A(E3[:, 2, :], PS[:, 1, :], ACT.Exp)
                    act.drain().then_inc(s_h[1], 1)
                    act.wait_ge(s_h[3], l * NT + t + 1)
                    A(TT[:, 0, :], PS[:, 2, :], ACT.Copy)
                    A(TT[:, 1, :], PS[:, 3, :], ACT.Copy)
                    act.drain().then_inc(s_h[4], 1)

                act.wait_ge(s_oss, l + 1)
                A(oss[:], oss[:], ACT.Sqrt, bias=eps64[:]).then_inc(s_or, 1)
                act.wait_ge(s_od, l + 1)
                for n in range(4):
                    hi(l * SPL + (S_G + n), n, 1024)
                for t in range(NT):
                    for c in range(2):
                        t_hi(l * TPL + (T_G + 2 * t + c), urblk[:, t, 2 * c:2 * c + 2, 1, :],
                             PS[:, 6 + c, :].rearrange("p (k n) -> p k n", n=256))
                for g in range(9):
                    if g < 8:
                        act.wait_ge(s_gl[g % 2], l * 256 + (g // 2 * 64 + 64))
                        A(gates_all[g % 2], gates_all[g % 2], ACT.Sigmoid).then_inc(s_sg, 1)
                    if g >= 1:
                        hi(l * SPL + (S_G + g + 3), g + 3, 1024)
                        act.wait_ge(s_mg, l * 8 + g)
                        A(hT[0][:, g - 1, :], merged[:, g - 1, :], ACT.Copy).then_inc(s_mh, 1)
                for c in range(2):
                    for n in range(4, 7):
                        hi(l * SPL + (S_O + 4 * c + n), 4 * c + n, 1024)
                    for t in range(NT):
                        accumulated(act, l * CPL + (C_O + c), l * SPL + (S_O + 4 * c + 3), t)
                        A(rows[:, t, c * 512:(c + 1) * 512], PS[:, t, :], ACT.Copy).then_inc(s_ea, 1)
                    hi(l * SPL + (S_O + 4 * c + 7), 4 * c + 7, 1024)

                mean_square(l * 3 + 1, 0)
                mean_square(l * 3 + 1, 1)
                for t in range(NT):
                    if t + 2 < NT:
                        mean_square(l * 3 + 1, t + 2)
                    for c in range(2):
                        t_hi(l * TPL + (T_N1 + 2 * t + c), hTf[:, 4 * c:4 * c + 4, t * 128:(t + 1) * 128], tbank(c))
                    act.dma_start(h2_d[t * 128:(t + 1) * 128, :], rows[:, t, :]).then_inc(s_h2[t % 2], 16)
                act.wait_ge(s_lm, l + 1)
                A(lg[:], lg[:], ACT.Exp).then_inc(s_le, 1)
                for c in range(2):
                    t_hi(l * TPL + (T_E + c), xeT[0][:, 4 * c:4 * c + 4, :], tbank(c, 4, CAP))
                with act.Fori(0, NE) as e:
                    for s in range(ES):
                        done = l * SPL + e * ES + (S_E + s + 1 + SPLIT)
                        j = l * TPL + e * 4 + (T_E + 2)
                        if s in (3, 11):
                            c = s // 8
                            act.wait_ge(s_used, done)
                            A(sil[:, c * 512:(c + 1) * 512], PS[0:CAP, c, :], ACT.Silu).then_inc(s_sil, 1)
                        if s == 11:
                            t_hi(j, hidT[0][:, 0:4, :], tbank(0, 4, CAP))
                        if s == 17:
                            t_hi(j + 1, hidT[0][:, 4:8, :], tbank(1, 4, CAP))
                        if s == 19:
                            t_hi(j + 2, xeT[0][:, 0:4, :], tbank(0, 4, CAP))
                        if s == 21:
                            t_hi(j + 3, xeT[0][:, 4:8, :], tbank(1, 4, CAP))
                        if s in (21, 23):
                            c = (s - 21) // 2
                            wait_alone(act, s_used, done)
                            A(ye[:, c * 512:(c + 1) * 512], PS[0:CAP, 4 + c, :], ACT.Copy,
                              scale=gateT[:, bass.ds(e, 1)]).then_inc(s_y, 1)
                        hi(l * SPL + e * ES + (S_E + s + 4), s + 4, 1024)

                norm(l, 2, T_N2, hT[0])
                for t in range(NT):
                    t_hi(l * TPL + (T_P + t), oT[0][:, :, t * 128:(t + 1) * 128], tbank(t, 2))
                for c in range(2):
                    s = l * SPL + (S_P + 8 * c)
                    for n in range(4, 7):
                        hi(s + n, n, 256)
                    for t in range(NT):
                        accumulated(act, l * CPL + (C_P + 2 * c), s + 3, t)
                        if c == 1:
                            act.wait_ge(s_ed, l * ADPL + (t + 1) + 6)
                        A(gsig[:, t, :], PS[:, t, :], ACT.Sigmoid).then_inc(s_ea, 1)
                    hi(s + 7, 7, 256)
                    if c == 0:
                        for n in range(8, 12):
                            hi(s + n, n, 1024)
            for t in range(NT):
                mean_square(DEPTH * 3, t)

        @block.vector
        def _(dve):
            V = nc.vector
            dve.drain().then_inc(s_lo, RAW)
            dve.drain().then_inc(s_tlo, 2)
            dve.drain().then_inc(s_ed, 6)

            def lo(step, j, w):
                dve.wait_ge(s_hi, step + 1)
                V.tensor_tensor(wlo[j % SPLIT][:, 0:w], raw[j % RAW][:, 0:w], whi[j % SPLIT][:, 0:w].bitcast(F32),
                                ALU.subtract).then_inc(s_lo, 1)

            def gate_lo(l, f):
                dve.wait_ge(s_fhi, l * NF + f + 1)
                V.tensor_tensor(flo[f % FSPLIT][:], raw[f % FRAW][:].rearrange("p (k n) -> p k n", n=128),
                                fhi[f % FSPLIT][:].bitcast(F32), ALU.subtract).then_inc(s_flo, 1)

            def t_lo(j, dst, src, hi_part):
                dve.wait_ge(s_thi, j + 1 + 2)
                V.tensor_tensor(dst, src, hi_part.bitcast(F32), ALU.subtract).then_inc(s_tlo, 1)

            def tbank(j, n=4, w=128):
                return PS[:, 6 + j % 2, 0:n * w].rearrange("p (k n) -> p k n", n=w)

            def normalise(l3, sq, t):
                if t == 0:
                    dve.wait_ge(s_gain, l3 * 16 + 16)
                dve.wait_ge(s_sq, sq + t + 1)
                V.reciprocal(rs[:, t:t + 1], ms[:, t:t + 1])
                dve.drain()
                V.scalar_tensor_tensor(rows[:, t, :], rows[:, t, :], rs[:, t:t + 1], gain[:], ALU.mult,
                                       ALU.mult).then_inc(s_xn, 1)

            def norm(l, n, j0):
                normalise(l * 3 + n, l * 18 + n * 6, 0)
                normalise(l * 3 + n, l * 18 + n * 6, 1)
                for t in range(NT):
                    for c in range(2):
                        k, s = slice(4 * c, 4 * c + 4), slice(t * 128, (t + 1) * 128)
                        t_lo(l * TPL + (j0 + 2 * t + c), hT[1][:, k, s], tbank(c), hT[0][:, k, s])
                    if t + 2 < NT:
                        normalise(l * 3 + n, l * 18 + n * 6, t + 2)

            def bc(ap, n):
                return ap.unsqueeze(2).broadcast_to([128, ap.shape[1], n])

            def heads(ap):
                return ap.rearrange("p (h d) -> p h d", d=HD)

            dve.wait_ge(s_cst, 16)
            with dve.Fori(0, DEPTH) as l:
                norm(l, 0, T_N0)
                with dve.Fori(0, NCH // 2) as i:
                    for j in range(8):
                        lo(l * SPL + i * 8 + j, j, 2 * CW)

                dve.wait_ge(s_smallx, l + 1)
                dve.wait_ge(s_ea, l * AAPL + 36 + 6)
                dve.wait_ge(s_used, l * SPL + (S_G + SPLIT))
                for t in range(NT):
                    x = u[:, t, QA:QA + 384]
                    V.tensor_tensor(s3[:] if t % 2 else s1[:], x, x, ALU.mult)
                    dve.drain()
                    V.tensor_reduce(rqk[:, t, :], heads(s3[:] if t % 2 else s1[:]), AX.X, ALU.add)
                dve.drain().then_inc(s_ssq, 1)
                gate_lo(l, 0)
                dve.wait_ge(s_rqk, l + 1)
                V.reciprocal(rqk[:], rqk[:])
                dve.drain()
                for t in range(NT):
                    pt = t - TILE_GROUP[t][0]
                    cs_ = cst[:, K_RA + pt * HD:K_RA + (pt + 1) * HD]
                    sn_ = cst[:, K_RA + 256 + pt * HD:K_RA + 256 + (pt + 1) * HD]
                    x = u[:, t, QA:QA + 384]
                    V.tensor_tensor(heads(s2[:]), heads(x), bc(rqk[:, t, :], HD), ALU.mult)
                    dve.drain()
                    V.tensor_tensor(s2[:], s2[:], gqk[:].rearrange("p h d -> p (h d)"), ALU.mult)
                    dve.drain()
                    V.tensor_tensor(heads(s1[:]), heads(s2[:]), cs_.unsqueeze(1).broadcast_to([128, 6, HD]), ALU.mult)
                    for hf in range(2):
                        o, i_ = 16 * hf, 16 * (1 - hf)
                        V.tensor_tensor(s3[:].rearrange("p (h a d) -> p h a d", a=2, d=32)[:, :, :, o:o + 16],
                                        s2[:].rearrange("p (h a d) -> p h a d", a=2, d=32)[:, :, :, i_:i_ + 16],
                                        sn_.rearrange("p (a d) -> p a d", d=32)[:, :, o:o + 16].unsqueeze(1)
                                        .broadcast_to([128, 6, 2, 16]), ALU.mult)
                    dve.drain()
                    if t >= 2:
                        dve.wait_ge(s_tA, l * NT + t - 1)
                    r = rA[:, t % 2, :]
                    V.tensor_tensor(r[:, 0:256].rearrange("p (a g d) -> p g a d", g=2, d=HD),
                                    s1[:, 0:256].rearrange("p (g a d) -> p g a d", g=2, d=HD),
                                    s3[:, 0:256].rearrange("p (g a d) -> p g a d", g=2, d=HD), ALU.add)
                    V.tensor_tensor(r[:, 256:384], s1[:, 256:384], s3[:, 256:384], ALU.add)
                    dve.drain().then_inc(s_rA, 1)
                    gate_lo(l, t + 1)

                for t in range(NT):
                    dve.wait_ge(s_zs, l * NT + t + 1)
                    if t >= 2:
                        dve.wait_ge(s_zt, l * NT + t - 1)
                    V.tensor_tensor(zr[:, t % 2, :], u[:, t, UB:UB + 256], zsg[:, t % 2, :],
                                    ALU.mult).then_inc(s_zr, 1)
                    if t in (2, 4):
                        gate_lo(l, F_Z + t // 2)
                dve.wait_ge(s_zT, l * NT + NT)

                def tap(n):
                    k, c = n // 2, n % 2
                    z = zT[:, c, k:k + AW]
                    if k == 0:
                        V.tensor_scalar(zacc[:, c, :], z, cw[:, c, 0:1], cb[:, c:c + 1], ALU.mult,
                                        ALU.add).then_inc(s_conv, 1)
                    else:
                        dve.wait_ge(s_conv, l * (2 * CONVW) + n - 1)
                        V.scalar_tensor_tensor(zacc[:, c, :], z, cw[:, c, k:k + 1], zacc[:, c, :], ALU.mult,
                                               ALU.add).then_inc(s_conv, 1)

                for n in range(51):
                    if n < 48:
                        kind, t, h, k0, nk = unit(n)
                        dve.wait_ge(s_sc, l * 48 + n + 1)
                        s = PS[:, n % 2, 0:nk * 128]
                        if kind == "A":
                            V.tensor_reduce(nm[:, n:n + 1], s, AX.X, ALU.max, negate=True).then_inc(s_nm, 1)
                        else:
                            m0 = K_WM + (k0 - (t - 1)) * 128
                            if n >= 26:
                                dve.wait_ge(s_p, l * 48 + n - 1)
                            V.scalar_tensor_tensor(sC[n % 2][:, 0:nk * 128], s, 0.125, cst[:, m0:m0 + nk * 128],
                                                   ALU.mult, ALU.add)
                            dve.drain()
                            V.tensor_reduce(small[:, 16:17], sC[n % 2][:, 0:nk * 128], AX.X, ALU.max)
                            dve.drain()
                            V.tensor_scalar(nm[:, n:n + 1], small[:, 16:17], sink_b[:, h:h + 1], -1.0, ALU.max,
                                            ALU.mult).then_inc(s_nm, 1)
                            if h == 3:
                                dve.drain()
                                V.tensor_tensor(sk[:, 4 * t:4 * t + 4], nm[:, n - 3:n + 1], sink_b[:],
                                                ALU.add).then_inc(s_sk, 1)
                    if 1 <= n <= 48 and unit(n - 1)[0] == "A":
                        m = n - 1
                        nk = unit(m)[4]
                        dve.wait_ge(s_pt, l * 48 + m + 1)
                        if m >= 2:
                            dve.wait_ge(s_pv, l * 48 + m - 1)
                        V.tensor_copy(PT[:, m % 2, 0:nk * 128], PS[:, 2 + m % 2, 0:nk * 128]).then_inc(s_ptA, 1)
                    if n >= 3 and unit(n - 3)[2] == 3:
                        m = n - 3
                        kind, t, h, k0, nk = unit(m)
                        dve.wait_ge(s_pv, l * 48 + m + 1)
                        tot = sm[:, m - 3:m + 1]
                        if kind == "C":
                            dve.wait_ge(s_es, l * NT + t + 1)
                            V.tensor_tensor(rcp[:, m - 3:m + 1], tot, es[:, 4 * t:4 * t + 4], ALU.add)
                            dve.drain()
                            tot = rcp[:, m - 3:m + 1]
                        V.reciprocal(rcp[:, m - 3:m + 1], tot)
                        dve.drain()
                        q0 = QA if kind == "A" else QC
                        V.tensor_tensor(heads(u[:, t, q0:q0 + 256]), heads(PS[:, 4 + (m // 4) % 2, 0:256]),
                                        bc(rcp[:, m - 3:m + 1], HD), ALU.mult).then_inc(s_o, 1)
                    for k in range(2 * CONVW * n // 48, min(2 * CONVW * (n + 1) // 48, 2 * CONVW)):
                        tap(k)
                    if n < 48 and n % 3 == 1:
                        gate_lo(l, F_ATT + n // 3 + 1)

                for t in range(NT):
                    dve.wait_ge(s_zb, l * NT + t + 1)
                    V.bn_stats(bns[:, t, :], PS[:, t, 0:256])
                    dve.drain()
                    V.bn_aggr(bnv[:, t, :], bns[:, t, :])
                dve.drain().then_inc(s_bn, 1)
                gate_lo(l, F_CONV + 1)
                dve.wait_ge(s_bnr, l + 1)
                V.reciprocal(bnv[:, :, 1], bnv[:, :, 1])
                dve.drain()
                for t in range(NT):
                    if t >= 2:
                        dve.wait_ge(s_ob, l * NT + t - 1)
                    V.tensor_scalar(zn[:, t % 2, :], PS[:, t, 0:256], bnv[:, t, 0:1], bnv[:, t, 1:2],
                                    ALU.subtract, ALU.mult)
                    dve.drain()
                    V.tensor_tensor(zn[:, t % 2, :], zn[:, t % 2, :], lng[:], ALU.mult)
                    dve.drain()
                    V.tensor_tensor(zn[:, t % 2, :], zn[:, t % 2, :], lnb[:], ALU.add).then_inc(s_zn, 1)
                    if t == 3:
                        gate_lo(l, F_GLA)

                dve.wait_ge(s_g[10], l + 1)
                dve.wait_ge(s_az, l + 1)
                for n in range(NT + 1):
                    buf = (E3 if n % 2 == 0 else TT)
                    old = (TT if n % 2 == 0 else E3)
                    if n >= 1:
                        m = n - 1
                        dve.wait_ge(s_g[6], l * NT + m + 1)
                        V.tensor_tensor(old[:, 1, :].rearrange("p (a n) -> p a n", a=2),
                                        u[:, m, KD:KD + 256].unsqueeze(1).broadcast_to([128, 2, 256]),
                                        old[:, 1, :].rearrange("p (a n) -> p a n", a=2), ALU.mult).then_inc(s_g[7], 1)
                        dve.wait_ge(s_g[8], l * NT + m + 1)
                        for c in range(2):
                            V.tensor_copy(kvs[:, 2 * m + c, :, :],
                                          PS[:, 4 + c, 0:256].rearrange("p (a n) -> p a n", n=HD))
                        dve.drain().then_inc(s_g[9], 1)
                    if n < NT:
                        dve.wait_ge(s_g[3], l * NT + n + 1)
                        V.scalar_tensor_tensor(la[:, n, :], PS[:, 1, :], 0.0, buf[:, 0, :], ALU.min,
                                               ALU.subtract).then_inc(s_g[4], 1)
                        if F_GLA + n + 1 < NF:
                            gate_lo(l, F_GLA + n + 1)
                for r in range(1, 8):
                    for (a, b) in GROUPS:
                        c0, c1_ = 2 * a, 2 * b
                        if r >= c1_ - c0:
                            continue
                        for d in range(2):
                            c = c0 + r if d == 0 else c1_ - 1 - r
                            prev = c - 1 if d == 0 else c + 1
                            for p in range(2):
                                k = 2 * d + p
                                V.scalar_tensor_tensor(kvs[:, c, k, :], kvs[:, prev, k, :],
                                                       dec[:, c // 2, 2 * k + c % 2:2 * k + c % 2 + 1],
                                                       kvs[:, c, k, :], ALU.mult, ALU.add)
                    dve.drain()
                dve.drain().then_inc(s_scan, 1)
                for n in range(NT + 1):
                    m = n - 1
                    if n >= 1:
                        wait_alone(dve, s_h[6], l * NT + m + 1)
                        for par in range(2):
                            V.copy_predicated(att[:, par, :], cst[:, K_GM:K_GM + 512].bitcast(I32), PS[:, 5 + par, :])
                        dve.drain().then_inc(s_h[7], 1)
                    if n < NT:
                        dve.wait_ge(s_h[1], l * NT + n + 1)
                        for k, (src, f) in enumerate(((QD, 0.125), (KD, 1.0), (QD, 0.125))):
                            e = E3[:, k, :].rearrange("p (a n) -> p a n", a=2)
                            V.scalar_tensor_tensor(e, u[:, n, src:src + 256].unsqueeze(1).broadcast_to([128, 2, 256]),
                                                   f, e, ALU.mult, ALU.mult)
                        dve.drain().then_inc(s_h[2], 1)
                    if n >= 1:
                        dve.wait_ge(s_h[8], l * NT + m + 1)
                        ob = u[:, m, QD:QD + 256].rearrange("p (a h d) -> p a h d", h=2, d=HD)
                        for par in range(2):
                            V.tensor_copy(ob[:, :, par, :], PS[:, (7, 2)[par], 0:128].rearrange("p (a d) -> p a d", d=HD))
                        dve.drain().then_inc(s_h[9], 1)
                    if n < NT:
                        dve.wait_ge(s_h[3], l * NT + n + 1)
                        V.tensor_copy(TT[:, 2, :], PS[:, 4, :]).then_inc(s_h[5], 1)
                    if n >= 1:
                        V.tensor_tensor(osq[:], u[:, m, QD:QD + 256], u[:, m, QD:QD + 256], ALU.mult)
                        dve.drain()
                        V.tensor_reduce(oss[:, m, :], heads(osq[:]), AX.X, ALU.add)
                dve.drain().then_inc(s_oss, 1)
                od = u[:, :, QD:QD + 256]
                od4 = od.rearrange("p t (h d) -> p t h d", d=HD)
                dve.wait_ge(s_or, l + 1)
                V.reciprocal(oss[:], oss[:])
                dve.drain()
                V.tensor_tensor(od4, od4, oss[:].unsqueeze(3).broadcast_to([128, NT, 4, HD]), ALU.mult)
                dve.drain()
                V.tensor_tensor(od4, od4, gng[:].unsqueeze(1).unsqueeze(1).broadcast_to([128, NT, 4, HD]), ALU.mult)
                dve.drain()
                V.tensor_tensor(od, od, u[:, :, RD:RD + 256], ALU.mult).then_inc(s_od, 1)

                for n in range(4):
                    lo(l * SPL + (S_G + n), n, 1024)
                for t in range(NT):
                    for c in range(2):
                        t_lo(l * TPL + (T_G + 2 * t + c), urblk[:, t, 2 * c:2 * c + 2, 0, :],
                             PS[:, 6 + c, :].rearrange("p (k n) -> p k n", n=256), urblk[:, t, 2 * c:2 * c + 2, 1, :])
                for g in range(9):
                    if g < 8:
                        dve.wait_ge(s_sg, l * 8 + g + 1)
                        for i in range(NB):
                            if i < NB - 1:
                                dve.wait_ge(s_br[i], l * 8 + g + 1)
                            else:
                                dve.wait_ge(s_used, l * SPL + (S_G + g + 1 + SPLIT))
                            G = gates[g % 2][:, i]
                            V.tensor_tensor(G, G, PS[:, 2 * i:2 * i + 2, :].rearrange("p a n -> p (a n)")[:, 0:TOK]
                                            .rearrange("p (t n) -> p t n", n=128), ALU.mult).then_inc(s_gm[i], 1)
                    if g >= 1:
                        lo(l * SPL + (S_G + g + 3), g + 3, 1024)
                        dve.wait_ge(s_mh, l * 8 + g)
                        V.tensor_tensor(hT[1][:, g - 1, :], merged[:, g - 1, :], hT[0][:, g - 1, :].bitcast(F32),
                                        ALU.subtract).then_inc(s_ml, 1)
                for j in range(4, 12):
                    lo(l * SPL + (S_O + j), j, 1024)

                for t in range(NT):
                    normalise(l * 3 + 1, l * 18 + 6, t)
                dve.wait_ge(s_rt, l + 1)
                pr = PS[:, 2, 0:NT * NE].rearrange("p (t e) -> p t e", e=NE)
                V.tensor_reduce(lmx[:], pr, AX.X, ALU.max)
                dve.drain()
                V.tensor_tensor(lg[:], pr, bc(lmx[:], NE), ALU.subtract).then_inc(s_lm, 1)
                dve.wait_ge(s_le, l + 1)
                V.tensor_reduce(lsm[:], lg[:], AX.X, ALU.add)
                dve.drain()
                V.reciprocal(lmx[:], lsm[:])
                dve.drain()
                V.tensor_tensor(lg[:], lg[:], bc(lmx[:], NE), ALU.mult).then_inc(s_af, 1)
                dve.wait_ge(s_aft, l + 1)
                dve.wait_ge(s_scz, l + 1)
                V.tensor_copy(scores[0:NE, :], PS[0:NE, 3, :])
                V.tensor_copy(scores[32:32 + NE, 0:DEC], PS[0:NE, 4, 0:DEC])
                dve.drain()
                for r in range(CAPP // 8):
                    v, ix = top[:, 8 * r:8 * r + 8], topi[:, 8 * r:8 * r + 8]
                    V.max(v, scores[:])
                    dve.drain()
                    V.max_index(ix, v, scores[:])
                    dve.drain()
                    V.match_replace(scores[:], v, scores[:], -1.0)
                    dve.drain()
                V.tensor_copy(pick[:, 0, 0:CAPP], topi[0:NE, :])
                V.tensor_copy(pick[:, 1, 0:CAPP], top[0:NE, :])
                V.tensor_scalar(pick[:, 0, CAPP:CAP], topi[32:32 + NE, 0:CAPS], float(SEQ), None, ALU.add)
                V.tensor_copy(pick[:, 1, CAPP:CAP], top[32:32 + NE, 0:CAPS])
                dve.drain().then_inc(s_pick, 1)
                dve.wait_ge(s_pickt, l + 1)
                V.tensor_copy(idxT[:, 0:NE], PS[0:CAP, 5, 0:NE])
                V.tensor_copy(idxT[:, NE:NE + 1], PS[0:CAP, 5, 0:1])
                V.tensor_copy(gateT[:], PS[0:CAP, 5, NE:2 * NE])
                dve.drain().then_inc(s_idx, 1)
                for c in range(2):
                    k = slice(4 * c, 4 * c + 4)
                    t_lo(l * TPL + (T_E + c), xeT[1][:, k, :], tbank(c, 4, CAP), xeT[0][:, k, :])
                with dve.Fori(0, NE) as e:
                    for s in range(ES):
                        j = l * TPL + e * 4 + (T_E + 2)
                        if s in (7, 15):
                            c = s // 8
                            dve.wait_ge(s_used, l * SPL + e * ES + (S_E + s + 1 + SPLIT))
                            dve.wait_ge(s_sil, l * 32 + e * 2 + (c + 1))
                            h = sil[:, c * 512:(c + 1) * 512]
                            V.tensor_tensor(h, h, PS[0:CAP, 2 + c, :], ALU.mult).then_inc(s_hid, 1)
                        if s == 11:
                            t_lo(j, hidT[1][:, 0:4, :], tbank(0, 4, CAP), hidT[0][:, 0:4, :])
                        if s == 17:
                            t_lo(j + 1, hidT[1][:, 4:8, :], tbank(1, 4, CAP), hidT[0][:, 4:8, :])
                        if s == 19:
                            t_lo(j + 2, xeT[1][:, 0:4, :], tbank(0, 4, CAP), xeT[0][:, 0:4, :])
                        if s == 21:
                            t_lo(j + 3, xeT[1][:, 4:8, :], tbank(1, 4, CAP), xeT[0][:, 4:8, :])
                        lo(l * SPL + e * ES + (S_E + s + 4), s + 4, 1024)

                norm(l, 2, T_N2)
                for t in range(NT):
                    s = slice(t * 128, (t + 1) * 128)
                    t_lo(l * TPL + (T_P + t), oT[1][:, :, s], tbank(t, 2), oT[0][:, :, s])
                for c in range(2):
                    s = l * SPL + (S_P + 8 * c)
                    for n in range(4, 8):
                        lo(s + n, n, 256)
                    if c == 0:
                        for n in range(8, 12):
                            lo(s + n, n, 1024)
                    for t in range(NT):
                        accumulated(dve, l * CPL + (C_P + 2 * c + 1), s + 7, t)
                        V.tensor_tensor(rows[:, t, c * 512:(c + 1) * 512], gsig[:, t, :], PS[:, t, :],
                                        ALU.mult).then_inc(s_ed, 1)
            for t in range(NT):
                normalise(DEPTH * 3, DEPTH * 18, t)

        @block.tensor
        def _(pe):
            pe.drain().then_inc(s_used, SPLIT)
            pe.drain().then_inc(s_fused, FSPLIT)
            pe.wait_ge(s_cst, 16)

            def transposes(j, b, blocks, free, np_=128, w=128):
                sm_, v = free
                pe.wait_ge(sm_, v)
                for n, x in enumerate(blocks):
                    m = nc.tensor.transpose(PS[:, 6 + b, n * np_:(n + 1) * np_], x, ident[0:np_, 0:np_])
                m.then_inc(s_tp, 1)

            def norm(l, n, j0, plain=False):
                for t in range(NT):
                    pe.wait_ge(s_xn, l * 18 + (n * 6 + t + 1))
                    for c in range(2):
                        j = j0 + 2 * t + c
                        if plain and j - 2 >= j0:
                            free = (s_thi, l * TPL + (j - 1) + 2)
                        else:
                            free = (s_tlo, l * TLL + lo_count(j - 2) + 2)
                        transposes(j, c, [rows[:, t, k * 128:(k + 1) * 128] for k in range(4 * c, 4 * c + 4)], free)

            def product(out, x, w, first, last):
                nc.tensor.matmul(out, x[0], w[0], start=first, stop=False)
                nc.tensor.matmul(out, x[0], w[1], start=False, stop=False)
                return nc.tensor.matmul(out, x[1], w[0], start=False, stop=last)

            def step(val, j, nk, n, x, k0, first, last, free=None, c0=0, final=True):
                pe.wait_ge(s_lo, val + 1 + RAW)
                for k in range(nk):
                    for t in range(NT):
                        if free is not None and k == 0:
                            pe.wait_ge(*free(t))
                        s = slice(t * 128, (t + 1) * 128)
                        m = product(PS[:, t, c0:c0 + n], (x[0][:, k0 + k, s], x[1][:, k0 + k, s]),
                                    (cols(whi[j % SPLIT], nk, n)[:, k, :], cols(wlo[j % SPLIT], nk, n)[:, k, :]),
                                    first and k == 0, last and k == nk - 1)
                        if last and final and k == nk - 1 and t < NT - 1:
                            m.then_inc(s_acc, 1)
                m.then_inc(s_used, 1)

            def chunk(val, n, free):
                for j in range(4):
                    step(val + j, j, 2, n, hT, 2 * j, j == 0, j == 3, free if j == 0 else None)

            def transposed(b, w, x, first, last):
                for p, (wn, xn) in enumerate(((0, 0), (0, 1), (1, 0))):
                    for t0, t1, bb in ((0, 4, b), (4, NT, b + 1)):
                        m = nc.tensor.matmul(PS[:, bb, 0:(t1 - t0) * 128], w[wn], x[xn](t0, t1),
                                             start=first and p == 0, stop=last and p == 2)
                return m

            def gate_step(l, f):
                pe.wait_ge(s_flo, l * NF + f + 1)
                pe.wait_ge(s_fev, l * NF + f + 1)
                for k in range(KT):
                    m = transposed(gate_bank(f), [w[f % FSPLIT][:, k, :] for w in (fhi, flo)],
                                   [lambda a, b, x=x: x[:, k, a * 128:b * 128] for x in hT], k == 0, k == KT - 1)
                m.then_inc(s_fused, 1)

            def branch_chunk(val, free):
                for j in range(4):
                    step(val + j, j, 1, 256, oT, j % 2, j % 2 == 0, j % 2 == 1, free if j == 0 else None,
                         (j // 2) * 256, j == 3)

            with pe.Fori(0, DEPTH) as l:
                norm(l, 0, T_N0)
                wait_alone(pe, s_tlo, l * TLL + lo_count(T_N0 + 11) + 2)
                with pe.Fori(0, NCH // 2) as i:
                    for j in range(2):
                        chunk(l * SPL + i * 8 + 4 * j, CW, lambda t: (s_ea, l * AAPL + i * 12 + (j * 6 + t + 1)))

                pe.wait_ge(s_ea, l * AAPL + 36 + 6)
                for t in range(NT):
                    gate_step(l, F_ROPE + t)
                    pe.wait_ge(s_rA, l * NT + t + 1)
                    if t >= 1:
                        pe.wait_ge(s_qA, l * NT + t)
                    for k in range(3):
                        m = nc.tensor.transpose(PS[:, 6, k * 128:(k + 1) * 128], rA[:, t % 2, k * 128:(k + 1) * 128], ident)
                    m.then_inc(s_tA, 1)
                    pe.wait_ge(s_rC, l * NT + t + 1)
                    if t >= 1:
                        pe.wait_ge(s_qC, l * NT + t)
                    for k in range(3):
                        m = nc.tensor.transpose(PS[:, 7, k * 128:(k + 1) * 128], rC[:, t % 2, k * 128:(k + 1) * 128], ident)
                    m.then_inc(s_tC, 1)
                pe.wait_ge(s_qA, l * NT + NT)
                pe.wait_ge(s_qC, l * NT + NT)
                for t in range(NT):
                    if t in (2, 4):
                        gate_step(l, F_Z + t // 2 - 1)
                    pe.wait_ge(s_zr, l * NT + t + 1)
                    if t >= 2:
                        pe.wait_ge(s_zT, l * NT + t - 1)
                    for c in range(2):
                        m = nc.tensor.transpose(PS[:, t % 2, c * 128:(c + 1) * 128], zr[:, t % 2, c * 128:(c + 1) * 128], ident)
                    m.then_inc(s_zt, 1)
                pe.wait_ge(s_zT, l * NT + NT)
                for n in range(50):
                    if n < 48:
                        kind, t, h, k0, nk = unit(n)
                        if n >= 2:
                            pe.wait_ge(s_p, l * 48 + n - 1)
                        qk = qkA if kind == "A" else qkC
                        g = slice(64 * (h // 2), 64 * (h // 2) + 64)
                        nc.tensor.matmul(PS[:, n % 2, 0:nk * 128], qk[g, h % 2, t * 128:(t + 1) * 128],
                                         qk[g, 2, k0 * 128:(k0 + nk) * 128], start=True, stop=True).then_inc(s_sc, 1)
                        if n % 3 == 0:
                            gate_step(l, F_ATT + n // 3)
                    if 1 <= n <= 48:
                        m = n - 1
                        kind, t, h, k0, nk = unit(m)
                        pe.wait_ge(s_p, l * 48 + m + 1)
                        if m >= 2:
                            pe.wait_ge(*pt_done(l, m - 2))
                        for k in range(nk):
                            mm = nc.tensor.transpose(PS[:, 2 + m % 2, k * 128:(k + 1) * 128],
                                                     P[:, m % 2, k * 128:(k + 1) * 128], ident)
                        mm.then_inc(s_pt, 1)
                    if n >= 2:
                        m = n - 2
                        kind, t, h, k0, nk = unit(m)
                        pe.wait_ge(*pt_done(l, m))
                        if h == 0 and m >= 8:
                            pe.wait_ge(s_o, l * 12 + m // 4 - 1)
                        v0 = (VA if kind == "A" else VC) + 64 * (h // 2)
                        for k in range(nk):
                            mm = nc.tensor.matmul(PS[:, 4 + (m // 4) % 2, h * HD:(h + 1) * HD],
                                                  PT[:, m % 2, k * 128:(k + 1) * 128], u[:, k0 + k, v0:v0 + HD],
                                                  start=k == 0, stop=k == nk - 1)
                        mm.then_inc(s_pv, 1)

                pe.wait_ge(s_conv, l * (2 * CONVW) + 2 * CONVW)
                pe.wait_ge(s_o, l * 12 + 12)
                for t in range(NT):
                    a0 = t * 128 + (PAD if t >= 4 else 0)
                    for c in range(2):
                        m = nc.tensor.transpose(PS[:, t, c * 128:(c + 1) * 128], zacc[:, c, a0:a0 + 128], ident)
                    m.then_inc(s_zb, 1)
                for f in range(2):
                    gate_step(l, F_CONV + f)

                pe.wait_ge(s_az, l + 1)
                cum = [cst[:, K_CUM + n * 128:K_CUM + (n + 1) * 128] for n in range(6)]
                for n in range(NT + 1):
                    m = n - 1
                    if n < NT:
                        pe.wait_ge(s_ob, l * NT + NT)
                        if n >= 1:
                            pe.wait_ge(s_g[1], l * NT + n)
                        nc.tensor.transpose(PS[0:32, 0, 0:128], u[:, n, ZL:ZL + 32], ident).then_inc(s_g[0], 1)
                    if n >= 1:
                        pe.wait_ge(s_g[4], l * NT + n)
                        for d in range(2):
                            nc.tensor.matmul(PS[:, 2, d * 256:(d + 1) * 256], cum[3 * d + 2],
                                             la[:, m, d * 256:(d + 1) * 256], start=True, stop=True)
                        for k in range(4):
                            mm = nc.tensor.matmul(PS[:, 3, 2 * k:2 * k + 2], la[:, m, k * 128:(k + 1) * 128],
                                                  cst[:, K_IND:K_IND + 2], start=True, stop=True)
                        mm.then_inc(s_g[5], 1)
                    if n < NT:
                        pe.wait_ge(s_g[1], l * NT + n + 1)
                        nc.tensor.matmul(PS[:, 1, :], zlT[0:33, :], w2b[0:33, :], start=True, stop=True).then_inc(s_g[2], 1)
                        gate_step(l, F_GLA + n)
                    if n >= 1:
                        wait_alone(pe, s_g[7], l * NT + n)
                        if n >= 2:
                            pe.wait_ge(s_g[9], l * NT + n - 1)
                        old = (TT if n % 2 == 0 else E3)
                        for c in range(2):
                            cr = slice(64 * c, 64 * c + 64)
                            for d in range(2):
                                for h in range(4):
                                    mm = nc.tensor.matmul(
                                        PS[64 * (h % 2):64 * (h % 2) + 64, 4 + c, (2 * d + h // 2) * HD:(2 * d + h // 2 + 1) * HD],
                                        old[cr, 1, d * 256 + h * HD:d * 256 + (h + 1) * HD],
                                        u[cr, m, VD + h * HD:VD + (h + 1) * HD], start=True, stop=True)
                        mm.then_inc(s_g[8], 1)
                pe.wait_ge(s_scan, l + 1)
                for n in range(NT + 1):
                    m = n - 1
                    if n < NT:
                        if n >= 1:
                            pe.wait_ge(s_h[1], l * NT + n)
                        for b, k in ((0, 1), (1, 0)):
                            for d in range(2):
                                mm = nc.tensor.matmul(PS[:, b, d * 256:(d + 1) * 256], cum[3 * d + k],
                                                      la[:, n, d * 256:(d + 1) * 256], start=True, stop=True)
                        mm.then_inc(s_h[0], 1)
                    if n >= 1:
                        pe.wait_ge(s_h[4], l * NT + n)
                        pe.wait_ge(s_h[5], l * NT + n)
                        if n >= 2:
                            pe.wait_ge(s_h[7], l * NT + n - 1)
                        for par in range(2):
                            g = slice(64 * par, 64 * par + 64)
                            for k in range(4):
                                mm = nc.tensor.matmul(PS[:, 5 + par, k * 128:(k + 1) * 128],
                                                      TT[g, 1, k * 128:(k + 1) * 128], TT[g, 0, k * 128:(k + 1) * 128],
                                                      start=True, stop=True)
                        mm.then_inc(s_h[6], 1)
                        pe.wait_ge(s_h[7], l * NT + n)
                        if n >= 2:
                            pe.wait_ge(s_h[9], l * NT + n - 1)
                        ga, gb = TILE_GROUP[m]
                        for par in range(2):
                            g = slice(64 * par, 64 * par + 64)
                            for p in range(2):
                                h = 2 * p + par
                                ob = PS[:, (7, 2)[par], p * HD:(p + 1) * HD]
                                for d in range(2):
                                    k = 2 * d + p
                                    mm = nc.tensor.matmul(ob, att[:, par, k * 128:(k + 1) * 128],
                                                          u[:, m, VD + h * HD:VD + (h + 1) * HD],
                                                          start=d == 0, stop=False, skip_group_check=True)
                                for d in range(2):
                                    k = 2 * d + p
                                    for c in range(2):
                                        ch = 2 * m + c
                                        if ch == (2 * ga if d == 0 else 2 * gb - 1):
                                            continue
                                        mm = nc.tensor.matmul(
                                            PS[64 * c:64 * c + 64, (7, 2)[par], p * HD:(p + 1) * HD],
                                            TT[g, 2, k * 128 + 64 * c:k * 128 + 64 * c + 64],
                                            kvs[g, ch - 1 if d == 0 else ch + 1, k, :],
                                            start=False, stop=True, skip_group_check=True)
                        mm.then_inc(s_h[8], 1)
                    if n < NT:
                        pe.wait_ge(s_h[2], l * NT + n + 1)
                        if n >= 1:
                            pe.wait_ge(s_h[9], l * NT + n)
                        for b in range(3):
                            for k in range(4):
                                mm = nc.tensor.transpose(PS[:, 2 + b, k * 128:(k + 1) * 128],
                                                         E3[:, b, k * 128:(k + 1) * 128], ident)
                        mm.then_inc(s_h[3], 1)

                wait_alone(pe, s_od, l + 1)
                for t in range(NT):
                    for c in range(2):
                        transposes(None, c, [ublk[:, t, 2 * c + k // 2, 0, (k % 2) * 128:(k % 2) * 128 + 128]
                                             for k in range(4)], (s_tlo, l * TLL + (T_G + 2 * t + c + 1)))
                pe.wait_ge(s_tlo, l * TLL + (T_G + 12 + 2))
                for g in range(8):
                    pe.wait_ge(s_lo, l * SPL + (S_G + g + 1 + RAW))
                    w = [x[g % SPLIT][:].rearrange("p (k n) -> p k n", n=128) for x in (whi, wlo)]
                    for i in range(NB):
                        if g >= 1:
                            pe.wait_ge(s_gm[i], l * 8 + g)
                        for k in range(2):
                            c = slice(k * 128, (k + 1) * 128)
                            m = transposed(2 * i, [x[:, 2 * i + k, :] for x in w],
                                           [lambda a, b, h=h: urblk[:, a:b, i, h, c] for h in (1, 0)], k == 0, k == 1)
                        m.then_inc(s_br[i] if i < NB - 1 else s_used, 1)
                for i in range(NB):
                    pe.wait_ge(s_gm[i], l * 8 + 8)
                pe.wait_ge(s_ml, l * 8 + 8)
                for c in range(2):
                    of = None if c == 0 else (lambda t: (s_ea, l * AAPL + (AA_O + t + 1 + 6)))
                    chunk(l * SPL + (S_O + 4 * c), 512, of)

                norm(l, 1, T_N1, plain=True)
                pe.wait_ge(s_thi, l * TPL + (T_N1 + 12 + 2))
                for t in range(NT):
                    for k in range(KT):
                        mm = nc.tensor.matmul(PS[:, 2, t * NE:(t + 1) * NE], hTf[:, k, t * 128:(t + 1) * 128],
                                              wr[:, k, :], start=k == 0, stop=k == KT - 1)
                mm.then_inc(s_rt, 1)
                pe.wait_ge(s_af, l + 1)
                for t in range(NT):
                    b, o = (3, t) if t < 4 else (4, t - 4)
                    mm = nc.tensor.transpose(PS[0:NE, b, o * 128:(o + 1) * 128], lg[:, t, :], ident)
                mm.then_inc(s_aft, 1)
                wait_alone(pe, s_pick, l + 1)
                for n in range(2):
                    mm = nc.tensor.transpose(PS[0:CAP, 5, n * NE:(n + 1) * NE], pick[:, n, :], ident[0:NE, 0:NE])
                mm.then_inc(s_pickt, 1)
                pe.wait_ge(s_ga, l * (17 * 16) + 16)
                pe.wait_ge(s_idx, l + 1)
                for c in range(2):
                    transposes(None, c, [xe[:, k * 128:(k + 1) * 128] for k in range(4 * c, 4 * c + 4)],
                               (s_thi, l * TPL + (T_E + c - 1 + 2)), CAP)

                def expert_steps(e, s0, n, bank, x, k0, first, last):
                    for j in range(n):
                        pe.wait_ge(s_lo, l * SPL + e * ES + (S_E + s0 + j + 1 + RAW))
                        w = [cols(x_[(s0 + j) % SPLIT], 2, 512) for x_ in (whi, wlo)]
                        for k in range(2):
                            kk = k0 + 2 * j + k
                            m = product(PS[0:CAP, bank, :], (x[0][:, kk, :], x[1][:, kk, :]), (w[0][:, k, :], w[1][:, k, :]),
                                        first and j == 0 and k == 0, last and j == n - 1 and k == 1)
                        m.then_inc(s_used, 1)

                with pe.Fori(0, NE) as e:
                    tl = l * TLL + e * 4 + (T_E - 12 + 2 + 2)
                    pe.wait_ge(s_tlo, tl)
                    for c in range(2):
                        expert_steps(e, 8 * c, 4, c, xeT, 0, True, True)
                        if c == 1:
                            pe.wait_ge(s_hid, l * 32 + e * 2 + 1)
                            transposes(None, 0, [sil[:, k * 128:(k + 1) * 128] for k in range(4)], (s_tlo, tl), CAP)
                        expert_steps(e, 8 * c + 4, 4, 2 + c, xeT, 0, True, True)
                    pe.wait_ge(s_tlo, tl + 1)
                    expert_steps(e, 16, 2, 4, hidT, 0, True, False)
                    pe.wait_ge(s_hid, l * 32 + e * 2 + 2)
                    transposes(None, 1, [sil[:, k * 128:(k + 1) * 128] for k in range(4, 8)], (s_tlo, tl), CAP)
                    expert_steps(e, 18, 2, 5, hidT, 0, True, False)
                    pe.wait_ge(s_ga, l * (17 * 16) + e * 16 + 32)
                    transposes(None, 0, [xe[:, k * 128:(k + 1) * 128] for k in range(4)], (s_tlo, tl + 1), CAP)
                    pe.wait_ge(s_tlo, tl + 2)
                    expert_steps(e, 20, 2, 4, hidT, 4, False, True)
                    transposes(None, 1, [xe[:, k * 128:(k + 1) * 128] for k in range(4, 8)], (s_tlo, tl + 2), CAP)
                    expert_steps(e, 22, 2, 5, hidT, 4, False, True)

                norm(l, 2, T_N2)
                pe.wait_ge(s_pin, l * 32 + 32)
                for t in range(NT):
                    transposes(None, t % 2, [prow[:, t, k * 128:(k + 1) * 128] for k in range(2)],
                               (s_tlo, l * TLL + lo_count(T_P + t - 2) + 2))
                pe.wait_ge(s_tlo, l * TLL + lo_count(T_P + 5) + 2)
                for c in range(2):
                    s = l * SPL + (S_P + 8 * c)
                    chunk(s, 512, lambda t: (s_ed, l * ADPL + (6 * (c - 1) + t + 1 + 6)))
                    branch_chunk(s + 4, lambda t: (s_ea, l * AAPL + (AA_P + c * 6 + t + 1 + 6)))


def unit(n):
    kind, t, h = ("A", "C")[n // 24], n % 24 // 4, n % 4
    a, b = TILE_GROUP[t]
    if kind == "C":
        a, b = max(a, t - 1), min(b, t + 2)
    return kind, t, h, a, b - a


_NAMES = ["x_prompt", "x_sample", "p_prompt", "p_sample", "norm_mix", "w_in", "qk_norm", "sink_logit", "conv_dw",
          "conv_dw_b", "conv_ln_g", "conv_ln_b", "gla_w2", "gla_b2", "gla_norm", "w_branch", "w_out", "norm_ffn",
          "w_router", "w_gate_e", "w_up_e", "w_down_e", "norm_ple", "w_ple_gate", "w_ple_proj", "norm_final"]


def kernel(**inputs):
    import concourse.bacc as bacc
    from concourse.bass_utils import run_bass_kernel_spmd

    nc = bacc.Bacc("TRN2", target_bir_lowering=False, num_devices=1)
    arrays, args = {}, []
    for name in _NAMES:
        a = np.asarray(inputs[name])
        if name == "conv_dw":
            a = a.transpose(0, 2, 1)
        arrays[f"in_{name}"] = np.ascontiguousarray(a)
    arrays["in_consts"] = shape_constants()
    for name, a in arrays.items():
        args.append(nc.dram_tensor(name, a.shape, mybir.dt.from_np(a.dtype), kind="ExternalInput").ap())
    for n, s in (("out_prompt", SEQ), ("out_sample", DEC)):
        args.append(nc.dram_tensor(n, [1, s, D], F32, kind="ExternalOutput").ap())
    build(nc, *args)
    r = run_bass_kernel_spmd(nc, [arrays], core_ids=[0])
    return r.results[0]["out_prompt"], r.results[0]["out_sample"]
```

```python
from contextlib import ExitStack

import concourse.bass as bass
from concourse import mybir
import numpy as np

F32 = mybir.dt.float32
F32R = mybir.dt.float32r
I32 = mybir.dt.int32
U32 = mybir.dt.uint32
ALU = mybir.AluOpType
ACT = mybir.ActivationFunctionType
AX = mybir.AxisListType

DEPTH, D, SEQ, DEC = 2, 1024, 512, 256
TOK = SEQ + DEC
NT = TOK // 128
GROUPS = [(0, SEQ // 128), (SEQ // 128, NT)]
TILE_GROUP = [GROUPS[0]] * (SEQ // 128) + [GROUPS[1]] * (DEC // 128)
KT = D // 128
HD = 64
EPS = 1e-6
UC = 2592
IN_COLS = UC + 4 * D
NCH = 6
CW = UC // NCH
NB = 4
NE, CAPP, CAPS = 16, 2 * SEQ // 16, 2 * DEC // 16
CAP = CAPP + CAPS
FF = 1024
PLE = 256
CONVW = 31
PAD = CONVW // 2
ZW = PAD + SEQ + PAD + DEC + PAD
AW = ZW - 2 * PAD

QA, KA, VA, UB, UG, QC, KC, VC, QD, KD, VD, RD, ZL = (
    0, 256, 384, 512, 768, 1024, 1280, 1408, 1536, 1792, 2048, 2304, 2560)

ES = 24
S_W, S_G, S_O, S_E = 0, 4 * NCH, 4 * NCH + 8, 4 * NCH + 16
S_P = S_E + ES * NE
SPL = S_P + 16
R_W, R_G, R_O, R_E, R_P = 0, 3, 4, 5, 5 + 16
LAND = (R_P + 2) * 16
RAW, SPLIT = 8, 4
NF, FRAW, FSPLIT = NB * D // 128, 3, 2
F_ROPE, F_Z, F_ATT, F_CONV, F_GLA, F_SCAN, F_GLB = 0, 6, 8, 17, 19, 25, 26

F_UNITS = [n for n in range(44) if n >= 16 or n % 2 == 0]

T_N0, T_G, T_N1 = 0, 12, 24
T_E = T_N1 + 12
T_P = T_E + 4 * NE + 2
T_N2 = T_P + 6
TPL = T_N2 + 12
C_O, C_P, CPL = 6, 8, 12
AA_P, AAPL = 36, 48
AD_P, ADPL = 12, 24

K_ID = 0
K_WM = 128
K_CUM = K_WM + 384
K_IND = K_CUM + 6 * 128
K_GM = K_IND + 2
K_RA = K_GM + 512
K_RC = K_RA + 2 * 4 * HD
K_N = K_RC + 2 * 4 * HD


def shape_constants():
    c = np.zeros((128, K_N), np.float32)
    i = np.arange(128)
    c[:, K_ID:K_ID + 128] = np.eye(128)
    c[:, K_WM:K_WM + 128] = np.where(i[None, :] >= i[:, None], 0, -1e30)
    c[:, K_WM + 256:K_WM + 384] = np.where(i[None, :] <= i[:, None], 0, -1e30)
    same = (i[:, None] // 64) == (i[None, :] // 64)
    j, q = i[:, None], i[None, :]
    jl = j % 64
    mats = [
        same & (j <= q), (same & (j <= q)) * 1 - (same & (jl <= 31)) * 1, same & (j > q),
        same & (j >= q), (same & (j >= q)) * 1 - (same & (jl >= 32)) * 1, same & (j < q),
    ]
    for n, m in enumerate(mats):
        c[:, K_CUM + n * 128:K_CUM + (n + 1) * 128] = np.asarray(m, np.float32) / 16
    c[:, K_IND] = (i < 64) / 16
    c[:, K_IND + 1] = (i >= 64) / 16
    for d in range(2):
        m = same & ((j <= q) if d == 0 else (j >= q))
        for p in range(2):
            c[:, K_GM + (2 * d + p) * 128:K_GM + (2 * d + p + 1) * 128] = m

    def tables(pos, dim):
        inv = np.float32(10000.0) ** (-np.arange(0, dim, 2, dtype=np.float32) / np.float32(dim))
        a = pos.astype(np.float32)[:, None] * inv[None, :]
        return np.cos(a), np.sin(a)

    s = np.arange(SEQ)
    rc, rs = tables(s // 64, 32)
    cc, cs = tables(s % 64, 32)
    tc, ts = tables(s, 64)
    ca = np.concatenate([rc, rc, cc, cc], 1)
    sa = np.concatenate([-rs, rs, -cs, cs], 1)
    cp = np.concatenate([tc, tc], 1)
    sp = np.concatenate([-ts, ts], 1)
    for n, m in enumerate([ca, sa, cp, sp]):
        c[:, K_RA + n * 256:K_RA + (n + 1) * 256] = m.reshape(4, 128, HD).transpose(1, 0, 2).reshape(128, 256)
    return c


def build(nc, x_p, x_s, p_p, p_s, norm_mix, w_in, qk_norm, sink, conv_w, conv_b, ln_g, ln_b, gla_w2, gla_b2,
          gla_norm, w_branch, w_out, norm_ffn, w_router, w_gate, w_up, w_down, norm_ple, w_pg, w_pp,
          norm_final, consts, y_p, y_s):
    ctx = ExitStack()
    with ctx:
        def sb(name, shape, dt=F32):
            return ctx.enter_context(nc.sbuf_tensor(name, shape, dt))

        def sem(name):
            return ctx.enter_context(nc.semaphore(name))

        x_d = nc.dram_tensor("x_res", [TOK, D], F32).ap()
        g_d = nc.dram_tensor("gate_logits", [NF, 128, TOK], F32).ap()
        h2_d = nc.dram_tensor("h2_rows", [TOK, D], F32).ap()

        cst = sb("cst", [128, K_N])
        ident = cst[:, K_ID:K_ID + 128]
        gqk = sb("gqk", [128, 6, HD])
        sink_b = sb("sink_b", [128, 4])
        cw = sb("cw", [128, 2, CONVW])
        cb = sb("cb", [128, 2])
        lng = sb("lng", [128, 256])
        lnb = sb("lnb", [128, 256])
        gng = sb("gng", [128, HD])
        w2b = sb("w2b", [33, 512])
        wr = sb("wr", [128, KT, NE])
        ms = sb("ms", [128, NT])
        rs = sb("rs", [128, NT])
        small = sb("small", [128, 64])
        nm = sb("nm", [128, 48])
        sm = sb("sm", [128, 48])
        sk = sb("sk", [128, 24])
        es = sb("es", [128, 24])
        rcp = sb("rcp", [128, 48])
        rqk = sb("rqk", [128, NT, 6])
        bns = sb("bns", [128, NT, 6])
        bnv = sb("bnv", [128, NT, 2])
        oss = sb("oss", [128, NT, 4])
        eps1, eps64 = sb("eps1", [128, 1]), sb("eps64", [128, 1])
        base = (nc.sbuf_base + 31) // 32 * 32
        R0 = base
        H0 = R0 + RAW * 4096
        U0 = H0 + 2 * KT * TOK * 4
        M0 = U0 + (NT * UC * 4 + 31) // 32 * 32
        MIX = 42752
        END = M0 + MIX + TOK * 4
        fence = sb("fence", [128, (END - base) // 4])
        assert nc.sbuf_base <= nc.sbuf_usable_end

        def at(name, shape, off, dt=F32):
            return nc.alloc_sbuf_tensor_at(name, shape, dt, offset=off)

        raw = [at(f"raw{i}", [128, 1024], R0 + i * 4096) for i in range(RAW)]
        raw += [at(f"raw{RAW + i}", [128, 1024], H0 + i * 4096) for i in range(12)]
        raw += [at(f"raw{RAW + 12 + i}", [128, 1024], M0 + 4 * 8192 + i * 4096) for i in range(3)]
        hT = [at(f"hT{n}", [128, KT, TOK], H0 + n * KT * TOK * 4, F32R) for n in range(2)]
        hTf = at("hTf", [128, KT, TOK], H0)
        merged = at("merged", [128, KT, TOK], H0 + KT * TOK * 4)
        u = at("u", [128, NT, UC], U0)
        rows = at("rows", [128, NT, D], U0)
        gain = at("gain", [128, D], U0 + NT * D * 4)
        gsig = at("gsig", [128, NT, 512], U0 + (NT * D + D) * 4)
        prow = at("prow", [128, NT, PLE], U0 + (NT * D + D + NT * 512) * 4)
        whi = [at(f"whi{n}", [128, 1024], M0 + n * 4096, F32R) for n in range(SPLIT)]
        wlo = [at(f"wlo{n}", [128, 1024], M0 + (SPLIT + n) * 4096, F32R) for n in range(SPLIT)]
        oT = [at(f"oT{n}", [128, 2, TOK], M0 + 4 * 8192 + n * 2 * TOK * 4, F32R) for n in range(2)]
        ur = at("ur", [128, NT, UC], U0, F32R)
        ublk = u[:, :, 0:2048].rearrange("p t (b h n) -> p t b h n", h=2, n=256)
        urblk = ur[:, :, 0:2048].rearrange("p t (b h n) -> p t b h n", h=2, n=256)
        gates0 = at("gates0", [128, NB, NT, 128], M0 + 4 * 8192)
        gates = (gates0, u[:, :, 2048:2560].rearrange("p t (i n) -> p i t n", n=128))
        gates_all = (gates0[:].rearrange("p i t n -> p (i t n)"), u[:, :, 2048:2560])
        fhi = [at(f"fhi{n}", [128, KT, 128], R0 + (4 + 2 * n) * 4096, F32R) for n in range(FSPLIT)]
        flo = [at(f"flo{n}", [128, KT, 128], R0 + (5 + 2 * n) * 4096, F32R) for n in range(FSPLIT)]
        fout = [raw[3][:, 0:TOK], at("fout1", [128, TOK], M0 + MIX)[:]]
        e_at = [U0 + (NT * D + D) * 4]

        def moe(name, shape, dt=F32):
            n = 4
            for v in shape[1:]:
                n *= v
            off = e_at[0]
            e_at[0] = (off + n + 31) // 32 * 32
            assert e_at[0] <= M0
            return at(name, shape, off, dt)

        xe = moe("xe", [CAP, D])
        xeT = [moe(f"xeT{n}", [128, KT, CAP], F32R) for n in range(2)]
        sil = moe("sil", [CAP, FF])
        hidT = [moe(f"hidT{n}", [128, KT, CAP], F32R) for n in range(2)]
        ye = moe("ye", [CAP, D])
        lg = moe("lg", [128, NT, NE])
        lmx = moe("lmx", [128, NT])
        lsm = moe("lsm", [128, NT])
        scores = moe("scores", [48, SEQ])
        top = moe("top", [48, CAPP])
        topi = moe("topi", [48, CAPP], U32)
        pick = moe("pick", [NE, 2, CAP])
        idxT = moe("idxT", [CAP, NE + 1], U32)
        gateT = moe("gateT", [CAP, NE])
        idx_g = moe("idx_g", [CAP, 1], U32)
        idx_s = moe("idx_s", [CAP, 1], U32)
        raw += [moe(f"raw{ES - 1}", [128, 1024])]
        m_at = [M0]

        def mix(name, shape):
            n = 4
            for v in shape[1:]:
                n *= v
            off = m_at[0]
            m_at[0] = (off + n + 31) // 32 * 32
            assert m_at[0] <= M0 + MIX, name
            return at(name, shape, off)

        qkA = mix("qkA", [128, 3, TOK])
        qkC = mix("qkC", [128, 3, TOK])
        s1 = mix("s1", [128, 384])
        s2 = mix("s2", [128, 384])
        at_z = m_at[0]
        zsg = mix("zsg", [128, 2, 256])
        zn = mix("zn", [128, 2, 256])
        zr = mix("zr", [128, 2, 256])
        m_at[0] = at_z
        P = mix("P", [128, 2, 512])
        PT = mix("PT", [128, 2, 512])
        at_r = m_at[0]
        zT = mix("zT", [128, 2, ZW])
        zacc = mix("zacc", [128, 2, AW])
        m_at[0] = at_r
        rA = mix("rA", [128, 2, 384])
        rC = mix("rC", [128, 2, 384])
        s3 = mix("s3", [128, 384])
        c1 = mix("c1", [128, 384])
        c2 = mix("c2", [128, 384])
        sC = s1, s2
        m_at[0] = M0
        la = mix("la", [128, NT, 512])
        kvs = mix("kvs", [128, 2 * NT, 4, HD])
        E3 = mix("E3", [128, 3, 512])
        TT = mix("TT", [128, 3, 512])
        att = mix("att", [128, 2, 512])
        dec = mix("dec", [128, NT, 8])
        zlT = mix("zlT", [33, 128])
        osq = mix("osq", [128, 256])

        PS = ctx.enter_context(nc.psum_tensor("PS", [128, 8, 512], F32))

        s_cst = sem("s_cst")
        s_raw = [sem(f"s_raw{i}") for i in range(ES)]
        s_hi = sem("s_hi")
        s_lo = sem("s_lo")
        s_used = sem("s_used")
        s_xin = [sem(f"s_xin{i}") for i in range(NT)]
        s_gain = sem("s_gain")
        s_small = sem("s_small")
        s_smallx = sem("s_smallx")
        s_sq = sem("s_sq")
        s_eps = sem("s_eps")
        s_ssq, s_rqk = sem("s_ssq"), sem("s_rqk")
        s_bn, s_bnr = sem("s_bn"), sem("s_bnr")
        s_oss, s_or = sem("s_oss"), sem("s_or")
        s_xn = sem("s_xn")
        s_tp = sem("s_tp")
        s_thi = sem("s_thi")
        s_tlo = sem("s_tlo")
        s_acc = sem("s_acc")
        s_ea = sem("s_ea")
        s_ed = sem("s_ed")
        s_xst = [sem(f"s_xst{i}") for i in range(NT)]
        s_rA, s_rC = sem("s_rA"), sem("s_rC")
        s_tA, s_tC = sem("s_tA"), sem("s_tC")
        s_qA, s_qC = sem("s_qA"), sem("s_qC")
        s_sc = sem("s_sc")
        s_nm = sem("s_nm")
        s_p = sem("s_p")
        s_pt = sem("s_pt")
        s_ptA, s_ptC = sem("s_ptA"), sem("s_ptC")
        s_pv = sem("s_pv")
        s_sk = sem("s_sk")
        s_es = sem("s_es")
        s_o = sem("s_o")
        s_zpad = sem("s_zpad")
        s_zs = sem("s_zs")
        s_zr = sem("s_zr")
        s_zt = sem("s_zt")
        s_zT = sem("s_zT")
        s_conv = sem("s_conv")
        s_zb = sem("s_zb")
        s_zn = sem("s_zn")
        s_ob = sem("s_ob")
        s_az = sem("s_az")
        s_g = [sem(f"s_g{i}") for i in range(11)]
        s_scan = sem("s_scan")
        s_h = [sem(f"s_h{i}") for i in range(11)]
        s_od = sem("s_od")
        s_fraw = [sem(f"s_fraw{i}") for i in range(FRAW)]
        s_fhi = sem("s_fhi")
        s_flo = sem("s_flo")
        s_fused = sem("s_fused")
        s_fev = sem("s_fev")
        s_fout = [sem(f"s_fout{i}") for i in range(2)]
        s_gl = [sem(f"s_gl{i}") for i in range(2)]
        s_sg = sem("s_sg")
        s_br = [sem(f"s_br{i}") for i in range(NB - 1)]
        s_gm = [sem(f"s_gm{i}") for i in range(NB)]
        s_mg = sem("s_mg")
        s_mh, s_ml = sem("s_mh"), sem("s_ml")
        s_h2 = [sem(f"s_h2{i}") for i in range(2)]
        s_rt = sem("s_rt")
        s_lm = sem("s_lm")
        s_le = sem("s_le")
        s_af = sem("s_af")
        s_aft = sem("s_aft")
        s_scz = sem("s_scz")
        s_pick = sem("s_pick")
        s_pickt = sem("s_pickt")
        s_idx = sem("s_idx")
        s_ga = sem("s_ga")
        s_sil = sem("s_sil")
        s_hid = sem("s_hid")
        s_y = sem("s_y")
        s_sca = sem("s_sca")
        s_pin = sem("s_pin")
        s_yo = sem("s_yo")

        w_in_f = w_in.rearrange("l k n -> (l k) n")
        w_br_f = w_branch.rearrange("l b k n -> (l b k) n")
        w_out_f = w_out.rearrange("l k n -> (l k) n")
        wg_f = w_gate.rearrange("l e k n -> (l e k) n")
        wu_f = w_up.rearrange("l e k n -> (l e k) n")
        wd_f = w_down.rearrange("l e k n -> (l e k) n")
        wpg_f = w_pg.rearrange("l k n -> (l k) n")
        wpp_f = w_pp.rearrange("l k n -> (l k) n")
        block = ctx.enter_context(nc.Block())

        def cols(tile, nk, n):
            return tile[:, 0:nk * n].rearrange("p (k n) -> p k n", n=n)

        def lo_count(j):
            return j + 1 if j < T_N1 else j + 1 - 12
        TLL = TPL - 12

        def gate_bank(f):
            return 4 if 0 < f < F_Z else 6

        def pt_done(l, m):
            return (s_ptA, l * 24 + m + 1) if m < 24 else (s_ptC, l * 24 + m - 24 + 1)

        def wait_alone(eng, sem_, value):
            value = eng.to_reg(value)
            eng.wait_ge(s_cst, 16)
            eng.wait_ge(sem_, value)

        def accumulated(eng, chunks, step_, t):
            if t < NT - 1:
                eng.wait_ge(s_acc, chunks * (NT - 1) + (t + 1))
            else:
                eng.wait_ge(s_used, step_ + (1 + SPLIT))

        @block.sync
        def _(sp):
            sp.dma_start(cst[:], consts).then_inc(s_cst, 16)
            def fetch(j, src, r0, nk, c0, n):
                sp.dma_start(cols(raw[j], nk, n),
                             src[bass.ds(r0, nk * 128), :][:, bass.ds(c0, n)].rearrange("(k p) n -> p k n", p=128)
                             ).then_inc(s_raw[j], 16)

            def load(step, j, src, r0, nk, c0, n):
                sp.wait_ge(s_lo, step + 1)
                fetch(j % RAW, src, r0, nk, c0, n)

            for t in range(2):
                sp.wait_ge(s_xin[t], 16)
            with sp.Fori(0, DEPTH) as l:
                with sp.Fori(0, NCH // 2) as i:
                    for j in range(8):
                        load(l * SPL + i * 8 + j, j, w_in_f, l * D + (j % 4) * 256, 2,
                             i * (2 * CW) + (j // 4) * CW, CW)
                def load_gate(f):
                    if f < FRAW:
                        sp.wait_ge(s_lo, l * SPL + (S_G + RAW))
                    else:
                        sp.wait_ge(s_flo, l * NF + (f - FRAW + 1))
                    sp.dma_start(raw[f % FRAW][:].rearrange("p (k n) -> p k n", n=128),
                                 w_in_f[bass.ds(l * D, D), UC + f % NB * D + f // NB * 128:UC + f % NB * D + f // NB * 128 + 128]
                                 .rearrange("(k p) n -> p k n", p=128)).then_inc(s_fraw[f % FRAW], 16)

                for f in range(FRAW):
                    load_gate(f)
                for f in range(NF):
                    if f + FRAW < NF:
                        load_gate(f + FRAW)
                    sp.wait_ge(s_fev, l * NF + f + 2)
                    sp.dma_start(g_d[f], fout[f % 2]).then_inc(s_fout[f % 2], 16)
                wait_alone(sp, s_flo, l * NF + NF)
                wait_alone(sp, s_fused, l * NF + NF + FSPLIT)
                for n in range(2):
                    wait_alone(sp, s_fout[n], l * (8 * NF) + 8 * NF)
                for g in range(8):
                    sp.wait_ge(s_lo, l * SPL + (S_G + g + 1))
                    sp.dma_start(raw[g][:].rearrange("p (k n) -> p k n", n=128),
                                 w_br_f[bass.ds(l * (NB * 256), NB * 256), g * 128:(g + 1) * 128]
                                 .rearrange("(k p) n -> p k n", p=128)).then_inc(s_raw[g], 16)
                for g in range(10):
                    if g < 8:
                        if g < 2:
                            sp.wait_ge(s_od, l + 1)
                        else:
                            sp.wait_ge(s_mg, l * 8 + (g - 1))
                        for i in range(NB):
                            sp.dma_start(gates[g % 2][:, i], g_d[g * NB + i].rearrange("p (t n) -> p t n", n=128)
                                         ).then_inc(s_gl[g % 2], 16)
                    if g >= 2:
                        j = g - 2
                        load(l * SPL + (S_O + j), j, w_out_f, l * D + (j % 4) * 256, 2, (j // 4) * 512, 512)
                def expert(e, s):
                    if s < 16:
                        fetch(s, (wg_f, wu_f)[s // 4 % 2], l * (NE * D) + e * D + s % 4 * 256, 2, s // 8 * 512, 512)
                    else:
                        j = s - 16
                        fetch(s, wd_f, l * (NE * FF) + e * FF + (j // 4 * 512 + j % 2 * 256), 2, j // 2 % 2 * 512, 512)

                for s in range(ES):
                    if s < RAW:
                        sp.wait_ge(s_lo, l * SPL + (S_E + s + 1))
                    elif s < RAW + 12:
                        sp.wait_ge(s_rt, l + 1)
                    expert(0, s)
                with sp.Fori(0, NE - 1) as e:
                    for s in range(ES):
                        sp.wait_ge(s_lo, l * SPL + e * ES + (S_E + s + 1 + RAW))
                        expert(e + 1, s)
                for c in range(2):
                    for j in range(4):
                        load(l * SPL + (S_P + 8 * c + j), j, wpg_f, l * D + j * 256, 2, c * 512, 512)
                    for j in range(4):
                        load(l * SPL + (S_P + 8 * c + 4 + j), 4 + j, wpp_f, l * PLE + (j % 2) * 128, 1,
                             c * 512 + (j // 2) * 256, 256)
            for t in range(NT):
                sp.wait_ge(s_xn, DEPTH * 18 + t + 1)
                dst = y_p[0, t * 128:(t + 1) * 128, :] if t < 4 else y_s[0, (t - 4) * 128:(t - 3) * 128, :]
                sp.dma_start(dst, rows[:, t, :]).then_inc(s_yo, 16)
            sp.wait_ge(s_yo, 16 * NT)

        @block.gpsimd
        def _(pool):
            def wait(s, value):
                if isinstance(value, int):
                    pool.wait_ge(s, value)
                else:
                    wait_alone(pool, s, value)

            for t in range(NT):
                src = x_p[0, t * 128:(t + 1) * 128, :] if t < 4 else x_s[0, (t - 4) * 128:(t - 3) * 128, :]
                pool.dma_start(rows[:, t, :], src).then_inc(s_xin[t], 16)
            pool.wait_ge(s_cst, 16)

            def load_gain(row):
                pool.dma_start(gain[:], row.broadcast_to([128, D])).then_inc(s_gain, 16)

            def load_x():
                for t in range(NT):
                    pool.dma_start(rows[:, t, :], x_d[t * 128:(t + 1) * 128, :]).then_inc(s_xin[t], 16)

            def store_x(ed):
                for t in range(NT):
                    wait(s_ed, ed + (t + 1))
                    pool.dma_start(x_d[t * 128:(t + 1) * 128, :], rows[:, t, :]).then_inc(s_xst[t], 16)

            def stored(n):
                for t in range(NT):
                    wait(s_xst[t], n * 16)

            nc.gpsimd.memset(w2b[:], 0.0)
            nc.gpsimd.memset(eps1[:], EPS)
            nc.gpsimd.memset(eps64[:], HD * EPS)
            pool.drain().then_inc(s_eps, 1)
            wait(s_cst, 16)
            for t in range(NT):
                wait(s_xin[t], 16)
                pool.dma_start(x_d[t * 128:(t + 1) * 128, :], rows[:, t, :]).then_inc(s_xst[t], 16)
            with pool.Fori(0, DEPTH) as l:
                load_gain(norm_mix[bass.ds(l, 1), :])
                for k in range(2):
                    src = qk_norm.rearrange("l k d -> l (k d)")[bass.ds(l, 1), k * HD:(k + 1) * HD]
                    for h in ((0, 1, 2, 3) if k == 0 else (4, 5)):
                        pool.dma_start(gqk[:, h, :], src.broadcast_to([128, HD])).then_inc(s_small, 16)
                pool.dma_start(sink_b[:], sink[bass.ds(l, 1), :].broadcast_to([128, 4])).then_inc(s_small, 16)
                pool.dma_start(cw[:], conv_w.rearrange("l c w -> (l c) w")[bass.ds(l * 256, 256), :]
                               .rearrange("(h p) w -> p h w", p=128)).then_inc(s_small, 16)
                pool.dma_start(cb[:], conv_b.rearrange("l (c o) -> (l c) o", o=1)[bass.ds(l * 256, 256), :]
                               .rearrange("(h p) o -> p (h o)", p=128), allow_slow_non_contiguous=True).then_inc(s_small, 16)
                pool.dma_start(lng[:], ln_g[bass.ds(l, 1), :].broadcast_to([128, 256])).then_inc(s_small, 16)
                pool.dma_start(lnb[:], ln_b[bass.ds(l, 1), :].broadcast_to([128, 256])).then_inc(s_small, 16)
                pool.dma_start(gng[:], gla_norm[bass.ds(l, 1), :].broadcast_to([128, HD])).then_inc(s_small, 16)
                for n in range(2):
                    pool.dma_start(w2b[16 * n:16 * n + 16, 256 * n:256 * n + 256],
                                   gla_w2.rearrange("l n r c -> (l n r) c")[bass.ds(l * 32 + n * 16, 16), :]
                                   ).then_inc(s_small, 16)
                pool.dma_start(w2b[32:33, :], gla_b2.rearrange("l n c -> l (n c)")[bass.ds(l, 1), :]).then_inc(s_small, 16)
                pool.dma_start(wr[:], w_router.rearrange("l k n -> (l k) n")[bass.ds(l * D, D), :]
                               .rearrange("(k p) n -> p k n", p=128)).then_inc(s_small, 16)
                NSM = 16 * 16
                wait(s_small, l * NSM + NSM)
                nc.gpsimd.tensor_scalar(gqk[:, 4:6, :], gqk[:, 4:6, :], 8.0, None, ALU.mult)
                nc.gpsimd.tensor_scalar(gng[:], gng[:], 8.0, None, ALU.mult).then_inc(s_smallx, 1)

                wait(s_ea, l * AAPL + 36 + 6)
                for t in range(NT):
                    pt = t - TILE_GROUP[t][0]
                    cs_ = cst[:, K_RC + pt * HD:K_RC + (pt + 1) * HD]
                    sn_ = cst[:, K_RC + 256 + pt * HD:K_RC + 256 + (pt + 1) * HD]
                    x = u[:, t, QC:QC + 384].rearrange("p (h d) -> p h d", d=HD)
                    a = c1[:].rearrange("p (h d) -> p h d", d=HD)
                    b = c2[:].rearrange("p (h d) -> p h d", d=HD)
                    nc.gpsimd.tensor_tensor(a, x, cs_.unsqueeze(1).broadcast_to([128, 6, HD]), ALU.mult)
                    for hf in range(2):
                        o, i_ = 32 * hf, 32 * (1 - hf)
                        nc.gpsimd.tensor_tensor(b[:, :, o:o + 32], x[:, :, i_:i_ + 32],
                                                sn_[:, o:o + 32].unsqueeze(1).broadcast_to([128, 6, 32]), ALU.mult)
                    pool.drain()
                    if t >= 2:
                        wait(s_tC, l * NT + t - 1)
                    r = rC[:, t % 2, :]
                    nc.gpsimd.tensor_tensor(r[:, 0:256].rearrange("p (a g d) -> p g a d", g=2, d=HD),
                                            c1[:, 0:256].rearrange("p (g a d) -> p g a d", g=2, d=HD),
                                            c2[:, 0:256].rearrange("p (g a d) -> p g a d", g=2, d=HD), ALU.add)
                    nc.gpsimd.tensor_tensor(r[:, 256:384], c1[:, 256:384], c2[:, 256:384], ALU.add)
                    pool.drain().then_inc(s_rC, 1)

                wait(s_tA, l * NT + NT)
                wait(s_tC, l * NT + NT)
                nc.gpsimd.memset(zT[:], 0.0).then_inc(s_zpad, 1)
                wait(s_ob, l * NT + NT)
                nc.gpsimd.memset(att[:], 0.0)
                pool.drain()
                nc.gpsimd.memset(zlT[32:33, :], 1.0)
                pool.drain().then_inc(s_az, 1)
                for g in range(8):
                    for i in range(NB):
                        wait(s_gm[i], l * 8 + g + 1)
                    G = gates[g % 2]
                    for i in range(2):
                        nc.gpsimd.tensor_tensor(G[:, 2 * i], G[:, 2 * i], G[:, 2 * i + 1], ALU.add)
                    pool.drain()
                    nc.gpsimd.tensor_tensor(merged[:, g, :].rearrange("p (t n) -> p t n", n=128), G[:, 0], G[:, 2],
                                            ALU.add).then_inc(s_mg, 1)

                wait(s_mg, l * 8 + 8)
                wait(s_used, l * SPL + (S_O + SPLIT))
                stored(l * 2 + 1)
                load_gain(norm_ffn[bass.ds(l, 1), :])
                load_x()
                store_x(l * ADPL + 6 + 6)
                stored(l * 2 + 2)

                wait(s_xn, l * 18 + 12)
                nc.gpsimd.memset(scores[:], -1.0).then_inc(s_scz, 1)
                for n in range(2):
                    wait(s_h2[n], l * 48 + 48)
                wait(s_idx, l + 1)
                nc.gpsimd.tensor_copy(idx_g[:], idxT[:, 0:1])
                pool.drain()
                pool.indirect_dma_start(out=xe[:], out_offset=None, in_=h2_d,
                                        in_offset=bass.IndirectOffsetOnAxis(ap=idx_g[:, 0:1], axis=0)).then_inc(s_ga, 16)
                with pool.Fori(0, NE) as e:
                    nc.gpsimd.tensor_copy(idx_s[:], idxT[:, bass.ds(e, 1)])
                    wait(s_tp, l * TPL + e * 4 + (T_E + 2))
                    wait(s_ga, l * (17 * 16) + e * 16 + 16)
                    nc.gpsimd.tensor_copy(idx_g[:], idxT[:, bass.ds(e + 1, 1)])
                    pool.drain()
                    pool.indirect_dma_start(out=xe[:], out_offset=None, in_=h2_d,
                                            in_offset=bass.IndirectOffsetOnAxis(ap=idx_g[:, 0:1], axis=0)
                                            ).then_inc(s_ga, 16)
                    wait(s_y, l * 32 + e * 2 + 2)
                    pool.indirect_dma_start(out=x_d, out_offset=bass.IndirectOffsetOnAxis(ap=idx_s[:, 0:1], axis=0),
                                            in_=ye[:], in_offset=None, compute_op=ALU.add).then_inc(s_sca, 16)
                    wait(s_sca, l * 256 + e * 16 + 16)

                wait(s_used, l * SPL + S_P + 2)
                for n, (src, t0, nt) in enumerate(((p_p, 0, 4), (p_s, 4, 2))):
                    pool.dma_start(prow[:, t0:t0 + nt, :],
                                   src.rearrange("l a s d -> (l a s) d")[bass.ds(l * (nt * 128), nt * 128), :]
                                   .rearrange("(t p) d -> p t d", p=128)).then_inc(s_pin, 16)
                load_gain(norm_ple[bass.ds(l, 1), :])
                load_x()
                wait(s_tp, l * TPL + (T_N2 + 12))
                load_x()
                store_x(l * ADPL + AD_P + 6 + 6)
            load_gain(norm_final.rearrange("(a d) -> a d", a=1))

        @block.scalar
        def _(act):
            A = nc.scalar.activation
            act.drain().then_inc(s_thi, 2)
            act.drain().then_inc(s_ea, 6)
            act.drain().then_inc(s_fev, 1)
            act.wait_ge(s_eps, 1)

            def hi_part(step, slot, w, landed):
                act.wait_ge(s_raw[slot], landed)
                act.wait_ge(s_used, step + 1)
                A(whi[slot % SPLIT][:, 0:w], raw[slot][:, 0:w], ACT.Copy).then_inc(s_hi, 1)

            def hi(step, j, w, rounds):
                hi_part(step, j % RAW, w, l * LAND + ((rounds + j // RAW) * 16 + 16))

            def gate_hi(l, f):
                act.wait_ge(s_fraw[f % FRAW], l * (16 * len(range(f % FRAW, NF, FRAW))) + (f // FRAW * 16 + 16))
                act.wait_ge(s_fused, l * NF + f + 1)
                A(fhi[f % FSPLIT][:], raw[f % FRAW][:].rearrange("p (k n) -> p k n", n=128), ACT.Copy).then_inc(s_fhi, 1)

            def gate_out(l, f):
                act.wait_ge(s_fused, l * NF + (f + 1 + FSPLIT))
                if f >= 2:
                    act.wait_ge(s_fout[f % 2], l * (8 * NF) + f // 2 * 16)
                b = gate_bank(f)
                A(fout[f % 2], PS[:, b:b + 2, :].rearrange("p a n -> p (a n)")[:, 0:TOK], ACT.Copy).then_inc(s_fev, 1)

            def mean_square(x, ed, t):
                act.wait_ge(s_xin[t], x * 16)
                act.wait_ge(s_ed, ed + max(t, 1) + 1)
                A(PS[:, 0:2, :], rows[:, t, :].rearrange("p (a n) -> p a n", a=2), ACT.Square, scale=1.0 / 32,
                  accum_out=ms[:, t:t + 1])
                act.drain()
                A(ms[:, t:t + 1], ms[:, t:t + 1], ACT.Sqrt, bias=eps1[:]).then_inc(s_sq, 1)

            def t_hi(j, dst, src):
                act.wait_ge(s_tp, j + 1)
                A(dst, src, ACT.Copy).then_inc(s_thi, 1)

            def tbank(j, n=4, w=128):
                return PS[:, 6 + j % 2, 0:n * w].rearrange("p (k n) -> p k n", n=w)

            def norm(l, n, j0, dst):
                x, ed = ((l * 3 + 1, l * ADPL), (l * 3 + 2, l * ADPL + (6 + 6)), (l * 3 + 3, l * ADPL + (6 + 6)))[n]
                mean_square(x, ed, 0)
                mean_square(x, ed, 1)
                for t in range(NT):
                    if t + 2 < NT:
                        mean_square(x, ed, t + 2)
                    for c in range(2):
                        t_hi(l * TPL + (j0 + 2 * t + c), dst[:, 4 * c:4 * c + 4, t * 128:(t + 1) * 128], tbank(c))

            with act.Fori(0, DEPTH) as l:
                norm(l, 0, T_N0, hT[0])

                def u_out(ck, t):
                    accumulated(act, l * CPL + ck, l * SPL + ck * 4 + 3, t)
                    A(u[:, t, bass.ds(ck * CW, CW)], PS[:, t, 0:CW], ACT.Copy).then_inc(s_ea, 1)

                def hi_w(ck, j, n):
                    hi_part(l * SPL + ck * 4 + n, (j + n) % RAW, 2 * CW,
                            l * LAND + (ck - j // 4) * 8 + ((j + n) // RAW * 16 + 16))

                def w_chunk(ck, j, ahead):
                    for n in range(3 if ahead else 0):
                        hi_w(ck, j, 4 + n)
                    for t in range(NT):
                        u_out(ck, t)
                    if ahead:
                        hi_w(ck, j, 7)

                for n in range(4):
                    hi(l * SPL + n, n, 2 * CW, R_W)
                with act.Fori(0, 2) as i:
                    for j in range(2):
                        w_chunk(i * 2 + j, 4 * j, True)
                w_chunk(4, 0, True)
                act.wait_ge(s_lo, l * SPL + (S_G + RAW))
                gate_hi(l, 0)
                w_chunk(5, 4, False)

                act.wait_ge(s_ssq, l + 1)
                A(rqk[:], rqk[:], ACT.Sqrt, bias=eps64[:]).then_inc(s_rqk, 1)
                for t in range(NT):
                    gate_hi(l, t + 1)
                    gate_out(l, t)
                    act.wait_ge(s_tA, l * NT + t + 1)
                    A(qkA[:, :, t * 128:(t + 1) * 128], PS[:, 6, 0:384].rearrange("p (k n) -> p k n", n=128),
                      ACT.Copy).then_inc(s_qA, 1)
                    act.wait_ge(s_tC, l * NT + t + 1)
                    A(qkC[:, :, t * 128:(t + 1) * 128], PS[:, 7, 0:384].rearrange("p (k n) -> p k n", n=128),
                      ACT.Copy).then_inc(s_qC, 1)
                act.wait_ge(s_zpad, l + 1)
                for t in range(NT + 1):
                    if t < NT:
                        if t >= 2:
                            act.wait_ge(s_zr, l * NT + t - 1)
                        A(zsg[:, t % 2, :], u[:, t, UG:UG + 256], ACT.Sigmoid).then_inc(s_zs, 1)
                    if t >= 1:
                        m = t - 1
                        act.wait_ge(s_zt, l * NT + m + 1)
                        z0 = PAD + m * 128 + (PAD if m >= 4 else 0)
                        A(zT[:, :, z0:z0 + 128], PS[:, m % 2, 0:256].rearrange("p (c n) -> p c n", c=2),
                          ACT.Copy).then_inc(s_zT, 1)
                    if t in (2, 4):
                        gate_hi(l, F_Z + t // 2)
                    if t in (3, 5):
                        gate_out(l, F_Z + t // 2 - 1)
                for n in range(49):
                    if n - 1 in F_UNITS and F_UNITS.index(n - 1) % 4 == 3:
                        gate_out(l, F_ATT + F_UNITS.index(n - 1) // 4)
                    if n < 48:
                        kind, t, h, k0, nk = unit(n)
                        act.wait_ge(s_nm, l * 48 + n + 1)
                        if n >= 2:
                            act.wait_ge(s_pt, l * 48 + n - 1)
                        src = PS[:, n % 2, 0:nk * 128] if kind == "A" else sC[n % 2][:, 0:nk * 128]
                        A(P[:, n % 2, 0:nk * 128], src, ACT.Exp, bias=nm[:, n:n + 1],
                          accum_out=sm[:, n:n + 1]).then_inc(s_p, 1)
                        if n in F_UNITS and F_UNITS.index(n) % 4 == 0:
                            gate_hi(l, F_ATT + F_UNITS.index(n) // 4 + 1)
                    if n >= 1 and unit(n - 1)[0] == "C":
                        m = n - 1
                        kind, t, h, k0, nk = unit(m)
                        act.wait_ge(s_pt, l * 48 + m + 1)
                        act.wait_ge(s_pv, l * 48 + m - 1)
                        A(PT[:, m % 2, 0:nk * 128], PS[:, 2 + m % 2, 0:nk * 128], ACT.Copy).then_inc(s_ptC, 1)
                        if h == 3:
                            act.wait_ge(s_sk, l * NT + t + 1)
                            A(es[:, 4 * t:4 * t + 4], sk[:, 4 * t:4 * t + 4], ACT.Exp).then_inc(s_es, 1)

                gate_hi(l, F_CONV + 1)
                act.wait_ge(s_bn, l + 1)
                A(bnv[:, :, 1], bnv[:, :, 1], ACT.Sqrt, bias=eps1[:]).then_inc(s_bnr, 1)
                for t in range(NT):
                    act.wait_ge(s_zn, l * NT + t + 1)
                    A(u[:, t, UB:UB + 256], zn[:, t % 2, :], ACT.Silu).then_inc(s_ob, 1)
                    if t == 1:
                        gate_out(l, F_CONV)
                        gate_hi(l, F_GLA)
                gate_out(l, F_CONV + 1)
                A(u[:, :, RD:RD + 256], u[:, :, RD:RD + 256], ACT.Silu)
                act.drain().then_inc(s_g[10], 1)

                act.wait_ge(s_az, l + 1)
                for n in range(NT + 1):
                    buf = (E3 if n % 2 == 0 else TT)
                    old = (TT if n % 2 == 0 else E3)
                    if n < NT:
                        act.wait_ge(s_g[0], l * NT + n + 1)
                        A(zlT[0:32, :], PS[0:32, 0, 0:128], ACT.Copy).then_inc(s_g[1], 1)
                    if n >= 1:
                        act.wait_ge(s_g[5], l * NT + n)
                        A(old[:, 1, :], PS[:, 2, :], ACT.Exp)
                        A(dec[:, n - 1, :], PS[:, 3, 0:8], ACT.Exp)
                        act.drain().then_inc(s_g[6], 1)
                    if n < NT:
                        act.wait_ge(s_g[2], l * NT + n + 1)
                        A(buf[:, 0, :], PS[:, 1, :], ACT.Abs)
                        act.drain()
                        A(buf[:, 0, :], buf[:, 0, :], ACT.Exp, scale=-1.0)
                        act.drain()
                        A(buf[:, 0, :], buf[:, 0, :], ACT.Ln, bias=1.0).then_inc(s_g[3], 1)
                        gate_hi(l, F_GLA + n + 1)
                        gate_out(l, F_GLA + n)
                gate_hi(l, F_GLB)
                gate_out(l, F_SCAN)
                act.wait_ge(s_scan, l + 1)
                for t in range(NT):
                    act.wait_ge(s_h[0], l * NT + t + 1)
                    A(E3[:, 0, :], PS[:, 0, :], ACT.Exp)
                    A(E3[:, 1, :], PS[:, 0, :], ACT.Exp, scale=-1.0)
                    A(E3[:, 2, :], PS[:, 1, :], ACT.Exp)
                    act.drain().then_inc(s_h[1], 1)
                    if t < NT - 1:
                        gate_hi(l, F_GLB + t + 1)
                    gate_out(l, F_GLB + t)
                    act.wait_ge(s_h[3], l * NT + t + 1)
                    A(TT[:, 0, :], PS[:, 2, :], ACT.Copy)
                    A(TT[:, 1, :], PS[:, 3, :], ACT.Copy)
                    act.drain().then_inc(s_h[4], 1)

                act.wait_ge(s_oss, l + 1)
                A(oss[:], oss[:], ACT.Sqrt, bias=eps64[:]).then_inc(s_or, 1)
                for c in range(2):
                    if c == 1:
                        act.wait_ge(s_od, l + 1)
                        for n in range(4):
                            hi(l * SPL + (S_G + n), n, 1024, R_G)
                    for t in range(NT):
                        t_hi(l * TPL + (T_G + 6 * c + t), urblk[:, t, 2 * c:2 * c + 2, 1, :],
                             PS[:, 6 + t % 2, :].rearrange("p (k n) -> p k n", n=256))
                for g in range(9):
                    if g < 8:
                        act.wait_ge(s_gl[g % 2], l * 256 + (g // 2 * 64 + 64))
                        A(gates_all[g % 2], gates_all[g % 2], ACT.Sigmoid).then_inc(s_sg, 1)
                    if g >= 1:
                        hi(l * SPL + (S_G + g + 3), g + 3, 1024, R_G)
                        act.wait_ge(s_mg, l * 8 + g)
                        A(hT[0][:, g - 1, :], merged[:, g - 1, :], ACT.Copy).then_inc(s_mh, 1)
                for j in range(4, 12):
                    hi(l * SPL + (S_O + j), j, 1024, R_O)

                x, ed = l * 3 + 2, l * ADPL + (6 + 6)
                mean_square(x, ed, 0)
                mean_square(x, ed, 1)
                for t in range(NT):
                    if t + 2 < NT:
                        mean_square(x, ed, t + 2)
                    for c in range(2):
                        t_hi(l * TPL + (T_N1 + 2 * t + c), hTf[:, 4 * c:4 * c + 4, t * 128:(t + 1) * 128], tbank(c))
                    act.dma_start(h2_d[t * 128:(t + 1) * 128, :], rows[:, t, :]).then_inc(s_h2[t % 2], 16)
                act.wait_ge(s_lm, l + 1)
                A(lg[:], lg[:], ACT.Exp).then_inc(s_le, 1)
                for c in range(2):
                    t_hi(l * TPL + (T_E + c), xeT[0][:, 4 * c:4 * c + 4, :], tbank(c, 4, CAP))
                with act.Fori(0, NE) as e:
                    for s in range(ES):
                        done = l * SPL + e * ES + (S_E + s + 1 + SPLIT)
                        j = l * TPL + e * 4 + (T_E + 2)
                        if s in (3, 11):
                            c = s // 8
                            act.wait_ge(s_used, done)
                            A(sil[:, c * 512:(c + 1) * 512], PS[0:CAP, c, :], ACT.Silu).then_inc(s_sil, 1)
                        if s == 11:
                            t_hi(j, hidT[0][:, 0:4, :], tbank(0, 4, CAP))
                        if s == 17:
                            t_hi(j + 1, hidT[0][:, 4:8, :], tbank(1, 4, CAP))
                        if s == 19:
                            t_hi(j + 2, xeT[0][:, 0:4, :], tbank(0, 4, CAP))
                        if s == 21:
                            t_hi(j + 3, xeT[0][:, 4:8, :], tbank(1, 4, CAP))
                        if s in (21, 23):
                            c = (s - 21) // 2
                            wait_alone(act, s_used, done)
                            A(ye[:, c * 512:(c + 1) * 512], PS[0:CAP, 4 + c, :], ACT.Copy,
                              scale=gateT[:, bass.ds(e, 1)]).then_inc(s_y, 1)
                        n = (s + 4) % ES
                        hi_part(l * SPL + e * ES + (S_E + s + 4), n, 1024,
                                (l * LAND + e * 16 + (R_E * 16 + 16 + (s + 4) // ES * 16)) if n < RAW else
                                (l * (16 * NE) + e * 16 + 16))

                for t in range(NT):
                    t_hi(l * TPL + (T_P + t), oT[0][:, :, t * 128:(t + 1) * 128], tbank(t, 2))
                norm(l, 2, T_N2, hT[0])
                for c in range(2):
                    s = l * SPL + (S_P + 8 * c)
                    for n in range(4, 7):
                        hi(s + n, 8 * c + n, 256, R_P)
                    for t in range(NT):
                        accumulated(act, l * CPL + (C_P + 2 * c), s + 3, t)
                        if c == 1:
                            act.wait_ge(s_ed, l * ADPL + (AD_P + t + 1) + 6)
                        A(gsig[:, t, :], PS[:, t, :], ACT.Sigmoid).then_inc(s_ea, 1)
                    hi(s + 7, 8 * c + 7, 256, R_P)
                    if c == 0:
                        for n in range(8, 12):
                            hi(s + n, 8 * c + n, 1024, R_P)
            for t in range(NT):
                mean_square(DEPTH * 3 + 1, DEPTH * ADPL, t)

        @block.vector
        def _(dve):
            V = nc.vector
            dve.drain().then_inc(s_lo, RAW)
            dve.drain().then_inc(s_tlo, 2)
            dve.drain().then_inc(s_ed, 6)

            def lo(step, j, w, slots=RAW):
                dve.wait_ge(s_hi, step + 1)
                V.tensor_tensor(wlo[j % SPLIT][:, 0:w], raw[j % slots][:, 0:w], whi[j % SPLIT][:, 0:w].bitcast(F32),
                                ALU.subtract).then_inc(s_lo, 1)

            def gate_lo(l, f):
                dve.wait_ge(s_fhi, l * NF + f + 1)
                V.tensor_tensor(flo[f % FSPLIT][:], raw[f % FRAW][:].rearrange("p (k n) -> p k n", n=128),
                                fhi[f % FSPLIT][:].bitcast(F32), ALU.subtract).then_inc(s_flo, 1)

            def t_lo(j, dst, src, hi_part):
                dve.wait_ge(s_thi, j + 1 + 2)
                V.tensor_tensor(dst, src, hi_part.bitcast(F32), ALU.subtract).then_inc(s_tlo, 1)

            def tbank(j, n=4, w=128):
                return PS[:, 6 + j % 2, 0:n * w].rearrange("p (k n) -> p k n", n=w)

            def normalise(l3, sq, st, t):
                if t == 0:
                    dve.wait_ge(s_gain, l3 * 16 + 16)
                dve.wait_ge(s_xst[t], (st + 1) * 16)
                dve.wait_ge(s_sq, sq + t + 1)
                V.reciprocal(rs[:, t:t + 1], ms[:, t:t + 1])
                dve.drain()
                V.scalar_tensor_tensor(rows[:, t, :], rows[:, t, :], rs[:, t:t + 1], gain[:], ALU.mult,
                                       ALU.mult).then_inc(s_xn, 1)

            def norm(l, n, j0):
                st = l * 2 + (0, 1, 1)[n]
                normalise(l * 3 + n, l * 18 + n * 6, st, 0)
                normalise(l * 3 + n, l * 18 + n * 6, st, 1)
                for t in range(NT):
                    for c in range(2):
                        k, s = slice(4 * c, 4 * c + 4), slice(t * 128, (t + 1) * 128)
                        t_lo(l * TPL + (j0 + 2 * t + c), hT[1][:, k, s], tbank(c), hT[0][:, k, s])
                    if t + 2 < NT:
                        normalise(l * 3 + n, l * 18 + n * 6, st, t + 2)

            def bc(ap, n):
                return ap.unsqueeze(2).broadcast_to([128, ap.shape[1], n])

            def heads(ap):
                return ap.rearrange("p (h d) -> p h d", d=HD)

            dve.wait_ge(s_cst, 16)
            with dve.Fori(0, DEPTH) as l:
                norm(l, 0, T_N0)
                with dve.Fori(0, NCH // 2) as i:
                    for j in range(8):
                        lo(l * SPL + i * 8 + j, j, 2 * CW)

                gate_lo(l, 0)
                dve.wait_ge(s_smallx, l + 1)
                dve.wait_ge(s_ea, l * AAPL + 36 + 6)
                dve.wait_ge(s_used, l * SPL + (S_G + SPLIT))
                for t in range(NT):
                    x = u[:, t, QA:QA + 384]
                    V.tensor_tensor(s3[:] if t % 2 else s1[:], x, x, ALU.mult)
                    dve.drain()
                    V.tensor_reduce(rqk[:, t, :], heads(s3[:] if t % 2 else s1[:]), AX.X, ALU.add)
                dve.drain().then_inc(s_ssq, 1)
                dve.wait_ge(s_rqk, l + 1)
                V.reciprocal(rqk[:], rqk[:])
                dve.drain()
                for t in range(NT):
                    pt = t - TILE_GROUP[t][0]
                    cs_ = cst[:, K_RA + pt * HD:K_RA + (pt + 1) * HD]
                    sn_ = cst[:, K_RA + 256 + pt * HD:K_RA + 256 + (pt + 1) * HD]
                    x = u[:, t, QA:QA + 384]
                    V.tensor_tensor(heads(s2[:]), heads(x), bc(rqk[:, t, :], HD), ALU.mult)
                    dve.drain()
                    V.tensor_tensor(s2[:], s2[:], gqk[:].rearrange("p h d -> p (h d)"), ALU.mult)
                    dve.drain()
                    V.tensor_tensor(heads(s1[:]), heads(s2[:]), cs_.unsqueeze(1).broadcast_to([128, 6, HD]), ALU.mult)
                    for hf in range(2):
                        o, i_ = 16 * hf, 16 * (1 - hf)
                        V.tensor_tensor(s3[:].rearrange("p (h a d) -> p h a d", a=2, d=32)[:, :, :, o:o + 16],
                                        s2[:].rearrange("p (h a d) -> p h a d", a=2, d=32)[:, :, :, i_:i_ + 16],
                                        sn_.rearrange("p (a d) -> p a d", d=32)[:, :, o:o + 16].unsqueeze(1)
                                        .broadcast_to([128, 6, 2, 16]), ALU.mult)
                    dve.drain()
                    if t >= 2:
                        dve.wait_ge(s_tA, l * NT + t - 1)
                    r = rA[:, t % 2, :]
                    V.tensor_tensor(r[:, 0:256].rearrange("p (a g d) -> p g a d", g=2, d=HD),
                                    s1[:, 0:256].rearrange("p (g a d) -> p g a d", g=2, d=HD),
                                    s3[:, 0:256].rearrange("p (g a d) -> p g a d", g=2, d=HD), ALU.add)
                    V.tensor_tensor(r[:, 256:384], s1[:, 256:384], s3[:, 256:384], ALU.add)
                    dve.drain().then_inc(s_rA, 1)
                    gate_lo(l, t + 1)

                for t in range(NT):
                    dve.wait_ge(s_zs, l * NT + t + 1)
                    if t >= 2:
                        dve.wait_ge(s_zt, l * NT + t - 1)
                    V.tensor_tensor(zr[:, t % 2, :], u[:, t, UB:UB + 256], zsg[:, t % 2, :],
                                    ALU.mult).then_inc(s_zr, 1)
                    if t in (2, 4):
                        gate_lo(l, F_Z + t // 2)
                dve.wait_ge(s_zT, l * NT + NT)

                def tap(n):
                    k, c = n // 2, n % 2
                    z = zT[:, c, k:k + AW]
                    if k == 0:
                        V.tensor_scalar(zacc[:, c, :], z, cw[:, c, 0:1], cb[:, c:c + 1], ALU.mult,
                                        ALU.add).then_inc(s_conv, 1)
                    else:
                        dve.wait_ge(s_conv, l * (2 * CONVW) + n - 1)
                        V.scalar_tensor_tensor(zacc[:, c, :], z, cw[:, c, k:k + 1], zacc[:, c, :], ALU.mult,
                                               ALU.add).then_inc(s_conv, 1)

                for n in range(51):
                    if n < 48:
                        kind, t, h, k0, nk = unit(n)
                        dve.wait_ge(s_sc, l * 48 + n + 1)
                        s = PS[:, n % 2, 0:nk * 128]
                        if kind == "A":
                            V.tensor_reduce(nm[:, n:n + 1], s, AX.X, ALU.max, negate=True).then_inc(s_nm, 1)
                        else:
                            m0 = K_WM + (k0 - (t - 1)) * 128
                            if n >= 26:
                                dve.wait_ge(s_p, l * 48 + n - 1)
                            V.scalar_tensor_tensor(sC[n % 2][:, 0:nk * 128], s, 0.125, cst[:, m0:m0 + nk * 128],
                                                   ALU.mult, ALU.add)
                            dve.drain()
                            V.tensor_reduce(small[:, 16:17], sC[n % 2][:, 0:nk * 128], AX.X, ALU.max)
                            dve.drain()
                            V.tensor_scalar(nm[:, n:n + 1], small[:, 16:17], sink_b[:, h:h + 1], -1.0, ALU.max,
                                            ALU.mult).then_inc(s_nm, 1)
                            if h == 3:
                                dve.drain()
                                V.tensor_tensor(sk[:, 4 * t:4 * t + 4], nm[:, n - 3:n + 1], sink_b[:],
                                                ALU.add).then_inc(s_sk, 1)
                    if n in F_UNITS:
                        i = F_UNITS.index(n)
                        for k in range(2 * CONVW * i // 36, 2 * CONVW * (i + 1) // 36):
                            tap(k)
                    if 1 <= n <= 48 and unit(n - 1)[0] == "A":
                        m = n - 1
                        nk = unit(m)[4]
                        dve.wait_ge(s_pt, l * 48 + m + 1)
                        if m >= 2:
                            dve.wait_ge(s_pv, l * 48 + m - 1)
                        V.tensor_copy(PT[:, m % 2, 0:nk * 128], PS[:, 2 + m % 2, 0:nk * 128]).then_inc(s_ptA, 1)
                    if n in F_UNITS and i % 4 == 1:
                        gate_lo(l, F_ATT + i // 4 + 1)
                    if n >= 3 and unit(n - 3)[2] == 3:
                        m = n - 3
                        kind, t, h, k0, nk = unit(m)
                        dve.wait_ge(s_pv, l * 48 + m + 1)
                        tot = sm[:, m - 3:m + 1]
                        if kind == "C":
                            dve.wait_ge(s_es, l * NT + t + 1)
                            V.tensor_tensor(rcp[:, m - 3:m + 1], tot, es[:, 4 * t:4 * t + 4], ALU.add)
                            dve.drain()
                            tot = rcp[:, m - 3:m + 1]
                        V.reciprocal(rcp[:, m - 3:m + 1], tot)
                        dve.drain()
                        q0 = QA if kind == "A" else QC
                        V.tensor_tensor(heads(u[:, t, q0:q0 + 256]), heads(PS[:, 4 + (m // 4) % 2, 0:256]),
                                        bc(rcp[:, m - 3:m + 1], HD), ALU.mult).then_inc(s_o, 1)

                for t in range(NT):
                    dve.wait_ge(s_zb, l * NT + t + 1)
                    V.bn_stats(bns[:, t, :], PS[:, t, 0:256])
                    dve.drain()
                    V.bn_aggr(bnv[:, t, :], bns[:, t, :])
                dve.drain().then_inc(s_bn, 1)
                gate_lo(l, F_CONV + 1)
                dve.wait_ge(s_bnr, l + 1)
                V.reciprocal(bnv[:, :, 1], bnv[:, :, 1])
                dve.drain()
                for t in range(NT):
                    if t >= 2:
                        dve.wait_ge(s_ob, l * NT + t - 1)
                    V.tensor_scalar(zn[:, t % 2, :], PS[:, t, 0:256], bnv[:, t, 0:1], bnv[:, t, 1:2],
                                    ALU.subtract, ALU.mult)
                    dve.drain()
                    V.tensor_tensor(zn[:, t % 2, :], zn[:, t % 2, :], lng[:], ALU.mult)
                    dve.drain()
                    V.tensor_tensor(zn[:, t % 2, :], zn[:, t % 2, :], lnb[:], ALU.add).then_inc(s_zn, 1)
                    if t == 3:
                        gate_lo(l, F_GLA)

                dve.wait_ge(s_g[10], l + 1)
                dve.wait_ge(s_az, l + 1)
                for n in range(NT + 1):
                    buf = (E3 if n % 2 == 0 else TT)
                    old = (TT if n % 2 == 0 else E3)
                    if n >= 1:
                        m = n - 1
                        dve.wait_ge(s_g[6], l * NT + m + 1)
                        V.tensor_tensor(old[:, 1, :].rearrange("p (a n) -> p a n", a=2),
                                        u[:, m, KD:KD + 256].unsqueeze(1).broadcast_to([128, 2, 256]),
                                        old[:, 1, :].rearrange("p (a n) -> p a n", a=2), ALU.mult).then_inc(s_g[7], 1)
                    if n < NT:
                        dve.wait_ge(s_g[3], l * NT + n + 1)
                        V.scalar_tensor_tensor(la[:, n, :], PS[:, 1, :], 0.0, buf[:, 0, :], ALU.min,
                                               ALU.subtract).then_inc(s_g[4], 1)
                        gate_lo(l, F_GLA + n + 1)
                    if n >= 1:
                        dve.wait_ge(s_g[8], l * NT + m + 1)
                        for c in range(2):
                            V.tensor_copy(kvs[:, 2 * m + c, :, :],
                                          PS[:, 4 + c, 0:256].rearrange("p (a n) -> p a n", n=HD))
                        dve.drain().then_inc(s_g[9], 1)
                for r in range(1, 8):
                    for (a, b) in GROUPS:
                        c0, c1_ = 2 * a, 2 * b
                        if r >= c1_ - c0:
                            continue
                        for d in range(2):
                            c = c0 + r if d == 0 else c1_ - 1 - r
                            prev = c - 1 if d == 0 else c + 1
                            for p in range(2):
                                k = 2 * d + p
                                V.scalar_tensor_tensor(kvs[:, c, k, :], kvs[:, prev, k, :],
                                                       dec[:, c // 2, 2 * k + c % 2:2 * k + c % 2 + 1],
                                                       kvs[:, c, k, :], ALU.mult, ALU.add)
                    dve.drain()
                dve.drain().then_inc(s_scan, 1)
                gate_lo(l, F_GLB)
                for n in range(NT + 1):
                    m = n - 1
                    if n >= 1:
                        wait_alone(dve, s_h[6], l * NT + m + 1)
                        for par in range(2):
                            V.copy_predicated(att[:, par, :], cst[:, K_GM:K_GM + 512].bitcast(I32), PS[:, par, :])
                        dve.drain().then_inc(s_h[7], 1)
                    if n < NT:
                        dve.wait_ge(s_h[1], l * NT + n + 1)
                        for k, (src, f) in enumerate(((QD, 0.125), (KD, 1.0), (QD, 0.125))):
                            e = E3[:, k, :].rearrange("p (a n) -> p a n", a=2)
                            V.scalar_tensor_tensor(e, u[:, n, src:src + 256].unsqueeze(1).broadcast_to([128, 2, 256]),
                                                   f, e, ALU.mult, ALU.mult)
                        dve.drain().then_inc(s_h[2], 1)
                        if n < NT - 1:
                            gate_lo(l, F_GLB + n + 1)
                    if n >= 1:
                        dve.wait_ge(s_h[8], l * NT + m + 1)
                        ob = u[:, m, QD:QD + 256].rearrange("p (a h d) -> p a h d", h=2, d=HD)
                        for par in range(2):
                            V.tensor_copy(ob[:, :, par, :], PS[:, (5, 2)[par], 0:128].rearrange("p (a d) -> p a d", d=HD))
                        dve.drain().then_inc(s_h[9], 1)
                    if n < NT:
                        dve.wait_ge(s_h[3], l * NT + n + 1)
                        V.tensor_copy(TT[:, 2, :], PS[:, 4, :]).then_inc(s_h[5], 1)
                    if n >= 1:
                        V.tensor_tensor(osq[:], u[:, m, QD:QD + 256], u[:, m, QD:QD + 256], ALU.mult)
                        dve.drain()
                        V.tensor_reduce(oss[:, m, :], heads(osq[:]), AX.X, ALU.add)
                        if n == NT:
                            dve.drain().then_inc(s_oss, 1)
                        ot = u[:, m, QD:QD + 256]
                        V.tensor_tensor(heads(ot), heads(ot), gng[:].unsqueeze(1).broadcast_to([128, 4, HD]), ALU.mult)
                        dve.drain()
                        V.tensor_tensor(ot, ot, u[:, m, RD:RD + 256], ALU.mult)

                def t_lo_branches(c, t):
                    t_lo(l * TPL + (T_G + 6 * c + t), urblk[:, t, 2 * c:2 * c + 2, 0, :],
                         PS[:, 6 + t % 2, :].rearrange("p (k n) -> p k n", n=256), urblk[:, t, 2 * c:2 * c + 2, 1, :])

                od4 = u[:, :, QD:QD + 256].rearrange("p t (h d) -> p t h d", d=HD)
                dve.wait_ge(s_or, l + 1)
                V.reciprocal(oss[:], oss[:])
                dve.drain()
                V.tensor_tensor(od4, od4, oss[:].unsqueeze(3).broadcast_to([128, NT, 4, HD]),
                                ALU.mult).then_inc(s_od, 1)
                for t in range(NT):
                    t_lo_branches(0, t)

                for t in range(NT):
                    t_lo_branches(1, t)
                for n in range(4):
                    lo(l * SPL + (S_G + n), n, 1024)
                for g in range(9):
                    if g < 8:
                        dve.wait_ge(s_sg, l * 8 + g + 1)
                        for i in range(NB):
                            if i < NB - 1:
                                dve.wait_ge(s_br[i], l * 8 + g + 1)
                            else:
                                dve.wait_ge(s_used, l * SPL + (S_G + g + 1 + SPLIT))
                            G = gates[g % 2][:, i]
                            V.tensor_tensor(G, G, PS[:, 2 * i:2 * i + 2, :].rearrange("p a n -> p (a n)")[:, 0:TOK]
                                            .rearrange("p (t n) -> p t n", n=128), ALU.mult).then_inc(s_gm[i], 1)
                    if g >= 1:
                        lo(l * SPL + (S_G + g + 3), g + 3, 1024)
                        dve.wait_ge(s_mh, l * 8 + g)
                        V.tensor_tensor(hT[1][:, g - 1, :], merged[:, g - 1, :], hT[0][:, g - 1, :].bitcast(F32),
                                        ALU.subtract).then_inc(s_ml, 1)
                for c in range(2):
                    for n in range(3):
                        lo(l * SPL + (S_O + 4 * c + 4 + n), 4 * c + 4 + n, 1024)
                    for t in range(NT):
                        accumulated(dve, l * CPL + (C_O + c), l * SPL + (S_O + 4 * c + 3), t)
                        if c == 0:
                            dve.wait_ge(s_xin[t], (l * 3 + 2) * 16)
                        r = rows[:, t, c * 512:(c + 1) * 512]
                        V.tensor_tensor(r, r, PS[:, t, :], ALU.add).then_inc(s_ed, 1)
                    lo(l * SPL + (S_O + 4 * c + 7), 4 * c + 7, 1024)

                for t in range(NT):
                    normalise(l * 3 + 1, l * 18 + 6, l * 2 + 1, t)
                dve.wait_ge(s_rt, l + 1)
                pr = PS[:, 2, 0:NT * NE].rearrange("p (t e) -> p t e", e=NE)
                V.tensor_reduce(lmx[:], pr, AX.X, ALU.max)
                dve.drain()
                V.tensor_tensor(lg[:], pr, bc(lmx[:], NE), ALU.subtract).then_inc(s_lm, 1)
                dve.wait_ge(s_le, l + 1)
                V.tensor_reduce(lsm[:], lg[:], AX.X, ALU.add)
                dve.drain()
                V.reciprocal(lmx[:], lsm[:])
                dve.drain()
                V.tensor_tensor(lg[:], lg[:], bc(lmx[:], NE), ALU.mult).then_inc(s_af, 1)
                dve.wait_ge(s_aft, l + 1)
                dve.wait_ge(s_scz, l + 1)
                V.tensor_copy(scores[0:NE, :], PS[0:NE, 3, :])
                V.tensor_copy(scores[32:32 + NE, 0:DEC], PS[0:NE, 4, 0:DEC])
                dve.drain()
                for r in range(CAPP // 8):
                    v, ix = top[:, 8 * r:8 * r + 8], topi[:, 8 * r:8 * r + 8]
                    V.max(v, scores[:])
                    dve.drain()
                    V.max_index(ix, v, scores[:])
                    dve.drain()
                    V.match_replace(scores[:], v, scores[:], -1.0)
                    dve.drain()
                V.tensor_copy(pick[:, 0, 0:CAPP], topi[0:NE, :])
                V.tensor_copy(pick[:, 1, 0:CAPP], top[0:NE, :])
                V.tensor_scalar(pick[:, 0, CAPP:CAP], topi[32:32 + NE, 0:CAPS], float(SEQ), None, ALU.add)
                V.tensor_copy(pick[:, 1, CAPP:CAP], top[32:32 + NE, 0:CAPS])
                dve.drain().then_inc(s_pick, 1)
                dve.wait_ge(s_pickt, l + 1)
                V.tensor_copy(idxT[:, 0:NE], PS[0:CAP, 5, 0:NE])
                V.tensor_copy(idxT[:, NE:NE + 1], PS[0:CAP, 5, 0:1])
                V.tensor_copy(gateT[:], PS[0:CAP, 5, NE:2 * NE])
                dve.drain().then_inc(s_idx, 1)
                for c in range(2):
                    k = slice(4 * c, 4 * c + 4)
                    t_lo(l * TPL + (T_E + c), xeT[1][:, k, :], tbank(c, 4, CAP), xeT[0][:, k, :])
                with dve.Fori(0, NE) as e:
                    for s in range(ES):
                        j = l * TPL + e * 4 + (T_E + 2)
                        if s in (7, 15):
                            c = s // 8
                            dve.wait_ge(s_used, l * SPL + e * ES + (S_E + s + 1 + SPLIT))
                            dve.wait_ge(s_sil, l * 32 + e * 2 + (c + 1))
                            h = sil[:, c * 512:(c + 1) * 512]
                            V.tensor_tensor(h, h, PS[0:CAP, 2 + c, :], ALU.mult).then_inc(s_hid, 1)
                        if s == 11:
                            t_lo(j, hidT[1][:, 0:4, :], tbank(0, 4, CAP), hidT[0][:, 0:4, :])
                        if s == 17:
                            t_lo(j + 1, hidT[1][:, 4:8, :], tbank(1, 4, CAP), hidT[0][:, 4:8, :])
                        if s == 19:
                            t_lo(j + 2, xeT[1][:, 0:4, :], tbank(0, 4, CAP), xeT[0][:, 0:4, :])
                        if s == 21:
                            t_lo(j + 3, xeT[1][:, 4:8, :], tbank(1, 4, CAP), xeT[0][:, 4:8, :])
                        lo(l * SPL + e * ES + (S_E + s + 4), s + 4, 1024, ES)

                for t in range(NT):
                    s = slice(t * 128, (t + 1) * 128)
                    t_lo(l * TPL + (T_P + t), oT[1][:, :, s], tbank(t, 2), oT[0][:, :, s])
                norm(l, 2, T_N2)
                for c in range(2):
                    s = l * SPL + (S_P + 8 * c)
                    for n in range(4, 8):
                        lo(s + n, n, 256)
                    if c == 0:
                        for n in range(8, 12):
                            lo(s + n, n, 1024)
                    for t in range(NT):
                        accumulated(dve, l * CPL + (C_P + 2 * c + 1), s + 7, t)
                        V.tensor_tensor(gsig[:, t, :], gsig[:, t, :], PS[:, t, :], ALU.mult)
                        dve.drain()
                        if c == 0:
                            dve.wait_ge(s_xin[t], (l * 3 + 4) * 16)
                        r = rows[:, t, c * 512:(c + 1) * 512]
                        V.tensor_tensor(r, r, gsig[:, t, :], ALU.add).then_inc(s_ed, 1)
            for t in range(NT):
                normalise(DEPTH * 3, DEPTH * 18, DEPTH * 2, t)

        @block.tensor
        def _(pe):
            pe.drain().then_inc(s_used, SPLIT)
            pe.drain().then_inc(s_fused, FSPLIT)
            pe.wait_ge(s_cst, 16)

            def transposes(j, b, blocks, free, np_=128, w=128):
                sm_, v = free
                pe.wait_ge(sm_, v)
                for n, x in enumerate(blocks):
                    m = nc.tensor.transpose(PS[:, 6 + b, n * np_:(n + 1) * np_], x, ident[0:np_, 0:np_])
                m.then_inc(s_tp, 1)

            def norm(l, n, j0, plain=False, between=None):
                for t in range(NT):
                    if between is not None and t >= 2:
                        between(t - 2)
                    pe.wait_ge(s_xn, l * 18 + (n * 6 + t + 1))
                    for c in range(2):
                        j = j0 + 2 * t + c
                        if plain and j - 2 >= j0:
                            free = (s_thi, l * TPL + (j - 1) + 2)
                        else:
                            free = (s_tlo, l * TLL + lo_count(j - 2) + 2)
                        transposes(j, c, [rows[:, t, k * 128:(k + 1) * 128] for k in range(4 * c, 4 * c + 4)], free)

            def product(out, x, w, first, last):
                nc.tensor.matmul(out, x[0], w[0], start=first, stop=False)
                nc.tensor.matmul(out, x[0], w[1], start=False, stop=False)
                return nc.tensor.matmul(out, x[1], w[0], start=False, stop=last)

            def step(val, j, nk, n, x, k0, first, last, free=None, c0=0, final=True):
                pe.wait_ge(s_lo, val + 1 + RAW)
                for k in range(nk):
                    for t in range(NT):
                        if free is not None and k == 0:
                            pe.wait_ge(*free(t))
                        s = slice(t * 128, (t + 1) * 128)
                        m = product(PS[:, t, c0:c0 + n], (x[0][:, k0 + k, s], x[1][:, k0 + k, s]),
                                    (cols(whi[j % SPLIT], nk, n)[:, k, :], cols(wlo[j % SPLIT], nk, n)[:, k, :]),
                                    first and k == 0, last and k == nk - 1)
                        if last and final and k == nk - 1 and t < NT - 1:
                            m.then_inc(s_acc, 1)
                m.then_inc(s_used, 1)

            def chunk(val, n, free):
                for j in range(4):
                    step(val + j, j, 2, n, hT, 2 * j, j == 0, j == 3, free if j == 0 else None)

            def transposed(b, w, x, first, last):
                for p, (wn, xn) in enumerate(((0, 0), (0, 1), (1, 0))):
                    for t0, t1, bb in ((0, 4, b), (4, NT, b + 1)):
                        m = nc.tensor.matmul(PS[:, bb, 0:(t1 - t0) * 128], w[wn], x[xn](t0, t1),
                                             start=first and p == 0, stop=last and p == 2)
                return m

            def gate_step(l, f, k0=0, k1=KT):
                if k0 == 0:
                    pe.wait_ge(s_flo, l * NF + f + 1)
                    pe.wait_ge(s_fev, l * NF + f + 1)
                for k in range(k0, k1):
                    m = transposed(gate_bank(f), [w[f % FSPLIT][:, k, :] for w in (fhi, flo)],
                                   [lambda a, b, x=x: x[:, k, a * 128:b * 128] for x in hT], k == 0, k == KT - 1)
                if k1 == KT:
                    m.then_inc(s_fused, 1)

            def branch_chunk(val, free):
                for j in range(4):
                    step(val + j, j, 1, 256, oT, j % 2, j % 2 == 0, j % 2 == 1, free if j == 0 else None,
                         (j // 2) * 256, j == 3)

            with pe.Fori(0, DEPTH) as l:
                norm(l, 0, T_N0)
                wait_alone(pe, s_tlo, l * TLL + lo_count(T_N0 + 11) + 2)
                with pe.Fori(0, NCH // 2) as i:
                    for j in range(2):
                        chunk(l * SPL + i * 8 + 4 * j, CW, lambda t: (s_ea, l * AAPL + i * 12 + (j * 6 + t + 1)))

                gate_step(l, F_ROPE)
                pe.wait_ge(s_ea, l * AAPL + 36 + 6)
                pe.wait_ge(s_fev, l * NF + 2)
                for t in range(NT):
                    if t > 0:
                        gate_step(l, F_ROPE + t)
                    pe.wait_ge(s_rA, l * NT + t + 1)
                    if t >= 1:
                        pe.wait_ge(s_qA, l * NT + t)
                    for k in range(3):
                        m = nc.tensor.transpose(PS[:, 6, k * 128:(k + 1) * 128], rA[:, t % 2, k * 128:(k + 1) * 128], ident)
                    m.then_inc(s_tA, 1)
                    pe.wait_ge(s_rC, l * NT + t + 1)
                    if t >= 1:
                        pe.wait_ge(s_qC, l * NT + t)
                    for k in range(3):
                        m = nc.tensor.transpose(PS[:, 7, k * 128:(k + 1) * 128], rC[:, t % 2, k * 128:(k + 1) * 128], ident)
                    m.then_inc(s_tC, 1)
                pe.wait_ge(s_qA, l * NT + NT)
                pe.wait_ge(s_qC, l * NT + NT)
                for t in range(NT):
                    if t in (2, 4):
                        gate_step(l, F_Z + t // 2 - 1)
                    pe.wait_ge(s_zr, l * NT + t + 1)
                    if t >= 2:
                        pe.wait_ge(s_zT, l * NT + t - 1)
                    for c in range(2):
                        m = nc.tensor.transpose(PS[:, t % 2, c * 128:(c + 1) * 128], zr[:, t % 2, c * 128:(c + 1) * 128], ident)
                    m.then_inc(s_zt, 1)
                pe.wait_ge(s_zT, l * NT + NT)
                for n in range(50):
                    if n < 48:
                        kind, t, h, k0, nk = unit(n)
                        if n >= 2:
                            pe.wait_ge(s_p, l * 48 + n - 1)
                        qk = qkA if kind == "A" else qkC
                        g = slice(64 * (h // 2), 64 * (h // 2) + 64)
                        nc.tensor.matmul(PS[:, n % 2, 0:nk * 128], qk[g, h % 2, t * 128:(t + 1) * 128],
                                         qk[g, 2, k0 * 128:(k0 + nk) * 128], start=True, stop=True).then_inc(s_sc, 1)
                        if n in F_UNITS:
                            i = F_UNITS.index(n)
                            gate_step(l, F_ATT + i // 4, i % 4 * 2, i % 4 * 2 + 2)
                    if 1 <= n <= 48:
                        m = n - 1
                        kind, t, h, k0, nk = unit(m)
                        pe.wait_ge(s_p, l * 48 + m + 1)
                        if m >= 2:
                            pe.wait_ge(*pt_done(l, m - 2))
                        for k in range(nk):
                            mm = nc.tensor.transpose(PS[:, 2 + m % 2, k * 128:(k + 1) * 128],
                                                     P[:, m % 2, k * 128:(k + 1) * 128], ident)
                        mm.then_inc(s_pt, 1)
                    if n >= 2:
                        m = n - 2
                        kind, t, h, k0, nk = unit(m)
                        pe.wait_ge(*pt_done(l, m))
                        if h == 0 and m >= 8:
                            pe.wait_ge(s_o, l * 12 + m // 4 - 1)
                        v0 = (VA if kind == "A" else VC) + 64 * (h // 2)
                        for k in range(nk):
                            mm = nc.tensor.matmul(PS[:, 4 + (m // 4) % 2, h * HD:(h + 1) * HD],
                                                  PT[:, m % 2, k * 128:(k + 1) * 128], u[:, k0 + k, v0:v0 + HD],
                                                  start=k == 0, stop=k == nk - 1)
                        mm.then_inc(s_pv, 1)

                pe.wait_ge(s_conv, l * (2 * CONVW) + 2 * CONVW)
                pe.wait_ge(s_o, l * 12 + 12)
                for t in range(NT):
                    a0 = t * 128 + (PAD if t >= 4 else 0)
                    for c in range(2):
                        m = nc.tensor.transpose(PS[:, t, c * 128:(c + 1) * 128], zacc[:, c, a0:a0 + 128], ident)
                    m.then_inc(s_zb, 1)
                for f in range(2):
                    gate_step(l, F_CONV + f)

                pe.wait_ge(s_az, l + 1)
                cum = [cst[:, K_CUM + n * 128:K_CUM + (n + 1) * 128] for n in range(6)]
                for n in range(NT + 1):
                    m = n - 1
                    if n < NT:
                        pe.wait_ge(s_ob, l * NT + NT)
                        if n >= 1:
                            pe.wait_ge(s_g[1], l * NT + n)
                        nc.tensor.transpose(PS[0:32, 0, 0:128], u[:, n, ZL:ZL + 32], ident).then_inc(s_g[0], 1)
                    if n >= 1:
                        pe.wait_ge(s_g[4], l * NT + n)
                        for d in range(2):
                            nc.tensor.matmul(PS[:, 2, d * 256:(d + 1) * 256], cum[3 * d + 2],
                                             la[:, m, d * 256:(d + 1) * 256], start=True, stop=True)
                        for k in range(4):
                            mm = nc.tensor.matmul(PS[:, 3, 2 * k:2 * k + 2], la[:, m, k * 128:(k + 1) * 128],
                                                  cst[:, K_IND:K_IND + 2], start=True, stop=True)
                        mm.then_inc(s_g[5], 1)
                    if n < NT:
                        pe.wait_ge(s_g[1], l * NT + n + 1)
                        nc.tensor.matmul(PS[:, 1, :], zlT[0:33, :], w2b[0:33, :], start=True, stop=True).then_inc(s_g[2], 1)
                        gate_step(l, F_GLA + n)
                    if n >= 1:
                        wait_alone(pe, s_g[7], l * NT + n)
                        if n >= 2:
                            pe.wait_ge(s_g[9], l * NT + n - 1)
                        old = (TT if n % 2 == 0 else E3)
                        for c in range(2):
                            cr = slice(64 * c, 64 * c + 64)
                            for d in range(2):
                                for h in range(4):
                                    mm = nc.tensor.matmul(
                                        PS[64 * (h % 2):64 * (h % 2) + 64, 4 + c, (2 * d + h // 2) * HD:(2 * d + h // 2 + 1) * HD],
                                        old[cr, 1, d * 256 + h * HD:d * 256 + (h + 1) * HD],
                                        u[cr, m, VD + h * HD:VD + (h + 1) * HD], start=True, stop=True)
                        mm.then_inc(s_g[8], 1)
                gate_step(l, F_SCAN)
                pe.wait_ge(s_scan, l + 1)
                for n in range(NT + 1):
                    m = n - 1
                    if n < NT:
                        if n >= 1:
                            pe.wait_ge(s_h[1], l * NT + n)
                        if n >= 2:
                            pe.wait_ge(s_h[7], l * NT + n - 1)
                        for b, k in ((0, 1), (1, 0)):
                            for d in range(2):
                                mm = nc.tensor.matmul(PS[:, b, d * 256:(d + 1) * 256], cum[3 * d + k],
                                                      la[:, n, d * 256:(d + 1) * 256], start=True, stop=True)
                        mm.then_inc(s_h[0], 1)
                        gate_step(l, F_GLB + n, 0, KT // 2)
                    if n >= 1:
                        pe.wait_ge(s_h[4], l * NT + n)
                        pe.wait_ge(s_h[5], l * NT + n)
                        if n < NT:
                            pe.wait_ge(s_h[1], l * NT + n + 1)
                        for par in range(2):
                            g = slice(64 * par, 64 * par + 64)
                            for k in range(4):
                                mm = nc.tensor.matmul(PS[:, par, k * 128:(k + 1) * 128],
                                                      TT[g, 1, k * 128:(k + 1) * 128], TT[g, 0, k * 128:(k + 1) * 128],
                                                      start=True, stop=True)
                        mm.then_inc(s_h[6], 1)
                    if n < NT:
                        gate_step(l, F_GLB + n, KT // 2, KT)
                    if n >= 1:
                        pe.wait_ge(s_h[7], l * NT + n)
                        if n >= 2:
                            pe.wait_ge(s_h[9], l * NT + n - 1)
                        ga, gb = TILE_GROUP[m]
                        for par in range(2):
                            g = slice(64 * par, 64 * par + 64)
                            for p in range(2):
                                h = 2 * p + par
                                ob = PS[:, (5, 2)[par], p * HD:(p + 1) * HD]
                                for d in range(2):
                                    k = 2 * d + p
                                    mm = nc.tensor.matmul(ob, att[:, par, k * 128:(k + 1) * 128],
                                                          u[:, m, VD + h * HD:VD + (h + 1) * HD],
                                                          start=d == 0, stop=False, skip_group_check=True)
                                for d in range(2):
                                    k = 2 * d + p
                                    for c in range(2):
                                        ch = 2 * m + c
                                        if ch == (2 * ga if d == 0 else 2 * gb - 1):
                                            continue
                                        mm = nc.tensor.matmul(
                                            PS[64 * c:64 * c + 64, (5, 2)[par], p * HD:(p + 1) * HD],
                                            TT[g, 2, k * 128 + 64 * c:k * 128 + 64 * c + 64],
                                            kvs[g, ch - 1 if d == 0 else ch + 1, k, :],
                                            start=False, stop=True, skip_group_check=True)
                        mm.then_inc(s_h[8], 1)
                    if n < NT:
                        pe.wait_ge(s_h[2], l * NT + n + 1)
                        if n >= 1:
                            pe.wait_ge(s_h[9], l * NT + n)
                        for b in range(3):
                            for k in range(4):
                                mm = nc.tensor.transpose(PS[:, 2 + b, k * 128:(k + 1) * 128],
                                                         E3[:, b, k * 128:(k + 1) * 128], ident)
                        mm.then_inc(s_h[3], 1)

                wait_alone(pe, s_fev, l * NF + NF + 1)
                for c in range(2):
                    if c == 1:
                        wait_alone(pe, s_od, l + 1)
                    for t in range(NT):
                        transposes(None, t % 2, [ublk[:, t, 2 * c + k // 2, 0, (k % 2) * 128:(k % 2) * 128 + 128]
                                                 for k in range(4)], (s_tlo, l * TLL + (T_G + 6 * c + t + 1)))
                pe.wait_ge(s_tlo, l * TLL + (T_G + 12 + 2))
                for g in range(8):
                    pe.wait_ge(s_lo, l * SPL + (S_G + g + 1 + RAW))
                    w = [x[g % SPLIT][:].rearrange("p (k n) -> p k n", n=128) for x in (whi, wlo)]
                    for i in range(NB):
                        if g >= 1:
                            pe.wait_ge(s_gm[i], l * 8 + g)
                        for k in range(2):
                            c = slice(k * 128, (k + 1) * 128)
                            m = transposed(2 * i, [x[:, 2 * i + k, :] for x in w],
                                           [lambda a, b, h=h: urblk[:, a:b, i, h, c] for h in (1, 0)], k == 0, k == 1)
                        m.then_inc(s_br[i] if i < NB - 1 else s_used, 1)
                for j in range(4):
                    pe.wait_ge(s_ml, l * 8 + (2 * j + 2))
                    step(l * SPL + (S_O + j), j, 2, 512, hT, 2 * j, j == 0, j == 3,
                         (lambda t: (s_gm[t // 2], l * 8 + 8)) if j == 0 else None)
                chunk(l * SPL + (S_O + 4), 512, lambda t: (s_ed, l * ADPL + (t + 1 + 6)))

                def router(t):
                    pe.wait_ge(s_thi, l * TPL + (T_N1 + 2 * t + 2 + 2))
                    for k in range(KT):
                        mm = nc.tensor.matmul(PS[:, 2, t * NE:(t + 1) * NE], hTf[:, k, t * 128:(t + 1) * 128],
                                              wr[:, k, :], start=k == 0, stop=k == KT - 1)
                    return mm

                norm(l, 1, T_N1, plain=True, between=router)
                for t in range(NT - 2, NT):
                    mm = router(t)
                mm.then_inc(s_rt, 1)
                pe.wait_ge(s_af, l + 1)
                for t in range(NT):
                    b, o = (3, t) if t < 4 else (4, t - 4)
                    mm = nc.tensor.transpose(PS[0:NE, b, o * 128:(o + 1) * 128], lg[:, t, :], ident)
                mm.then_inc(s_aft, 1)
                wait_alone(pe, s_pick, l + 1)
                for n in range(2):
                    mm = nc.tensor.transpose(PS[0:CAP, 5, n * NE:(n + 1) * NE], pick[:, n, :], ident[0:NE, 0:NE])
                mm.then_inc(s_pickt, 1)
                pe.wait_ge(s_ga, l * (17 * 16) + 16)
                pe.wait_ge(s_idx, l + 1)
                for c in range(2):
                    transposes(None, c, [xe[:, k * 128:(k + 1) * 128] for k in range(4 * c, 4 * c + 4)],
                               (s_thi, l * TPL + (T_E + c - 1 + 2)), CAP)

                def expert_steps(e, s0, n, bank, x, k0, first, last):
                    for j in range(n):
                        pe.wait_ge(s_lo, l * SPL + e * ES + (S_E + s0 + j + 1 + RAW))
                        w = [cols(x_[(s0 + j) % SPLIT], 2, 512) for x_ in (whi, wlo)]
                        for k in range(2):
                            kk = k0 + 2 * j + k
                            m = product(PS[0:CAP, bank, :], (x[0][:, kk, :], x[1][:, kk, :]), (w[0][:, k, :], w[1][:, k, :]),
                                        first and j == 0 and k == 0, last and j == n - 1 and k == 1)
                        m.then_inc(s_used, 1)

                with pe.Fori(0, NE) as e:
                    tl = l * TLL + e * 4 + (T_E - 12 + 2 + 2)
                    pe.wait_ge(s_tlo, tl)
                    for c in range(2):
                        expert_steps(e, 8 * c, 4, c, xeT, 0, True, True)
                        if c == 1:
                            pe.wait_ge(s_hid, l * 32 + e * 2 + 1)
                            transposes(None, 0, [sil[:, k * 128:(k + 1) * 128] for k in range(4)], (s_tlo, tl), CAP)
                        expert_steps(e, 8 * c + 4, 4, 2 + c, xeT, 0, True, True)
                    pe.wait_ge(s_tlo, tl + 1)
                    expert_steps(e, 16, 2, 4, hidT, 0, True, False)
                    pe.wait_ge(s_hid, l * 32 + e * 2 + 2)
                    transposes(None, 1, [sil[:, k * 128:(k + 1) * 128] for k in range(4, 8)], (s_tlo, tl), CAP)
                    expert_steps(e, 18, 2, 5, hidT, 0, True, False)
                    pe.wait_ge(s_ga, l * (17 * 16) + e * 16 + 32)
                    transposes(None, 0, [xe[:, k * 128:(k + 1) * 128] for k in range(4)], (s_tlo, tl + 1), CAP)
                    pe.wait_ge(s_tlo, tl + 2)
                    expert_steps(e, 20, 2, 4, hidT, 4, False, True)
                    transposes(None, 1, [xe[:, k * 128:(k + 1) * 128] for k in range(4, 8)], (s_tlo, tl + 2), CAP)
                    expert_steps(e, 22, 2, 5, hidT, 4, False, True)

                pe.wait_ge(s_pin, l * 32 + 32)
                for t in range(NT):
                    transposes(None, t % 2, [prow[:, t, k * 128:(k + 1) * 128] for k in range(2)],
                               (s_tlo, l * TLL + lo_count(T_P + t - 2) + 2))
                norm(l, 2, T_N2)
                pe.wait_ge(s_tlo, l * TLL + lo_count(T_N2 + 11) + 2)
                for c in range(2):
                    s = l * SPL + (S_P + 8 * c)
                    chunk(s, 512, lambda t: (s_ed, l * ADPL + (AD_P + 6 * (c - 1) + t + 1 + 6)))
                    branch_chunk(s + 4, lambda t: (s_ea, l * AAPL + (AA_P + c * 6 + t + 1 + 6)))


def unit(n):
    kind, t, h = ("A", "C")[n // 24], n % 24 // 4, n % 4
    a, b = TILE_GROUP[t]
    if kind == "C":
        a, b = max(a, t - 1), min(b, t + 2)
    return kind, t, h, a, b - a


_NAMES = ["x_prompt", "x_sample", "p_prompt", "p_sample", "norm_mix", "w_in", "qk_norm", "sink_logit", "conv_dw",
          "conv_dw_b", "conv_ln_g", "conv_ln_b", "gla_w2", "gla_b2", "gla_norm", "w_branch", "w_out", "norm_ffn",
          "w_router", "w_gate_e", "w_up_e", "w_down_e", "norm_ple", "w_ple_gate", "w_ple_proj", "norm_final"]


def kernel(**inputs):
    import concourse.bacc as bacc
    from concourse.bass_utils import run_bass_kernel_spmd

    nc = bacc.Bacc("TRN2", target_bir_lowering=False, num_devices=1)
    arrays, args = {}, []
    for name in _NAMES:
        a = np.asarray(inputs[name])
        if name == "conv_dw":
            a = a.transpose(0, 2, 1)
        arrays[f"in_{name}"] = np.ascontiguousarray(a)
    arrays["in_consts"] = shape_constants()
    for name, a in arrays.items():
        args.append(nc.dram_tensor(name, a.shape, mybir.dt.from_np(a.dtype), kind="ExternalInput").ap())
    for n, s in (("out_prompt", SEQ), ("out_sample", DEC)):
        args.append(nc.dram_tensor(n, [1, s, D], F32, kind="ExternalOutput").ap())
    build(nc, *args)
    r = run_bass_kernel_spmd(nc, [arrays], core_ids=[0])
    return r.results[0]["out_prompt"], r.results[0]["out_sample"]
```
